# Optimizing a Trainium2 kernel written in Bass

```python
import math
import jax
import jax.numpy as jnp
from jax import lax
import numpy as np

D_MODEL = 1024
BATCH = 1
SEQ = 512
DEPTH = 1
DEC_BATCH = 8
DEC_SEQ = 8
PAST_LEN = 256
PAGE_SIZE = 128

HEAD_DIM = 64
CONV_DIM = 512
CONV_WIDTH = 3
DIL_PAIRS = ((128, 1), (512, 4), (2048, 16))
DIL_GROUP_HEADS = 4
DIL_HEADS = DIL_GROUP_HEADS * len(DIL_PAIRS)
DIL_DIM = DIL_HEADS * HEAD_DIM
DIL_OUT_DIM = DIL_GROUP_HEADS * HEAD_DIM
DIL_BLOCK = 128
NSA_HEADS = 8
NSA_KV_HEADS = 2
NSA_GROUP = NSA_HEADS // NSA_KV_HEADS
NSA_Q_DIM = NSA_HEADS * HEAD_DIM
NSA_KV_DIM = NSA_KV_HEADS * HEAD_DIM
CMP_BLOCK = 32
CMP_STRIDE = 16
CMP_HIDDEN = 128
SEL_BLOCK = 64
SEL_TOPK = 16
SEL_FORCE = 1000.0
SEL_QCHUNK = 64
NSA_WINDOW = 512
WIN_BLOCK = 128
REL_BUCKETS = 32
REL_MAX_DIST = 2048
N_BIAS_HEADS = DIL_HEADS + NSA_HEADS
N_EXPERTS = 16
N_EXPERT_GROUPS = 4
EXPERTS_PER_GROUP = N_EXPERTS // N_EXPERT_GROUPS
TOP_K = 2
D_EXPERT = 512
MOE_BLOCK = 128
PLE_DIM = 256
DEEPNORM_ALPHA = (2 * DEPTH) ** 0.25
DEEPNORM_BETA = (8 * DEPTH) ** -0.25
LN_EPS = 1e-5
NEG = -1e30
TINY = 1e-30

PROJ_SPLITS = (
    ('conv_b', CONV_DIM), ('conv_c', CONV_DIM), ('conv_h', CONV_DIM),
    ('dil_q', DIL_DIM), ('dil_k', DIL_DIM), ('dil_v', DIL_DIM),
    ('nsa_q', NSA_Q_DIM),
    ('cmp_k', NSA_KV_DIM), ('cmp_v', NSA_KV_DIM),
    ('sel_k', NSA_KV_DIM), ('sel_v', NSA_KV_DIM),
    ('win_k', NSA_KV_DIM), ('win_v', NSA_KV_DIM),
    ('nsa_gate', 3 * NSA_HEADS), ('merge_gate', 3 * D_MODEL),
)
PROJ_DIM = sum(w for _, w in PROJ_SPLITS)

kernel_name = 'hybrid_conv_dilated_nsa_moe_decoder_step'

F32 = jnp.float32

def layer_norm(x, g, b):
    xf = x.astype(F32)
    mu = xf.mean(-1, keepdims=True)
    var = jnp.square(xf - mu).mean(-1, keepdims=True)
    y = (xf - mu) * lax.rsqrt(var + LN_EPS) * g.astype(F32) + b.astype(F32)
    return y.astype(x.dtype)

def rel_bucket(dist):
    max_exact = REL_BUCKETS // 2
    d = jnp.maximum(dist, 0)
    df = jnp.maximum(d, 1).astype(F32)
    large = max_exact + (jnp.log(df / max_exact) / math.log(REL_MAX_DIST / max_exact)
                         * (REL_BUCKETS - max_exact)).astype(jnp.int32)
    return jnp.where(d < max_exact, d, jnp.minimum(large, REL_BUCKETS - 1))

def masked_softmax(s, valid):
    s = jnp.where(valid, s, NEG)
    m = jnp.max(s, axis=-1, keepdims=True)
    p = jnp.where(valid, jnp.exp(s - m), 0.0)
    return p / jnp.maximum(p.sum(-1, keepdims=True), TINY)

def split_projection(z):
    parts, off = {}, 0
    for name, width in PROJ_SPLITS:
        parts[name] = z[..., off:off + width]
        off += width
    return parts

def heads(t, n):
    return t.reshape(t.shape[:-1] + (n, HEAD_DIM))

def short_conv_mixer(parts, conv_prev, conv_w):
    u = parts['conv_c'] * parts['conv_h']
    u_ext = jnp.concatenate([conv_prev.astype(u.dtype), u], axis=1)
    T = u.shape[1]
    y = conv_w[0] * u_ext[:, 0:T]
    for k in range(1, CONV_WIDTH):
        y = y + conv_w[k] * u_ext[:, k:k + T]
    return parts['conv_b'] * y, u_ext[:, -(CONV_WIDTH - 1):]

def dilated_group_prompt(q, k, v, window, dilation, bias_tbl):
    B, S, H, dh = q.shape
    n_back = window // dilation
    span = dilation * DIL_BLOCK
    s_pad = -(-S // span) * span
    nb = s_pad // span

    def to_blocks(t):
        t = jnp.pad(t, ((0, 0), (0, s_pad - S), (0, 0), (0, 0)))
        return t.reshape(B, nb, DIL_BLOCK, dilation, H, dh)

    def with_prev(t):
        prev = jnp.pad(t, ((0, 0), (1, 0), (0, 0), (0, 0), (0, 0), (0, 0)))[:, :-1]
        return jnp.concatenate([prev, t], axis=2)

    qb = to_blocks(q)
    kk, vv = with_prev(to_blocks(k)), with_prev(to_blocks(v))
    s = jnp.einsum('bnqrhd,bnkrhd->bnrhqk', qb, kk).astype(F32) * (dh ** -0.5)
    qi = jnp.arange(DIL_BLOCK)[:, None]
    kj = jnp.arange(2 * DIL_BLOCK)[None, :]
    sd = DIL_BLOCK + qi - kj
    band = (sd >= 0) & (sd <= n_back)
    first = (jnp.arange(nb)[:, None, None] > 0) | (kj[None] >= DIL_BLOCK)
    valid = (band[None] & first)[None, :, None, None]
    bias = jnp.transpose(bias_tbl[rel_bucket(sd * dilation)], (2, 0, 1))
    s = jnp.where(valid, s + bias, NEG)
    m = s.max(-1, keepdims=True)
    p = jnp.exp(s - m)
    l = p.sum(-1, keepdims=True)
    o = jnp.einsum('bnrhqk,bnkrhd->bnqrhd', (p / l).astype(v.dtype), vv)
    lse = (m + jnp.log(l))[..., 0]
    o = o.reshape(B, s_pad, H, dh)[:, :S]
    lse = jnp.transpose(lse, (0, 1, 4, 2, 3)).reshape(B, s_pad, H)[:, :S]
    return o, lse

def dilated_group_sample(q, k_ctx, v_ctx, n_past, window, dilation, bias_tbl):
    T = q.shape[1]
    steps = jnp.arange(window // dilation + 1)
    idx = n_past + jnp.arange(T)[:, None] - steps[None, :] * dilation
    valid = idx >= 0
    idx = jnp.maximum(idx, 0)
    kg = jnp.take(k_ctx, idx, axis=1)
    vg = jnp.take(v_ctx, idx, axis=1)
    s = jnp.einsum('nthd,ntkhd->nthk', q, kg).astype(F32) * (HEAD_DIM ** -0.5)
    s = s + bias_tbl[rel_bucket(steps * dilation)].T
    s = jnp.where(valid[None, :, None, :], s, NEG)
    m = s.max(-1, keepdims=True)
    p = jnp.exp(s - m)
    l = p.sum(-1, keepdims=True)
    o = jnp.einsum('nthk,ntkhd->nthd', (p / l).astype(v_ctx.dtype), vg)
    return o, (m + jnp.log(l))[..., 0]

def combine_by_denominator(outs, lses):
    w = jax.nn.softmax(jnp.stack(lses, 0), axis=0)
    o = jnp.einsum('gnth,gnthd->nthd', w, jnp.stack(outs, 0).astype(F32))
    return o.reshape(o.shape[:2] + (DIL_OUT_DIM,))

def dilated_branch_prompt(parts, bias_dil):
    q, k, v = heads(parts['dil_q'], DIL_HEADS), heads(parts['dil_k'], DIL_HEADS), heads(parts['dil_v'], DIL_HEADS)
    S = q.shape[1]
    outs, lses, states = [], [], []
    for g, (window, dilation) in enumerate(DIL_PAIRS):
        hs = slice(g * DIL_GROUP_HEADS, (g + 1) * DIL_GROUP_HEADS)
        o, lse = dilated_group_prompt(q[:, :, hs], k[:, :, hs], v[:, :, hs], window, dilation, bias_dil[:, hs])
        outs.append(o)
        lses.append(lse)
        keep = min(window, S)
        states.append(jnp.stack([k[:, S - keep:, hs], v[:, S - keep:, hs]], axis=2))
    return combine_by_denominator(outs, lses).astype(q.dtype), states

def dilated_branch_sample(parts, bufs, bias_dil):
    q, k, v = heads(parts['dil_q'], DIL_HEADS), heads(parts['dil_k'], DIL_HEADS), heads(parts['dil_v'], DIL_HEADS)
    outs, lses, states = [], [], []
    for g, (window, dilation) in enumerate(DIL_PAIRS):
        hs = slice(g * DIL_GROUP_HEADS, (g + 1) * DIL_GROUP_HEADS)
        buf = bufs[g].astype(k.dtype)
        n_past = buf.shape[1]
        k_ctx = jnp.concatenate([buf[:, :, 0], k[:, :, hs]], axis=1)
        v_ctx = jnp.concatenate([buf[:, :, 1], v[:, :, hs]], axis=1)
        o, lse = dilated_group_sample(q[:, :, hs], k_ctx, v_ctx, n_past, window, dilation, bias_dil[:, hs])
        outs.append(o)
        lses.append(lse)
        states.append(jnp.stack([k[:, :, hs], v[:, :, hs]], axis=2))
    return combine_by_denominator(outs, lses).astype(q.dtype), states

def nsa_compress(rows, pos_emb, w1, w2):
    N, L, G, dh = rows.shape
    n_cmp = (L - CMP_BLOCK) // CMP_STRIDE + 1
    idx = jnp.arange(n_cmp)[:, None] * CMP_STRIDE + jnp.arange(CMP_BLOCK)[None, :]
    blocks = jnp.take(rows, idx, axis=1) + pos_emb[None, None, :, None, :]
    blocks = jnp.transpose(blocks, (0, 1, 3, 2, 4)).reshape(N, n_cmp, G, CMP_BLOCK * dh)
    return jax.nn.gelu(blocks @ w1) @ w2

def selected_attention(qg, q_pos, top_idx, top_valid, k_blocks, v_blocks, bias_g):
    Tq = qg.shape[1]
    C = Tq if Tq <= SEL_QCHUNK else SEL_QCHUNK
    n_chunks = Tq // C
    g_ar = jnp.arange(NSA_KV_HEADS)
    pos_chunks = q_pos.reshape(n_chunks, C)
    scale = HEAD_DIM ** -0.5

    def one_chunk(kb, vb, args):
        qc, ic, vc, pc = args
        it = jnp.transpose(ic, (1, 0, 2))
        kg = kb[g_ar[:, None, None], it]
        vg = vb[g_ar[:, None, None], it]
        s = jnp.einsum('cgjd,gckpd->cgjkp', qc, kg).astype(F32) * scale
        key_pos = ic[..., None] * SEL_BLOCK + jnp.arange(SEL_BLOCK)
        dist = pc[:, None, None, None] - key_pos
        valid = vc[..., None] & (dist >= 0)
        bias = bias_g[g_ar[None, :, None, None], rel_bucket(dist)]
        s = s + jnp.transpose(bias, (0, 1, 4, 2, 3))
        sh = s.shape
        p = masked_softmax(s.reshape(sh[:3] + (-1,)), valid.reshape(sh[0], sh[1], 1, -1))
        return jnp.einsum('cgjkp,gckpd->cgjd', p.reshape(sh).astype(vg.dtype), vg)

    def one_seq(args):
        qn, inn, vn, kb, vb = args
        split = lambda t: t.reshape((n_chunks, C) + t.shape[1:])
        o = lax.map(lambda a: one_chunk(kb, vb, a), (split(qn), split(inn), split(vn), pos_chunks))
        return o.reshape((Tq,) + o.shape[2:])

    return lax.map(one_seq, (qg, top_idx, top_valid, k_blocks, v_blocks))

def nsa_cmp_sel(qg, q_pos, kc_rows, vc_rows, ks_rows, vs_rows, cmp_pos, cmp_w1, cmp_w2, bias_g):
    N = qg.shape[0]
    L = kc_rows.shape[1]
    kc = nsa_compress(kc_rows, cmp_pos[0], cmp_w1[0], cmp_w2[0])
    vc = nsa_compress(vc_rows, cmp_pos[1], cmp_w1[1], cmp_w2[1])
    n_cmp = kc.shape[1]
    c_start = jnp.arange(n_cmp) * CMP_STRIDE
    c_valid = (c_start + CMP_BLOCK - 1)[None, :] <= q_pos[:, None]
    s = jnp.einsum('ntgjd,ncgd->ntgjc', qg, kc).astype(F32) * (HEAD_DIM ** -0.5)
    p_cmp = masked_softmax(s, c_valid[None, :, None, None, :])
    o_cmp = jnp.einsum('ntgjc,ncgd->ntgjd', p_cmp.astype(vc.dtype), vc)
    n_sel = -(-L // SEL_BLOCK)
    s_start = jnp.arange(n_sel) * SEL_BLOCK
    overlap = ((c_start[None, :] < s_start[:, None] + SEL_BLOCK)
               & (c_start[None, :] + CMP_BLOCK > s_start[:, None])).astype(F32)
    importance = jnp.einsum('ntgjc,sc->ntgs', p_cmp, overlap)
    blk = jnp.arange(n_sel)[None, :]
    cur = (q_pos // SEL_BLOCK)[:, None]
    s_valid = s_start[None, :] <= q_pos[:, None]
    forced = (blk == 0) | (blk == cur) | (blk == cur - 1)
    score = jnp.where(s_valid[None, :, None, :],
                      importance + jnp.where(forced, SEL_FORCE, 0.0)[None, :, None, :], NEG)
    top_score, top_idx = lax.top_k(score, min(SEL_TOPK, n_sel))
    top_valid = top_score > 0.5 * NEG
    pad = n_sel * SEL_BLOCK - L

    def to_blocks(r):
        r = jnp.pad(r, ((0, 0), (0, pad), (0, 0), (0, 0)))
        return jnp.transpose(r.reshape(N, n_sel, SEL_BLOCK, NSA_KV_HEADS, HEAD_DIM), (0, 3, 1, 2, 4))

    o_sel = selected_attention(qg, q_pos, top_idx, top_valid, to_blocks(ks_rows), to_blocks(vs_rows), bias_g)
    return o_cmp, o_sel

def nsa_window_prompt(qg, k, v, bias_g):
    N, S = qg.shape[:2]
    nb = S // WIN_BLOCK
    n_prev = -(-(NSA_WINDOW - 1) // WIN_BLOCK)
    qb = qg.reshape(N, nb, WIN_BLOCK, NSA_KV_HEADS, NSA_GROUP, HEAD_DIM)

    def band(t):
        tb = t.reshape(N, nb, WIN_BLOCK, NSA_KV_HEADS, HEAD_DIM)
        tp = jnp.pad(tb, ((0, 0), (n_prev, 0), (0, 0), (0, 0), (0, 0)))
        return jnp.concatenate([tp[:, i:i + nb] for i in range(n_prev + 1)], axis=2)

    kk, vv = band(k), band(v)
    s = jnp.einsum('nbqgjd,nbkgd->nbqgjk', qb, kk).astype(F32) * (HEAD_DIM ** -0.5)
    qi = jnp.arange(WIN_BLOCK)[:, None]
    kj = jnp.arange((n_prev + 1) * WIN_BLOCK)[None, :]
    dist = n_prev * WIN_BLOCK + qi - kj
    key_pos = jnp.arange(nb)[:, None, None] * WIN_BLOCK - n_prev * WIN_BLOCK + kj[None]
    valid = ((dist >= 0) & (dist < NSA_WINDOW))[None] & (key_pos >= 0)
    bias = jnp.transpose(bias_g[:, rel_bucket(dist)], (1, 0, 3, 2))
    p = masked_softmax(s + bias, valid[None, :, :, None, None, :])
    o = jnp.einsum('nbqgjk,nbkgd->nbqgjd', p.astype(vv.dtype), vv)
    return o.reshape(N, S, NSA_KV_HEADS, NSA_GROUP, HEAD_DIM)

def nsa_window_sample(qg, k_ctx, v_ctx, n_past, bias_g):
    T = qg.shape[1]
    Lc = k_ctx.shape[1]
    dist = (n_past + jnp.arange(T))[:, None] - jnp.arange(Lc)[None, :]
    valid = (dist >= 0) & (dist < NSA_WINDOW)
    s = jnp.einsum('ntgjd,nugd->ntgju', qg, k_ctx).astype(F32) * (HEAD_DIM ** -0.5)
    bias = jnp.transpose(bias_g[:, rel_bucket(dist)], (1, 0, 3, 2))
    p = masked_softmax(s + bias, valid[None, :, None, None, :])
    return jnp.einsum('ntgju,nugd->ntgjd', p.astype(v_ctx.dtype), v_ctx)

def nsa_combine(parts, o_cmp, o_sel, o_win):
    g = jax.nn.sigmoid(parts['nsa_gate'].astype(F32))
    g = g.reshape(g.shape[:2] + (3, NSA_KV_HEADS, NSA_GROUP, 1))
    o = g[:, :, 0] * o_cmp.astype(F32) + g[:, :, 1] * o_sel.astype(F32) + g[:, :, 2] * o_win.astype(F32)
    return o.reshape(o.shape[:2] + (NSA_Q_DIM,)).astype(parts['nsa_q'].dtype)

def nsa_rows(parts):
    return [heads(parts[n], NSA_KV_HEADS) for n in ('cmp_k', 'cmp_v', 'sel_k', 'sel_v', 'win_k', 'win_v')]

def nsa_branch_prompt(parts, cmp_pos, cmp_w1, cmp_w2, bias_g):
    q = heads(parts['nsa_q'], NSA_HEADS)
    N, S = q.shape[:2]
    qg = q.reshape(N, S, NSA_KV_HEADS, NSA_GROUP, HEAD_DIM)
    ck, cv, sk, sv, wk, wv = nsa_rows(parts)
    q_pos = jnp.arange(S, dtype=jnp.int32)
    o_cmp, o_sel = nsa_cmp_sel(qg, q_pos, ck, cv, sk, sv, cmp_pos, cmp_w1, cmp_w2, bias_g)
    o_win = nsa_window_prompt(qg, wk, wv, bias_g)
    keep = min(NSA_WINDOW, S)
    kv_rows = jnp.stack([ck, cv, sk, sv], axis=2)
    win_state = jnp.stack([wk[:, S - keep:], wv[:, S - keep:]], axis=2)
    return nsa_combine(parts, o_cmp, o_sel, o_win), kv_rows, win_state

def nsa_branch_sample(parts, kv_past, win_buf, cmp_pos, cmp_w1, cmp_w2, bias_g):
    q = heads(parts['nsa_q'], NSA_HEADS)
    N, T = q.shape[:2]
    qg = q.reshape(N, T, NSA_KV_HEADS, NSA_GROUP, HEAD_DIM)
    ck, cv, sk, sv, wk, wv = nsa_rows(parts)
    n_past = kv_past.shape[1]
    kv_new = jnp.stack([ck, cv, sk, sv], axis=2)
    kv_full = jnp.concatenate([kv_past.astype(kv_new.dtype), kv_new], axis=1)
    q_pos = n_past + jnp.arange(T, dtype=jnp.int32)
    o_cmp, o_sel = nsa_cmp_sel(qg, q_pos, kv_full[:, :, 0], kv_full[:, :, 1], kv_full[:, :, 2], kv_full[:, :, 3],
                               cmp_pos, cmp_w1, cmp_w2, bias_g)
    wb = win_buf.astype(wk.dtype)
    n_win = wb.shape[1]
    k_ctx = jnp.concatenate([wb[:, :, 0], wk], axis=1)
    v_ctx = jnp.concatenate([wb[:, :, 1], wv], axis=1)
    o_win = nsa_window_sample(qg, k_ctx, v_ctx, n_win, bias_g)
    win_new = jnp.stack([wk, wv], axis=2)
    return nsa_combine(parts, o_cmp, o_sel, o_win), kv_new, win_new

def merge_branches(parts, y_conv, y_dil, y_nsa, w_bc, w_bd, w_bn, w_o):
    g = jax.nn.sigmoid(parts['merge_gate'])
    g = g.reshape(g.shape[:-1] + (3, D_MODEL))
    m = g[..., 0, :] * (y_conv @ w_bc) + g[..., 1, :] * (y_dil @ w_bd) + g[..., 2, :] * (y_nsa @ w_bn)
    return m @ w_o

def moe_ffn(x2d, router_w, router_b, w_gate, w_up, w_down):
    n_tok = x2d.shape[0]
    affinity = jax.nn.sigmoid(jnp.matmul(x2d, router_w).astype(F32))
    grouped = (affinity + router_b.astype(F32)).reshape(n_tok, N_EXPERT_GROUPS, EXPERTS_PER_GROUP)
    group_score = lax.top_k(grouped, TOP_K)[0].sum(-1)
    best = jnp.argmax(group_score, axis=-1)
    in_group = jnp.take_along_axis(grouped, best[:, None, None], axis=1)[:, 0]
    local = lax.top_k(in_group, TOP_K)[1]
    expert = best[:, None] * EXPERTS_PER_GROUP + local
    a = jnp.take_along_axis(affinity, expert, axis=1)
    gate = a / a.sum(-1, keepdims=True)
    n_assign = n_tok * TOP_K
    e_flat = expert.reshape(-1)
    tok_flat = jnp.repeat(jnp.arange(n_tok, dtype=jnp.int32), TOP_K)
    order = jnp.argsort(e_flat)
    e_s, tok_s, g_s = e_flat[order], tok_flat[order], gate.reshape(-1)[order]
    counts = jnp.bincount(e_flat, length=N_EXPERTS)
    padded = (counts + MOE_BLOCK - 1) // MOE_BLOCK * MOE_BLOCK
    p_end = jnp.cumsum(padded)
    dst = (p_end - padded)[e_s] + jnp.arange(n_assign) - (jnp.cumsum(counts) - counts)[e_s]
    n_blocks = -(-(n_assign + N_EXPERTS * (MOE_BLOCK - 1)) // MOE_BLOCK)
    n_rows = n_blocks * MOE_BLOCK
    row_tok = jnp.zeros((n_rows,), jnp.int32).at[dst].set(tok_s)
    row_gate = jnp.zeros((n_rows,), F32).at[dst].set(g_s)
    blk_expert = jnp.minimum(jnp.searchsorted(p_end, jnp.arange(n_blocks) * MOE_BLOCK, side='right'),
                             N_EXPERTS - 1)

    def expert_block(args):
        toks, e = args
        xb = x2d[toks]
        h = jax.nn.silu(xb @ w_gate[e]) * (xb @ w_up[e])
        return h @ w_down[e]

    rows = lax.map(expert_block, (row_tok.reshape(n_blocks, MOE_BLOCK), blk_expert))
    y = jnp.zeros((n_tok, D_MODEL), F32).at[row_tok].add(
        rows.reshape(n_rows, D_MODEL).astype(F32) * row_gate[:, None])
    return y.astype(x2d.dtype)

def channel_and_ple(x, mix, p_l, ln1_g, ln1_b, ln2_g, ln2_b, router_w, router_b,
                    w_gate, w_up, w_down, ple_gate, ple_proj):
    x = layer_norm(x * DEEPNORM_ALPHA + mix, ln1_g, ln1_b)
    N, T, _ = x.shape
    ffn = moe_ffn(x.reshape(N * T, D_MODEL), router_w, router_b, w_gate, w_up, w_down).reshape(N, T, D_MODEL)
    ple = jax.nn.sigmoid(x @ ple_gate) * (p_l.astype(x.dtype) @ ple_proj)
    return layer_norm(x * DEEPNORM_ALPHA + ffn + ple, ln2_g, ln2_b)

def setup_inputs(seed: int = 0) -> dict:
    key = jax.random.key(seed)
    keys = iter(jax.random.split(key, 48))

    def nrm(shape, scale=1.0):
        return jax.random.normal(next(keys), shape, F32) * scale

    n_pages = PAST_LEN // PAGE_SIZE
    n_used = DEC_BATCH * n_pages
    n_pool = n_used + n_used // 4
    perm = jax.random.permutation(next(keys), n_pool).astype(jnp.int32)
    page_table = perm[:n_used].reshape(DEC_BATCH, n_pages)

    def dil_buf(g):
        return nrm((DEPTH, DEC_BATCH, min(DIL_PAIRS[g][0], PAST_LEN), 2, DIL_GROUP_HEADS, HEAD_DIM))

    return {
        'x_prompt': nrm((BATCH, SEQ, D_MODEL)),
        'x_sample': nrm((DEC_BATCH, DEC_SEQ, D_MODEL)),
        'state_conv': nrm((DEPTH, DEC_BATCH, CONV_WIDTH - 1, CONV_DIM)),
        'cache_dil_w128': dil_buf(0),
        'cache_dil_w512': dil_buf(1),
        'cache_dil_w2048': dil_buf(2),
        'cache_nsa_win': nrm((DEPTH, DEC_BATCH, min(NSA_WINDOW, PAST_LEN), 2, NSA_KV_HEADS, HEAD_DIM)),
        'cache_nsa_kv': nrm((DEPTH, n_pool, PAGE_SIZE, 4, NSA_KV_HEADS, HEAD_DIM)),
        'page_table': page_table,
        'p_prompt': nrm((DEPTH, BATCH, SEQ, PLE_DIM)),
        'p_sample': nrm((DEPTH, DEC_BATCH, DEC_SEQ, PLE_DIM)),
        'w_in': nrm((DEPTH, D_MODEL, PROJ_DIM), D_MODEL ** -0.5),
        'conv_w': nrm((DEPTH, CONV_WIDTH, CONV_DIM), CONV_WIDTH ** -0.5),
        'cmp_pos': nrm((DEPTH, 2, CMP_BLOCK, HEAD_DIM), 0.1),
        'cmp_w1': nrm((DEPTH, 2, CMP_BLOCK * HEAD_DIM, CMP_HIDDEN), (CMP_BLOCK * HEAD_DIM) ** -0.5),
        'cmp_w2': nrm((DEPTH, 2, CMP_HIDDEN, HEAD_DIM), CMP_HIDDEN ** -0.5),
        'w_branch_conv': nrm((DEPTH, CONV_DIM, D_MODEL), CONV_DIM ** -0.5 * DEEPNORM_BETA),
        'w_branch_dil': nrm((DEPTH, DIL_OUT_DIM, D_MODEL), DIL_OUT_DIM ** -0.5 * DEEPNORM_BETA),
        'w_branch_nsa': nrm((DEPTH, NSA_Q_DIM, D_MODEL), NSA_Q_DIM ** -0.5 * DEEPNORM_BETA),
        'w_out': nrm((DEPTH, D_MODEL, D_MODEL), D_MODEL ** -0.5 * DEEPNORM_BETA),
        'ln1_g': 1.0 + nrm((DEPTH, D_MODEL), 0.05),
        'ln1_b': nrm((DEPTH, D_MODEL), 0.02),
        'ln2_g': 1.0 + nrm((DEPTH, D_MODEL), 0.05),
        'ln2_b': nrm((DEPTH, D_MODEL), 0.02),
        'router_w': nrm((D_MODEL, N_EXPERTS), D_MODEL ** -0.5),
        'router_b': nrm((N_EXPERTS,), 0.01),
        'expert_w_gate': nrm((DEPTH, N_EXPERTS, D_MODEL, D_EXPERT), D_MODEL ** -0.5),
        'expert_w_up': nrm((DEPTH, N_EXPERTS, D_MODEL, D_EXPERT), D_MODEL ** -0.5),
        'expert_w_down': nrm((DEPTH, N_EXPERTS, D_EXPERT, D_MODEL), D_EXPERT ** -0.5 * DEEPNORM_BETA),
        'ple_w_gate': nrm((DEPTH, D_MODEL, D_MODEL), D_MODEL ** -0.5),
        'ple_w_proj': nrm((DEPTH, PLE_DIM, D_MODEL), PLE_DIM ** -0.5 * DEEPNORM_BETA),
        'rel_bias': nrm((REL_BUCKETS, N_BIAS_HEADS), 0.2),
    }

def reference(x_prompt, x_sample, state_conv, cache_dil_w128, cache_dil_w512, cache_dil_w2048,
              cache_nsa_win, cache_nsa_kv, page_table, p_prompt, p_sample,
              w_in, conv_w, cmp_pos, cmp_w1, cmp_w2, w_branch_conv, w_branch_dil, w_branch_nsa, w_out,
              ln1_g, ln1_b, ln2_g, ln2_b, router_w, router_b, expert_w_gate, expert_w_up, expert_w_down,
              ple_w_gate, ple_w_proj, rel_bias):
    bias_dil = rel_bias[:, :DIL_HEADS]
    bias_nsa = jnp.transpose(rel_bias[:, DIL_HEADS:].reshape(REL_BUCKETS, NSA_KV_HEADS, NSA_GROUP), (1, 0, 2))
    dil_caches = (cache_dil_w128, cache_dil_w512, cache_dil_w2048)
    xp, xs = x_prompt, x_sample
    conv_p, conv_s, win_p, win_s, kv_p, kv_s = [], [], [], [], [], []
    dil_p = [[] for _ in DIL_PAIRS]
    dil_s = [[] for _ in DIL_PAIRS]
    for l in range(DEPTH):
        tail = (ln1_g[l], ln1_b[l], ln2_g[l], ln2_b[l], router_w, router_b,
                expert_w_gate[l], expert_w_up[l], expert_w_down[l], ple_w_gate[l], ple_w_proj[l])
        branch_w = (w_branch_conv[l], w_branch_dil[l], w_branch_nsa[l], w_out[l])
        parts = split_projection(xp @ w_in[l])
        conv0 = jnp.zeros((xp.shape[0], CONV_WIDTH - 1, CONV_DIM), xp.dtype)
        y_conv, c_st = short_conv_mixer(parts, conv0, conv_w[l])
        y_dil, d_st = dilated_branch_prompt(parts, bias_dil)
        y_nsa, kv_rows, w_st = nsa_branch_prompt(parts, cmp_pos[l], cmp_w1[l], cmp_w2[l], bias_nsa)
        xp = channel_and_ple(xp, merge_branches(parts, y_conv, y_dil, y_nsa, *branch_w), p_prompt[l], *tail)
        conv_p.append(c_st)
        win_p.append(w_st)
        kv_p.append(kv_rows)
        for g in range(len(DIL_PAIRS)):
            dil_p[g].append(d_st[g])
        parts = split_projection(xs @ w_in[l])
        y_conv, c_st = short_conv_mixer(parts, state_conv[l], conv_w[l])
        y_dil, d_st = dilated_branch_sample(parts, tuple(c[l] for c in dil_caches), bias_dil)
        pages = cache_nsa_kv[l][page_table]
        kv_past = pages.reshape((pages.shape[0], pages.shape[1] * pages.shape[2]) + pages.shape[3:])
        y_nsa, kv_rows, w_st = nsa_branch_sample(parts, kv_past, cache_nsa_win[l], cmp_pos[l], cmp_w1[l],
                                                 cmp_w2[l], bias_nsa)
        xs = channel_and_ple(xs, merge_branches(parts, y_conv, y_dil, y_nsa, *branch_w), p_sample[l], *tail)
        conv_s.append(c_st)
        win_s.append(w_st)
        kv_s.append(kv_rows)
        for g in range(len(DIL_PAIRS)):
            dil_s[g].append(d_st[g])
    return (xp, xs,
            jnp.stack(conv_p), jnp.stack(conv_s),
            jnp.stack(dil_p[0]), jnp.stack(dil_s[0]),
            jnp.stack(dil_p[1]), jnp.stack(dil_s[1]),
            jnp.stack(dil_p[2]), jnp.stack(dil_s[2]),
            jnp.stack(win_p), jnp.stack(win_s),
            jnp.stack(kv_p), jnp.stack(kv_s))


_drawn_inputs = setup_inputs


def setup_inputs(seed=0):
    import zlib

    import numpy as np

    out = dict(_drawn_inputs(seed))
    spreads = {}
    factors = {'ln2_b': 2.912}
    for name, (base, spread) in spreads.items():
        noise = np.random.default_rng([zlib.crc32(name.encode()), seed]).standard_normal(out[name].shape)
        drawn = base * np.exp(spread * noise) if base else spread * noise
        out[name] = jnp.asarray(drawn.astype(out[name].dtype))
    for name, factor in factors.items():
        out[name] = (out[name] * factor).astype(out[name].dtype)
    return out
```

```python
from contextlib import ExitStack

import numpy as np

import concourse.bass as bass
from concourse import mybir

F32 = mybir.dt.float32
I32 = mybir.dt.int32
U32 = mybir.dt.uint32
ALU = mybir.AluOpType
ACT = mybir.ActivationFunctionType
AX_X = mybir.AxisListType.X

P = 128
D = 1024
KC = D // P
SEQ = 512
NSEQ = 8
TNEW = 8
NS = NSEQ * TNEW
TOK = SEQ + NS
NT = (TOK + P - 1) // P
QT = SEQ // P
HALF = TOK // 2
PAST = 256
DH = 64
CONV = 512
PAGE_COLS = 512
CMP_BLOCK, CMP_STRIDE, CMP_HID = 32, 16, 128
N_EXP, D_EXP = 16, 512
MERGE0 = 5144
NEG = -1e30
TINY = 1e-30
CLAMP = 1e29
ALPHA = 2.0 ** 0.25
LN_EPS = 1e-5
RLEN = 640
NCMP = (SEQ + NSEQ * PAST) // CMP_STRIDE
ROWS_W = SEQ + NSEQ * PAST + CMP_BLOCK + NS
POS0 = SEQ + NSEQ * PAST
NEW0 = POS0 + CMP_BLOCK
PROMPT_CMP = (SEQ - CMP_BLOCK) // CMP_STRIDE + 1
SAMPLE_CMP = (PAST + TNEW - CMP_BLOCK) // CMP_STRIDE + 1
BIG_BLOCKS = (TOK + P - 1) // P
N_BLOCK = N_EXP * BIG_BLOCKS
VW = 1176
SEL_V, WIN_K, WIN_V, GATES = 768, 896, 1024, 1152
KT_W = 2 * 136 + 4 * 264 + 2 * 264
SCALE = DH ** -0.5


def token_rows(i):
    return P if i < NT - 1 else NS


def bucket_of(dist):
    if dist < 16:
        return dist
    return min(16 + int(np.log(dist / 16) / np.log(2048 / 16) * 16), 31)


def bias_one_hot():
    hot = np.zeros((33, 4, RLEN), np.float32)
    for kind, (step, reach) in enumerate([(1, 511), (1, 128), (4, 512), (16, 2048)]):
        for i in range(RLEN):
            dist = 511 - i
            masked = dist < 0 or dist % step or dist > reach
            hot[32 if masked else bucket_of(dist), kind, i] = 1.0
    return hot


def shape_constants():
    query = np.arange(SEQ)[:, None]
    end = np.arange(PROMPT_CMP)[None, :] * CMP_STRIDE + CMP_BLOCK - 1
    unseen = np.where(end <= query, 0.0, NEG).astype(np.float32)
    ramp = np.zeros((P, 52), np.float32)
    ramp[:, 0:16] = 16 - np.arange(16)
    ramp[:, 16:20] = 4 - np.arange(4)
    ramp[:, 20:36] = np.arange(16) * P
    ramp[:, 36:52] = np.arange(16)
    token = np.arange(NT)[None, :] * P + np.arange(P)[:, None]
    return {
        "c_ident": np.eye(P, dtype=np.float32),
        "c_before": np.triu(np.ones((P, P), np.float32), 1),
        "c_hot": bias_one_hot(),
        "c_neg": np.full((1, 20), NEG, np.float32),
        "c_unseen": np.ascontiguousarray(unseen.reshape(QT, P, PROMPT_CMP).transpose(1, 0, 2)),
        "c_ramp": ramp,
        "c_token": token.astype(np.int32),
    }


GROUPS = [(512, 512), (1024, 512), (0, 512), (4352, 384), (4736, 408), (3072, 384), (3456, 384),
          (1536, 384), (1920, 384), (2304, 384), (2688, 384), (3840, 512)]
WSLOTS = 3
NSA_Q_GROUP = 11
FEATURE = {"conv_c": (0, 4), "conv_h": (1, 4), "conv_b": (2, 4), "cmp": (3, 3), "dil_q": (7, 3),
           "dil_k": (9, 3), "nsa_q": (11, 4)}


def projection_tasks():
    t = [("x_T", (i, h)) for i in range(NT) for h in range(2)]
    t += [("bias_row", k) for k in range(4)]
    t += [("state_T", 0)]
    t += [("conv_c", c) for c in range(4)] + [("conv_h", c) for c in range(4)]
    t += [("u_T", 0)]
    t += [("conv_b", c) for c in range(4)]
    t += [("pos_T", 0)]
    t += [("cmp", c) for c in range(3)]
    t += [("rows", (c, i)) for c in range(3) for i in range(NT)]
    t += [("win_k_T", 0)]
    t += [("page_T", s) for s in range(NSEQ)]
    t += [("dil_q", c) for c in range(6)] + [("dil_k", c) for c in range(6)]
    t += [("k_rows", c) for c in range(9)]
    t += [("nsa_q", c) for c in range(4)]
    t += [("hidden", (kv, g)) for kv in range(2) for g in range(2)]
    t += [("cmp_k_T", 0), ("cmp_v", 0), ("cmp_v", 1)]
    return t


ACT_EMPTIES = {"conv_c", "u_T", "cmp", "dil_k", "hidden"}


def emptied_by_act(kind, a):
    if kind == "x_T":
        return a[1] == 1
    if kind == "rows":
        return a[1] % 2 == 1
    if kind == "cmp":
        return a < 2
    if kind in ("dil_q", "nsa_q"):
        return a % 2 == 1
    return kind in ACT_EMPTIES


def owners(tasks, by_act):
    done, out = [0, 0], []
    for kind, a in tasks:
        act = by_act(kind, a)
        done[act] += 1
        out.append((act, done[act]))
    return out, done[1], done[0]


def attention_units():
    dil = [("dil", 2 * c + r, qt) for c in range(2) for qt in range(QT) for r in range(2)]
    nsa = [("nsa", (g, j), qt) for j in range(4) for qt in range(QT) for g in range(2)]
    return dil + nsa


def sample_units():
    out = []
    for half in range(2):
        out += [("sdil", half, 0), ("snsa", 2 * half, 0), ("snsa", 2 * half + 1, 0)]
    return out


UNITS = attention_units() + sample_units()
N_PROMPT = QT * 12


def segments(unit):
    kind, _, qt = unit
    if kind == "dil":
        return [P * min(2, qt + 1), P * (qt + 1), P * (qt + 1)]
    if kind == "nsa":
        return [PROMPT_CMP, P * (qt + 1), P * (qt + 1)]
    if kind == "sdil":
        return [136, 264, 264]
    return [SAMPLE_CMP, 264, 264]


def first_column(unit, s):
    if unit[0] in ("dil", "nsa"):
        return (0, 256, 768)[s]
    return (0, 136, 400)[s] if unit[0] == "sdil" else (0, 16, 280)[s]


def key_tiles(unit):
    out = []
    for s, w in enumerate(segments(unit)):
        out += [(s, a, min(P, w - a)) for a in range(0, w, P)]
    return out


def begins_half(u):
    return u < len(UNITS) and UNITS[u][0] == "sdil"


def fill_plan():
    fills = []
    for u in range(len(UNITS) + 3):
        if 2 <= u < len(UNITS) + 2:
            tiles = len(key_tiles(UNITS[u - 2]))
            fills += [("probs", u - 2, f) for f in range((tiles + 3) // 4)]
        if begins_half(u):
            half = UNITS[u][1]
            fills += [("keys", 4 * half + n, f) for n in range(4) for f in range(4)]
        if u >= 4 and UNITS[u - 4][0] == "sdil":
            fills.append(("sums", u - 4, 0))
    return fills


FILLS = fill_plan()


def later_tasks():
    t = []
    for c in range(KC):
        for b in range(3):
            t += [("gate", (c, b)), ("branch", (c, b))]
    t += [("mix", i) for i in range(NT)]
    t += [("x1_T", (i, h)) for i in range(NT) for h in range(2)]
    t += [("router", 0)]
    t += [("p_T", i) for i in range(NT)]
    for i in range(NT):
        t += [("ple_gate", i), ("ple_proj", i)]
        if i == 1:
            t += [("rank", 0)]
    return t


def later_by_act(kind, a):
    return kind in ("gate", "ple_gate", "router") or (kind == "x1_T" and a[1] == 1)


def emptied_before(owner, n):
    return owner[n]


def bass_hybrid_decoder_step_kernel(nc, A, C, O):
    proj = projection_tasks()
    p_owner, p_act, p_dve = owners(proj, emptied_by_act)
    at = {}
    for n, t in enumerate(proj):
        at[t] = n
    later = later_tasks()
    l_owner, l_act, l_dve = owners(later, later_by_act)
    lat = {t: n for n, t in enumerate(later)}
    fill_at = {f: n for n, f in enumerate(FILLS)}
    f_owner, f_act, f_dve = owners([(k, (w, f)) for k, w, f in FILLS], lambda k, a: k == "probs")

    def group_of(kind, a):
        if kind == "rows":
            return 4 + a[0], 0
        first, n = FEATURE[kind]
        return first + a // n, a % n * P

    group_done = [0] * len(GROUPS)
    for n, (kind, a) in enumerate(proj):
        if kind in FEATURE or kind == "rows":
            group_done[group_of(kind, a)[0]] = n + 1

    ctx = ExitStack()
    with ctx:
        arena = ctx.enter_context(nc.sbuf_tensor("arena", [P, 53200], F32))
        ps = ctx.enter_context(nc.psum_tensor("ps", [P, 8, 512], F32))

        def sem(name):
            return ctx.enter_context(nc.semaphore(name))

        def sems(name, n):
            return [sem(f"{name}{i}") for i in range(n)]

        def view(off, *shape):
            n = int(np.prod(shape))
            flat = arena[:, off:off + n]
            if len(shape) == 1:
                return flat
            names = "abcde"[:len(shape)]
            sizes = {c: s for c, s in zip(names, shape)}
            return flat.rearrange(f"p ({' '.join(names)}) -> p {' '.join(names)}", **sizes)

        def dram(name, shape, dt=F32):
            return nc.dram_tensor(name, shape, dt, kind="Internal").ap()

        xT = view(0, KC, TOK)
        qT = view(4608, 10, TOK)
        kT = view(10368, 8, TOK)
        vtok = view(14976, NT, VW)
        yconvT = view(20856, 4, TOK)
        ydilT = view(23160, 2, TOK)
        ynsaT = view(24312, 4, TOK)
        hot = view(23160, 4, RLEN)
        bias_rows = view(14976, 4, RLEN)
        state_tok = view(25720, CONV)
        pos_tok = view(26232, P)
        u_rows = view(25720, CONV)
        wslot = [view(26616 + 4096 * i, 4096) for i in range(WSLOTS)]
        xtok = view(38904, NT, D)
        rowsT = view(38904, 2, ROWS_W)
        uext_flat = view(44216, 4, 594)
        conv_tmp = view(46592, 4, TOK)
        stage = [view(48896 + 640 * i, NT, P) for i in range(3)]
        pages = [view(50816 + 512 * i, 2, 256) for i in range(2)]
        w1 = view(26616, 2, CMP_BLOCK, CMP_HID)
        hidden = view(44216, 4, 160)
        vcs = view(44856, NSEQ, P)
        vcp = view(45880, P)
        w2 = view(46008, 2, DH)
        kcT = view(46136, 160)
        tab_dil0 = view(26616, 4, 256)
        tab_dil = view(27640, 2, 4, 512)
        tab_nsa = view(31736, 8, 512)
        probs = [view(o, 1280) for o in (42232, 35832, 37112)]
        probsT = [view(38904 + 1280 * i, 10, P) for i in range(2)]
        q_pad = [view(41464 + 384 * r, 3, P) for r in range(2)]
        cacheT = [view(4608 + KT_W * i, KT_W) for i in range(4)]
        new_dil_v = [view(o, 768) for o in (12032, 12800, 13568, 34712)]
        new_nsa_v = [view(o, 256) for o in (14336, 14592, 38392, 35480)]
        sum_rows = view(46296, 256)
        k_new = view(43512, 8, NS)
        q_nsa = view(44216, NSEQ, 64)
        k_cache = [view(o, 1792) for o in (46592, 48384, 41464)]
        q_dil = view(50176, 6, NSEQ, 32)
        v_cache = [view(26616 + 1792 * i, 1792) for i in range(4)]
        tab_sdil = view(33784, 664)
        tab_snsa = view(34448, 264)
        sample_probs = [view(o, 664) for o in (36448, 35832, 37112)]
        gate_w = [view(26616 + 6144 * i, KC, 3, 256) for i in range(2)]
        w_conv = view(38904, 4, D)
        w_dil = view(43000, 2, D)
        w_nsa = view(45048, 4, D)
        sig = [view(49144 + 576 * i, TOK) for i in range(2)]
        gated = view(50296, TOK)
        mT = view(14976, KC, TOK)
        w_out = view(4608, KC, D)
        res = view(46720, NT, D)
        x1T = view(42112, KC, TOK)
        ln = view(38016, 4, D)
        ple_w = view(29824, KC, D)
        ple_p = view(27776, 2, D)
        p_tok = view(24576, NT, 256)
        pT = view(25856, 2, TOK)
        ple_sig = [view(19584 + 1024 * i, D) for i in range(2)]
        group_score = view(21632 + 80 * 12, NT, 4)
        group_hot = view(21632 + 80 * 13, NT, 4)
        pair_sums = view(21632 + 80 * 14, NT, 4, 6)

        def routing(k):
            return view(21632 + 80 * k, NT, 16)

        ew = [[view(12288 * i + 4096 * j, 4096) for j in range(3)] for i in range(2)]
        xg = [view(29824 + 1024 * i, D) for i in range(2)]
        xgT = [view(31872 + 1024 * i, KC, P) for i in range(2)]
        silu = view(33920, D_EXP)
        h_tok = view(34432, D_EXP)
        hT = view(34944, 4, P)
        y_exp = [view(35456 + 1024 * i, D) for i in range(2)]
        picked = [[view(42112 + 2048 * i + 1024 * j, D) for j in range(2)] for i in range(2)]
        ident = view(51840, P)
        before = view(51968, P)
        ones = view(52096, P)
        ramp = view(52224, 52)
        unseen = view(52280, QT, PROMPT_CMP)
        conv_w = view(52404, 4, 3)
        token_f = view(52416, NT)
        rel = view(52424, 20)
        nsa_gate = view(52444, NT, 24)
        gate_s = view(52564, 4, 3)
        router_w = view(52576, KC, 16)
        router_b = view(52704, 16)
        u_last = view(52720, 4, 18)
        stat = [[view(52792 + 16 * i + 4 * j, 3) for j in range(4)] for i in range(2)]
        gelu_b = view(52824, 4)
        lnst = view(52828, 12)
        lnmv = view(52840, 2)
        lnsd = view(52842, 4)
        gates2 = view(52846, 2, NT)
        dst_f = view(52856, 4, NT)
        tmp1 = view(52876, 20)
        token = view(52416, NT).bitcast(I32)
        dst_i = view(52896, 4, NT).bitcast(U32)
        count_i = view(52916, 1).bitcast(I32)
        block_tok = view(52920, N_BLOCK).bitcast(U32)
        page_ids = view(53000, 16).bitcast(I32)
        zeros_i = view(53016, N_BLOCK).bitcast(I32)

        bias_d = dram("bias_d", [20, P, RLEN])
        gates_d = dram("gates_d", [NS, 24])
        x1_d = dram("x1_d", [TOK, D])
        list_d = dram("list_d", [P * N_BLOCK, 1], I32)
        y_d = dram("y_d", [N_BLOCK * P, D])

        x_in = sems("x_in", NT)
        const_in = sem("const_in")
        early_in = sem("early_in")
        w_in = sems("w_in", WSLOTS)
        page_in = sems("page_in", 2)
        page_ids_in = sem("page_ids_in")
        filled = sem("filled")
        act_emptied, dve_emptied = sem("act_emptied"), sem("dve_emptied")
        zeroed = sem("zeroed")
        u_ready = sem("u_ready")
        bias_out = sem("bias_out")
        u_out = sem("u_out")
        stage_out = sems("stage_out", 3)
        v_out = sem("v_out")
        cmp_in = sem("cmp_in")
        tables_in = sem("tables_in")
        sample_tables_in = sem("sample_tables_in")
        gates_ready, gates_out, gates_in = sem("gates_ready"), sem("gates_out"), sem("gates_in")
        k_in, dil_v_in, nsa_v_in = sems("k_in", 3), sems("dil_v_in", 4), sems("nsa_v_in", 4)
        q_pad_zeroed = sem("q_pad_zeroed")
        q_put = sem("q_put")
        queries_zeroed = sem("queries_zeroed")
        queries_built = sem("queries_built")
        keys_kept = sem("keys_kept")
        new_keys_put = sem("new_keys_put")
        scored = sem("scored")
        score_read = sem("score_read")
        max_ready = sem("max_ready")
        exp_ready = sem("exp_ready")
        scaled = sem("scaled")
        turned = sem("turned")
        act_turned, dve_turned = sem("act_turned"), sem("dve_turned")
        summed = sem("summed")
        out_read = sem("out_read")
        merge_w_in, gate_w_in, w_out_in = sem("merge_w_in"), sems("gate_w_in", 2), sem("w_out_in")
        res_in, late_in, ple_in = sems("res_in", NT), sem("late_in"), sem("ple_in")
        later_filled = sem("later_filled")
        act_later, dve_later = sem("act_later"), sem("dve_later")
        var_ready, sqrt_ready = sem("var_ready"), sem("sqrt_ready")
        x1_ready, x1_stored = sem("x1_ready"), sems("x1_stored", NT)
        route_zeroed, chosen = sem("route_zeroed"), sem("chosen")
        indices_ready = sem("indices_ready")
        zeros_ready, list_zeroed, listed, list_in = sem("zeros_ready"), sem("list_zeroed"), sem("listed"), sem("list_in")
        res_ready = sem("res_ready")
        ew_in = [sems(f"{w}_in", 2) for w in ("gate_w_e", "up_w_e", "down_w_e")]
        xg_in = sems("xg_in", 2)
        x_turned, gated_done, up_done, h_turned, down_done = (sem(s) for s in
            ("x_turned", "gated_done", "up_done", "h_turned", "down_done"))
        act_x, dve_x, silu_done, h_ready, hT_ready = (sem(s) for s in ("act_x", "dve_x", "silu_done", "h_ready", "hT_ready"))
        act_y, dve_y, y_stored = sem("act_y"), sem("dve_y"), sems("y_stored", 2)
        over = {name: sem("over_" + name) for name in
                ("w", "x", "x_turned", "act_x", "dve_x", "gated", "up", "silu", "h", "h_turned", "hT", "down",
                 "act_y", "dve_y", "stored", "list")}
        picked_in = sems("picked_in", 2)
        combined, y_out = sem("combined"), sem("y_out")
        dve_chain, act_chain, pool_chain = sem("dve_chain"), sem("act_chain"), sem("pool_chain")

        block = ctx.enter_context(nc.Block())

        def bank(n, b):
            return ps[:, 2 * (n % 4) + b, :]

        def pair(n):
            return ps[:, 2 * (n % 4):2 * (n % 4) + 2, :]

        def wait_emptied(eng, owner, n, act_sem, dve_sem):
            by_act, count = owner[n]
            eng.wait_ge(act_sem if by_act else dve_sem, count)

        def proj_emptied(eng, *task):
            wait_emptied(eng, p_owner, at[task], act_emptied, dve_emptied)

        def chained(eng, chain):
            count = [0]

            def link(ins):
                count[0] += 1
                ins.then_inc(chain, 1)
                eng.wait_ge(chain, count[0])
            return link

        x_p, x_s = A["x_prompt"][0], A["x_sample"].rearrange("n t d -> (n t) d")

        def x_rows(i):
            return x_p[i * P:(i + 1) * P, :] if i < QT else x_s

        def weights_of(kind, a):
            g, col = group_of(kind, a)
            w = GROUPS[g][1]
            slot = wslot[g % WSLOTS][:, 0:KC * w].rearrange("p (k c) -> p k c", k=KC)
            return lambda k: slot[:, k, col:col + P]

        kv_pool = A["cache_nsa_kv"][0].rearrange("n r k g d -> n r (k g d)")


        def bias_ap(head, start, *dims):
            return bass.AP(tensor=bias_d.tensor, offset=head * P * RLEN + start, ap=[list(d) for d in dims])

        caches = [A["cache_dil_w128"], A["cache_dil_w512"], A["cache_dil_w2048"], A["cache_nsa_win"]]

        def load_rows(eng, t, n, kv, dst, signal):
            src = caches[t][0, n].rearrange("r k h d -> r k (h d)")[:, kv]
            rows, w = src.shape
            o = (0, 256, 768, 1536)[t]
            eng.dma_start(dst[:, o:o + rows // P * w].rearrange("p (a c) -> p a c", c=w),
                          src.rearrange("(a p) c -> p a c", p=P)).then_inc(signal, 16)

        def probs_of(u, s, a, w):
            o = first_column(UNITS[u], s) + a
            return (probs if u < N_PROMPT else sample_probs)[u % 3][:, o:o + w]

        def turn_bank(f):
            return ps[:, 4 + f % 2, :]

        def fill_emptied(eng, kind, which, f):
            wait_emptied(eng, f_owner, fill_at[kind, which, f], act_turned, dve_turned)

        def proj_all_emptied(eng):
            eng.wait_ge(act_emptied, p_act)
            eng.wait_ge(dve_emptied, p_dve)

        def cache_key_rows(n, f):
            if f == 0:
                return cacheT[n % 4][:, 0:272].rearrange("p (r c) -> p r c", r=2)[:, :, 0:P]
            o = 272 + 528 * (f - 1)
            return cacheT[n % 4][:, o:o + 528].rearrange("p (r c) -> p r c", r=2)[:, :, 0:PAST]

        def later_emptied(eng, *task):
            wait_emptied(eng, l_owner, lat[task], act_later, dve_later)

        def halves(ap):
            return ap.rearrange("p (b c) -> p b c", b=2)

        sample_u = [uext_flat[:, c, 2 + SEQ:594].rearrange("p (s t) -> p s t", s=NSEQ) for c in range(4)]

        def copy_rows(eng, n, a):
            c, i = a
            m, w, dst = token_rows(i), GROUPS[4 + c][1], (768, 0, 384)[c]
            src = bank(n, 0)[0:m, 0:w]
            return eng.copy(vtok[0:m, i, dst:dst + w], src) if eng is nc.scalar or p_owner[n][0] else \
                eng.tensor_copy(vtok[0:m, i, dst:dst + w], src)

        def token_view(name):
            return O[name].rearrange("l n t k g d -> (l n t) (k g d)")

        def store_rows(eng, name, col, src, w):
            first = QT - O[name + "_prompt"].shape[2] // P
            dst = token_view(name + "_prompt").rearrange("(i p) c -> p i c", p=P)
            eng.dma_start(dst[:, :, col:col + w], vtok[:, first:QT, src:src + w]).then_inc(v_out, 16)
            eng.dma_start(token_view(name + "_sample")[:, col:col + w], vtok[0:NS, QT, src:src + w]).then_inc(v_out, 16)

        @block.sync
        def _(sp):
            for i in range(NT):
                sp.dma_start(xtok[0:token_rows(i), i, :], x_rows(i)).then_inc(x_in[i], 16)
                if i == 0:
                    sp.dma_start(ident, C["c_ident"]).then_inc(const_in, 16)

            def load_group(g):
                if g >= WSLOTS:
                    sp.wait_ge(filled, group_done[g - WSLOTS])
                c0, w = GROUPS[g]
                dst = wslot[g % WSLOTS][:, 0:KC * w].rearrange("p (k c) -> p k c", k=KC)
                src = A["w_in"][0, :, c0:c0 + w].rearrange("(k p) c -> p k c", p=P)
                if g < NSA_Q_GROUP:
                    sp.dma_start(dst, src).then_inc(w_in[g % WSLOTS], 16)
                    return
                for j in range(4):
                    for kv in range(2):
                        sp.dma_start(dst[:, :, P * j + DH * kv:P * j + DH * (kv + 1)],
                                     src[:, :, 256 * kv + DH * j:256 * kv + DH * (j + 1)]).then_inc(w_in[g % WSLOTS], 16)

            load_group(0)
            for dst, src in ((hot[0:33], C["c_hot"]), (rel[0:32], A["rel_bias"]), (rel[32:33], C["c_neg"]),
                             (state_tok[0:16], A["state_conv"][0].rearrange("n r c -> (n r) c")),
                             (pos_tok[0:64, 0:DH], A["cmp_pos"][0].rearrange("v l d -> (v l) d")),
                             (pos_tok[0:64, DH:P], A["cmp_pos"][0].rearrange("v l d -> (v l) d")),
                             (unseen, C["c_unseen"]), (ramp, C["c_ramp"]), (token, C["c_token"]),
                             (before, C["c_before"]), (state_tok[16:19], A["conv_w"][0])):
                sp.dma_start(dst, src).then_inc(early_in, 16)
            sp.dma_start(page_ids[0:1], A["page_table"].rearrange("n g -> (n g)").unsqueeze(0)).then_inc(page_ids_in, 16)
            load_group(1)
            load_group(2)
            sp.wait_ge(page_ids_in, 16)

            def load_page(s):
                if s >= 2:
                    sp.wait_ge(filled, at["page_T", s - 2] + 1)
                for g in range(2):
                    page = sp.value_load(page_ids[0:1, 2 * s + g:2 * s + g + 1], min_val=0,
                                         max_val=A["cache_nsa_kv"].shape[1] - 1)
                    src = kv_pool[bass.ds(page, 1), :, 0:256].rearrange("o p c -> (o p) c")
                    sp.dma_start(pages[s % 2][:, g, :], src).then_inc(page_in[s % 2], 16)

            for g in range(3, 7):
                load_group(g)
            load_page(0)
            load_page(1)
            load_group(7)
            for s in range(2, NSEQ):
                load_page(s)
            for g in range(8, len(GROUPS)):
                load_group(g)
            sp.wait_ge(filled, at["dil_k", 5] + 1)
            for g in range(2):
                sp.dma_start(w1[g * DH:(g + 1) * DH], A["cmp_w1"][0].rearrange("v (l d) h -> d v l h", d=DH)).then_inc(cmp_in, 16)
            sp.wait_ge(dve_emptied, p_owner[at["conv_b", 3]][1])
            sp.dma_start(w2, A["cmp_w2"][0].rearrange("v h d -> h v d")).then_inc(cmp_in, 16)

            sp.wait_ge(filled, at["hidden", (1, 1)] + 1)
            sp.wait_ge(bias_out, 16 * 4)

            sp.dma_start(tab_dil0, bias_ap(0, 383, (RLEN - 1, P), (P * RLEN, 4), (1, 256))).then_inc(tables_in, 16)
            for t in (1, 2):
                sp.dma_start(tab_dil[:, t - 1], bias_ap(4 * t, 127, (RLEN - 1, P), (P * RLEN, 4), (1, 512))).then_inc(tables_in, 16)
            sp.dma_start(tab_nsa, bias_ap(12, 127, (RLEN - 1, P), (P * RLEN, 8), (1, 512))).then_inc(tables_in, 16)

            def load_page_half(n, kv, dst, signal):
                for g in range(2):
                    page = sp.value_load(page_ids[0:1, 2 * n + g:2 * n + g + 1], min_val=0,
                                         max_val=A["cache_nsa_kv"].shape[1] - 1)
                    src = kv_pool[bass.ds(page, 1), :, 256 + P * kv:256 + P * (kv + 1)].rearrange("o p c -> (o p) c")
                    sp.dma_start(dst[:, 1280 + P * g:1280 + P * (g + 1)], src).then_inc(signal, 16)

            def load_keys(n):
                if n >= 3:
                    sp.wait_ge(turned, fill_at["keys", n - 3, 3] + 1)
                for t in range(4):
                    load_rows(sp, t, n, 0, k_cache[n % 3], k_in[n % 3])
                load_page_half(n, 0, k_cache[n % 3], k_in[n % 3])

            def load_nsa_values(n):
                load_rows(sp, 3, n, 1, v_cache[n % 4], nsa_v_in[n % 4])
                load_page_half(n, 1, v_cache[n % 4], nsa_v_in[n % 4])
                for c, src in ((0, SEL_V), (P, WIN_V)):
                    sp.dma_start(new_nsa_v[n % 4][0:TNEW, c:c + P], vtok[n * TNEW:(n + 1) * TNEW, QT, src:src + P])\
                      .then_inc(nsa_v_in[n % 4], 16)

            for i in range(3):
                sp.wait_ge(stage_out[i], 96)
            load_keys(0)
            load_keys(1)
            sp.wait_ge(scored, 3 * N_PROMPT)
            sp.wait_ge(turned, fill_at["probs", N_PROMPT - 3, len(key_tiles(UNITS[N_PROMPT - 3])) // 4] + 1)
            load_keys(2)
            load_keys(3)
            sp.wait_ge(score_read, 3 * N_PROMPT)
            sp.wait_ge(keys_kept, 1)
            for n in range(4):
                load_nsa_values(n)
            for n in range(4, NSEQ):
                load_keys(n)
            for n in range(4, NSEQ):
                if n % 2 == 0:
                    sp.wait_ge(summed, N_PROMPT + n // 2)
                load_nsa_values(n)

            def load_gates(cc):
                if cc >= 2:
                    sp.wait_ge(later_filled, lat["gate", (2 * cc - 3, 2)] + 1)
                for b in range(3):
                    c0 = MERGE0 + D * b + 256 * cc
                    sp.dma_start(gate_w[cc % 2][:, :, b, :], A["w_in"][0, :, c0:c0 + 256].rearrange("(k p) c -> p k c", p=P))\
                      .then_inc(gate_w_in[cc % 2], 16)

            sp.wait_ge(summed, len(UNITS))
            load_gates(0)
            for dst, name in ((w_conv, "w_branch_conv"), (w_dil, "w_branch_dil"), (w_nsa, "w_branch_nsa")):
                if name != "w_branch_nsa":
                    sp.dma_start(dst, A[name][0].rearrange("(k p) c -> p k c", p=P)).then_inc(merge_w_in, 16)
                    continue
                for g in range(2):
                    sp.dma_start(dst[g * DH:(g + 1) * DH], A[name][0, 256 * g:256 * g + 256, :]
                                 .rearrange("(j d) c -> d j c", d=DH)).then_inc(merge_w_in, 16)
            load_gates(1)
            sp.dma_start(w_out, A["w_out"][0].rearrange("(k p) c -> p k c", p=P)).then_inc(w_out_in, 16)
            load_gates(2)
            load_gates(3)

            sp.wait_ge(later_filled, lat["branch", (KC - 1, 2)] + 1)
            later_emptied(sp, "branch", (KC - 1, 2))
            for i in range(NT):
                sp.dma_start(res[0:token_rows(i), i, :], x_rows(i)).then_inc(res_in[i], 16)
                if i == 0:
                    for k, name in enumerate(("ln1_g", "ln1_b", "ln2_g", "ln2_b")):
                        sp.dma_start(ln[:, k, :], A[name].partition_broadcast(P).rearrange("p o c -> p (o c)")).then_inc(late_in, 16)
            sp.dma_start(router_b, A["router_b"].unsqueeze(0).partition_broadcast(P).rearrange("p o c -> p (o c)")).then_inc(late_in, 16)
            sp.dma_start(router_w, A["router_w"].rearrange("(k p) e -> p k e", p=P)).then_inc(ple_in, 16)
            sp.dma_start(p_tok[:, 0:QT, :], A["p_prompt"][0, 0].rearrange("(i p) c -> p i c", p=P)).then_inc(ple_in, 16)
            sp.dma_start(p_tok[0:NS, QT, :], A["p_sample"][0].rearrange("n t c -> (n t) c")).then_inc(ple_in, 16)
            sp.dma_start(ple_w, A["ple_w_gate"][0].rearrange("(k p) c -> p k c", p=P)).then_inc(ple_in, 16)
            sp.dma_start(ple_p, A["ple_w_proj"][0].rearrange("(k p) c -> p k c", p=P)).then_inc(ple_in, 16)

            names = ("expert_w_gate", "expert_w_up", "expert_w_down")

            def load_expert_weights(q, s, j):
                if not (isinstance(q, int) and q == 0):
                    sp.wait_ge((gated_done, up_done, down_done)[j], 2 * q + s - 1)
                src = A[names[j]][0][bass.ds(2 * q + s, 1)].rearrange("o (k p) c -> p (o k) c", p=P)
                dst = ew[s][j].rearrange("p (k c) -> p k c", k=src.shape[1])
                sp.dma_start(dst, src).then_inc(ew_in[j][s], 16)

            sp.wait_ge(later_filled, lat["mix", NT - 1] + 1)
            for j in range(3):
                load_expert_weights(0, 0, j)
            sp.wait_ge(later_filled, len(later))
            sp.wait_ge(dve_later, l_dve)
            sp.wait_ge(indices_ready, 1)
            for j in range(3):
                load_expert_weights(0, 1, j)
            load_expert_weights(1, 0, 0)
            load_expert_weights(1, 0, 1)
            load_expert_weights(1, 1, 0)
            load_expert_weights(1, 1, 1)
            load_expert_weights(1, 0, 2)
            with sp.Fori(2, N_EXP // 2) as q:
                load_expert_weights(q, 0, 0)
                load_expert_weights(q, 0, 1)
                load_expert_weights(q - 1, 1, 2)
                load_expert_weights(q, 1, 0)
                load_expert_weights(q, 1, 1)
                load_expert_weights(q, 0, 2)
            load_expert_weights(N_EXP // 2 - 1, 1, 2)

            most = sp.value_load(count_i[0:1, :], min_val=0, max_val=TOK)
            with sp.If(most > P):
                sp.wait_ge(down_done, N_EXP)
                with sp.Fori(1, N_BLOCK - N_EXP + 1) as b:
                    sp.wait_ge(over["down"], b)
                    for j, name in enumerate(names):
                        src = A[name][0][bass.ds((b + N_EXP - 1) % N_EXP, 1)].rearrange("o (k p) c -> p (o k) c", p=P)
                        sp.dma_start(ew[0][j].rearrange("p (k c) -> p k c", k=src.shape[1]), src).then_inc(over["w"], 16)

            for i in range(NT):
                sp.wait_ge(combined, i + 1)
                dst = O["y_prompt"][0, i * P:(i + 1) * P, :] if i < QT else O["y_sample"].rearrange("n t d -> (n t) d")
                sp.dma_start(dst, res[0:token_rows(i), i, :]).then_inc(y_out, 16)
            sp.wait_ge(y_out, 16 * NT)


        @block.tensor
        def _(pe):
            def feature_major(n, lhs, chunks, rhs):
                for b in range(2):
                    for k in range(chunks):
                        mm = nc.tensor.matmul(bank(n, b)[:, 0:HALF], lhs(k), rhs[:, k, b * HALF:(b + 1) * HALF],
                                              start=(k == 0), stop=(k == chunks - 1))
                return mm

            pe.wait_ge(const_in, 16)
            for n, (kind, a) in enumerate(proj):
                if n >= 4:
                    wait_emptied(pe, p_owner, n - 4, act_emptied, dve_emptied)
                if kind in FEATURE or kind == "rows":
                    g = group_of(kind, a)[0]
                    pe.wait_ge(w_in[g % WSLOTS], 16 * (g // WSLOTS + 1 + 7 * (g == NSA_Q_GROUP)))
                if kind == "x_T":
                    i, h = a
                    pe.wait_ge(x_in[i], 16)
                    m = token_rows(i)
                    for k in range(4):
                        mm = nc.tensor.transpose(bank(n, 0)[:, k * m:(k + 1) * m],
                                                 xtok[0:m, i, (4 * h + k) * P:(4 * h + k + 1) * P], ident[0:m, 0:m])
                elif kind == "bias_row":
                    pe.wait_ge(early_in, 16 * 11)
                    for h in range(2):
                        mm = nc.tensor.matmul(bank(n, h)[0:20, 0:320], rel[0:33], hot[0:33, a, 320 * h:320 * h + 320],
                                              start=True, stop=True)
                elif kind == "state_T":
                    for c in range(4):
                        mm = nc.tensor.transpose(bank(n, 0)[:, 19 * c:19 * c + 19], state_tok[0:19, c * P:(c + 1) * P],
                                                 ident[0:19, 0:19])
                elif kind == "pos_T":
                    mm = nc.tensor.transpose(bank(n, 0)[:, 0:64], pos_tok[0:64], ident[0:64, 0:64])
                elif kind in FEATURE:
                    if n == at["conv_c", 0]:
                        for h in range(2):
                            proj_emptied(pe, "x_T", (NT - 1, h))
                    mm = feature_major(n, weights_of(kind, a), KC, xT)
                elif kind == "rows":
                    c, i = a
                    w = GROUPS[4 + c][1]
                    m = token_rows(i)
                    slot = wslot[(4 + c) % WSLOTS][:, 0:KC * w].rearrange("p (k c) -> p k c", k=KC)
                    for k in range(KC):
                        mm = nc.tensor.matmul(bank(n, 0)[0:m, 0:w], xT[:, k, i * P:i * P + m], slot[:, k, :],
                                              start=(k == 0), stop=(k == KC - 1))
                elif kind == "u_T":
                    pe.wait_ge(u_ready, 1)
                    for c in range(4):
                        mm = nc.tensor.transpose(bank(n, 0)[0:18, c * P:(c + 1) * P], u_last[:, c, :], ident)
                elif kind == "win_k_T":
                    for i in range(NT):
                        proj_emptied(pe, "rows", (0, i))
                    for i in range(NT):
                        m = token_rows(i)
                        dst = bank(n, 0)[:, i * P:(i + 1) * P] if i < QT else bank(n, 1)[:, 0:m]
                        mm = nc.tensor.transpose(dst, vtok[0:m, i, WIN_K:WIN_K + P], ident[0:m, 0:m])
                elif kind == "page_T":
                    pe.wait_ge(page_in[a % 2], 32 * (a // 2 + 1))
                    for kv in range(2):
                        for g in range(2):
                            mm = nc.tensor.transpose(bank(n, 0)[:, (2 * kv + g) * P:(2 * kv + g + 1) * P],
                                                     pages[a % 2][:, g, kv * P:(kv + 1) * P], ident)
                elif kind == "k_rows":
                    proj_emptied(pe, *(("dil_k", a) if a < 6 else ("cmp", (2, 0, 1)[a - 6])))
                    for i in range(NT):
                        src = kT[:, a] if a < 7 else rowsT[:, a - 7]
                        col = i * P if a < 7 or i < QT else NEW0
                        m = token_rows(i)
                        dst = bank(n, 0)[:, i * P:(i + 1) * P] if i < QT else bank(n, 1)[0:m, 0:P]
                        mm = nc.tensor.transpose(dst, src[:, col:col + m], ident)
                elif kind == "hidden":
                    kv, g = a
                    if a == (0, 0):
                        pe.wait_ge(cmp_in, 16 * 3)
                        proj_emptied(pe, "cmp", 1)
                        proj_emptied(pe, "page_T", NSEQ - 1)
                    half = slice(g * DH, (g + 1) * DH)
                    for l in range(CMP_BLOCK):
                        mm = nc.tensor.matmul(bank(n, 0)[:, 0:NCMP + 1], w1[half, kv, l, :],
                                              rowsT[half, kv, l:l + CMP_STRIDE * NCMP + 1:CMP_STRIDE],
                                              start=(l == 0), stop=(l == CMP_BLOCK - 1))
                elif kind == "cmp_k_T":
                    for g in range(2):
                        proj_emptied(pe, "hidden", (0, g))
                        mm = nc.tensor.matmul(bank(n, 0)[g * DH:(g + 1) * DH, 0:NCMP - 1], w2[:, 0, :],
                                              hidden[:, g, 0:NCMP - 1], start=True, stop=True)
                elif kind == "cmp_v":
                    for g in range(2):
                        proj_emptied(pe, "hidden", (1, g))
                        h = hidden[:, 2 + g]
                        if a == 0:
                            mm = nc.tensor.matmul(bank(n, 0)[0:PROMPT_CMP, g * DH:(g + 1) * DH], h[:, 0:PROMPT_CMP],
                                                  w2[:, 1, :], start=True, stop=True)
                            continue
                        for s in range(NSEQ):
                            c0 = (SEQ + PAST * s) // CMP_STRIDE
                            mm = nc.tensor.matmul(bank(n, s // 4)[0:SAMPLE_CMP, s % 4 * P + g * DH:s % 4 * P + (g + 1) * DH],
                                                  h[:, c0:c0 + SAMPLE_CMP], w2[:, 1, :], start=True, stop=True)
                mm.then_inc(filled, 1)

            proj_all_emptied(pe)

            def scores(u):
                kind, h, qt = UNITS[u]
                widths = segments(UNITS[u])
                if kind == "sdil":
                    half = h
                    for n in range(4 * half, 4 * half + 4):
                        fill_emptied(pe, "keys", n, 3)
                    pe.wait_ge(new_keys_put, 4 * (half + 1))
                if u < N_PROMPT:
                    pe.wait_ge(q_put, u + 1)
                for s, w in enumerate(widths):
                    seg = 3 * u + s
                    if seg >= 4:
                        pe.wait_ge(score_read, seg - 3)
                    dst = ps[:, seg % 4, :]
                    if kind == "dil":
                        end = (qt + 1) * P
                        mm = nc.tensor.matmul(dst[:, 0:w], q_pad[h % 2][:, s, :], kT[:, 2 * s + h // 2, end - w:end],
                                              start=True, stop=True)
                    elif kind == "nsa":
                        g, j = h
                        keys = kcT[:, 0:w] if s == 0 else kT[:, 5 + s, 0:w]
                        mm = nc.tensor.matmul(dst[:, 0:w], q_pad[g][:, 0, :], keys, start=True, stop=True)
                    elif kind == "sdil":
                        o = 272 + 528 * (s - 1) if s else 0
                        for pr in range(2):
                            for n in range(4):
                                mm = nc.tensor.matmul(dst[32 * n:32 * n + 32, 0:w], q_dil[:, 2 * s + pr, 4 * half + n, :],
                                                      cacheT[n][:, o + pr * w:o + (pr + 1) * w],
                                                      start=(pr == 0), stop=(pr == 1))
                    else:
                        for n2 in range(2):
                            n = 2 * h + n2
                            c0 = (SEQ + PAST * n) // CMP_STRIDE
                            o = 1328 + 264 * (s - 1)
                            keys = kcT[:, c0:c0 + w] if s == 0 else cacheT[n % 4][:, o:o + w]
                            mm = nc.tensor.matmul(dst[64 * n2:64 * n2 + 64, 0:w], q_nsa[:, n, :], keys,
                                                  start=True, stop=True)
                    mm.then_inc(scored, 1)

            def turn(u):
                pe.wait_ge(scaled, u + 1)
                tiles = key_tiles(UNITS[u])
                for f in range((len(tiles) + 3) // 4):
                    n = fill_at["probs", u, f]
                    if n >= 2:
                        wait_emptied(pe, f_owner, n - 2, act_turned, dve_turned)
                    for x, (s, a, w) in enumerate(tiles[4 * f:4 * f + 4]):
                        mm = nc.tensor.transpose(turn_bank(n)[0:w, x * P:(x + 1) * P],
                                                 probs_of(u, s, a, w), ident)
                    mm.then_inc(turned, 1)

            def turn_keys(n):
                pe.wait_ge(k_in[n % 3], 96 * (n // 3 + 1))
                keys = k_cache[n % 3]
                for f in range(4):
                    m = fill_at["keys", n, f]
                    wait_emptied(pe, f_owner, m - 2, act_turned, dve_turned)
                    if f == 0:
                        cols = [P * pr for pr in range(2)]
                    elif f < 3:
                        cols = [512 * f - 256 + 256 * a + P * pr for pr in range(2) for a in range(2)]
                    else:
                        cols = [1280 + P * x for x in range(4)]
                    for x, c in enumerate(cols):
                        mm = nc.tensor.transpose(turn_bank(m)[:, x * P:(x + 1) * P], keys[:, c:c + P], ident)
                    mm.then_inc(turned, 1)

            def sums(u):
                kind, h, qt = UNITS[u]
                tiles = key_tiles(UNITS[u])
                fill_emptied(pe, "probs", u, (len(tiles) - 1) // 4)
                if u >= 2:
                    pe.wait_ge(out_read, u - 1)
                dst = ps[:, 6 + u % 2, :]
                pT_u = probsT[u % 2]
                first, final = 0, len(tiles) - 1
                if kind in ("dil", "nsa"):
                    r0 = h % 2 * DH if kind == "dil" else h[0] * DH
                    start = (qt + 1) * P - segments(UNITS[u])[0]
                    for x, (s, a, w) in enumerate(tiles):
                        if kind == "dil":
                            key = a + (start if s == 0 else 0)
                            vals = vtok[:, key // P, s * 256 + h * DH:s * 256 + h * DH + DH]
                        elif s == 0:
                            vals = vcp[0:w, h[0] * DH:h[0] * DH + DH]
                        else:
                            c = (SEL_V, WIN_V)[s - 1] + h[0] * DH
                            vals = vtok[:, a // P, c:c + DH]
                        mm = nc.tensor.matmul(dst[r0:r0 + DH, 0:P], vals, pT_u[0:w, x, :],
                                              start=(x == first), stop=(x == final))
                elif kind == "sdil":
                    for n in range(4):
                        pe.wait_ge(dil_v_in[n], 64 * (h + 1))
                    for x, (s, a, w) in enumerate(tiles):
                        for n in range(4):
                            if w == TNEW:
                                vals = new_dil_v[n][0:w, s * 256:(s + 1) * 256]
                            else:
                                o = (0, 256, 768)[s] + 2 * a
                                vals = v_cache[n][:, o:o + 256]
                            mm = nc.tensor.matmul(dst[32 * n:32 * n + 32, 0:256], pT_u[0:w, x, 32 * n:32 * n + 32], vals,
                                                  start=(x == first), stop=(x == final))
                else:
                    for n2 in range(2):
                        n = 2 * h + n2
                        pe.wait_ge(nsa_v_in[n % 4], 80 * (n // 4 + 1))
                        for x, (s, a, w) in enumerate(tiles):
                            if s == 0:
                                vals = vcs[0:w, n, :]
                            elif w == TNEW:
                                vals = new_nsa_v[n % 4][0:w, P * (s - 1):P * s]
                            else:
                                o = 1280 + 256 * (s - 1) + a
                                vals = v_cache[n % 4][:, o:o + P]
                            mm = nc.tensor.matmul(dst[:, 64 * n2:64 * n2 + 64], vals,
                                                  pT_u[0:w, x, 64 * n2:64 * n2 + 64], start=(x == first), stop=(x == final))
                mm.then_inc(summed, 1)

            def turn_sums(u):
                m = fill_at["sums", u, 0]
                wait_emptied(pe, f_owner, m - 2, act_turned, dve_turned)
                pe.wait_ge(out_read, u + 1)
                for pr in range(2):
                    mm = nc.tensor.transpose(turn_bank(m)[:, pr * P:(pr + 1) * P], sum_rows[:, pr * P:(pr + 1) * P], ident)
                mm.then_inc(turned, 1)

            for u in range(len(UNITS) + 3):
                if u == N_PROMPT:
                    pe.wait_ge(queries_built, 1)
                if u < len(UNITS) and not begins_half(u):
                    scores(u)
                if 2 <= u < len(UNITS) + 2:
                    turn(u - 2)
                if u >= 3:
                    sums(u - 3)
                if begins_half(u):
                    for n in range(4 * UNITS[u][1], 4 * UNITS[u][1] + 4):
                        turn_keys(n)
                    scores(u)
                if u >= 4 and UNITS[u - 4][0] == "sdil":
                    turn_sums(u - 4)

            pe.wait_ge(out_read, len(UNITS))
            pe.wait_ge(dve_turned, f_dve)
            for n, (kind, a) in enumerate(later):
                if n >= 4:
                    wait_emptied(pe, l_owner, n - 4, act_later, dve_later)
                if kind == "gate":
                    c, b = a
                    pe.wait_ge(gate_w_in[c // 2 % 2], 48 * (c // 4 + 1))
                    w = gate_w[c // 2 % 2]
                    mm = feature_major(n, lambda k: w[:, k, b, c % 2 * P:(c % 2 + 1) * P], KC, xT)
                elif kind == "branch":
                    c, b = a
                    pe.wait_ge(merge_w_in, 64)
                    w, y = ((w_conv, yconvT), (w_dil, ydilT), (w_nsa, ynsaT))[b]
                    mm = feature_major(n, lambda k: w[:, k, c * P:(c + 1) * P], (4, 2, 4)[b], y)
                elif kind == "mix":
                    pe.wait_ge(w_out_in, 16)
                    if a == 0:
                        later_emptied(pe, "branch", (KC - 1, 2))
                    m = token_rows(a)
                    for h in range(2):
                        for k in range(KC):
                            mm = nc.tensor.matmul(bank(n, h)[0:m, :], mT[:, k, a * P:a * P + m],
                                                  w_out[:, k, 512 * h:512 * h + 512], start=(k == 0), stop=(k == KC - 1))
                elif kind == "x1_T":
                    i, h = a
                    pe.wait_ge(x1_ready, i + 1)
                    m = token_rows(i)
                    for k in range(4):
                        mm = nc.tensor.transpose(bank(n, 0)[:, k * m:(k + 1) * m],
                                                 res[0:m, i, (4 * h + k) * P:(4 * h + k + 1) * P], ident[0:m, 0:m])
                elif kind == "router":
                    for h in range(2):
                        later_emptied(pe, "x1_T", (NT - 1, h))
                    pe.wait_ge(ple_in, 80)
                    for i in range(NT):
                        m = token_rows(i)
                        for k in range(KC):
                            mm = nc.tensor.matmul(bank(n, 0)[0:m, 16 * i:16 * i + 16], x1T[:, k, i * P:i * P + m],
                                                  router_w[:, k, :], start=(k == 0), stop=(k == KC - 1))
                elif kind == "p_T":
                    m = token_rows(a)
                    for k in range(2):
                        mm = nc.tensor.transpose(bank(n, 0)[:, k * m:(k + 1) * m], p_tok[0:m, a, k * P:(k + 1) * P],
                                                 ident[0:m, 0:m])
                elif kind in ("ple_gate", "ple_proj"):
                    gate = kind == "ple_gate"
                    if not gate and a == 0:
                        later_emptied(pe, "p_T", NT - 1)
                    m = token_rows(a)
                    lhs, w, chunks = (x1T, ple_w, KC) if gate else (pT, ple_p, 2)
                    for h in range(2):
                        for k in range(chunks):
                            mm = nc.tensor.matmul(bank(n, h)[0:m, :], lhs[:, k, a * P:a * P + m],
                                                  w[:, k, 512 * h:512 * h + 512], start=(k == 0), stop=(k == chunks - 1))
                elif kind == "rank":
                    pe.wait_ge(chosen, 1)
                    for i in range(NT):
                        for x in range(i + 1):
                            mm = nc.tensor.matmul(bank(n, 0)[:, 16 * i:16 * i + 16], before if x == i else ones,
                                                  routing(5)[:, x, :], start=(x == 0), stop=(x == i))
                    for i in range(NT):
                        mm = nc.tensor.matmul(bank(n, 1)[:, 0:16], ones, routing(5)[:, i, :], start=(i == 0), stop=(i == NT - 1))
                mm.then_inc(later_filled, 1)

            pe.wait_ge(act_later, l_act)
            pe.wait_ge(dve_later, l_dve)

            def turn_x(s):
                for k in range(KC):
                    mm = nc.tensor.transpose(ps[:, k // 4, k % 4 * P:(k % 4 + 1) * P], xg[s][:, k * P:(k + 1) * P], ident)
                return mm

            def up_product(s, j):
                w = ew[s][j].rearrange("p (k c) -> p k c", k=KC)
                for k in range(KC):
                    mm = nc.tensor.matmul(ps[:, 2 + j, :], xgT[s][:, k, :], w[:, k, :], start=(k == 0), stop=(k == KC - 1))
                return mm

            def turn_h():
                for k in range(4):
                    mm = nc.tensor.transpose(ps[:, 4, k * P:(k + 1) * P], h_tok[:, k * P:(k + 1) * P], ident)
                return mm

            def down_product(s):
                w = ew[s][2].rearrange("p (k c) -> p k c", k=4)
                for h in range(2):
                    for k in range(4):
                        mm = nc.tensor.matmul(ps[:, 5 + h, :], hT[:, k, :], w[:, k, 512 * h:512 * h + 512],
                                              start=(k == 0), stop=(k == 3))
                return mm

            def finish_expert(q, s):
                e = 2 * q + s
                first = isinstance(q, int) and q == 0 and s == 0
                pe.wait_ge(hT_ready, e + 1)
                pe.wait_ge(ew_in[2][s], 16 * q + 16)
                if not first:
                    pe.wait_ge(act_y, e)
                    pe.wait_ge(dve_y, e)
                down_product(s).then_inc(down_done, 1)

            def turn_hidden(q, s):
                e = 2 * q + s
                pe.wait_ge(h_ready, e + 1)
                if not (isinstance(q, int) and q == 0 and s == 0):
                    pe.wait_ge(hT_ready, e)
                turn_h().then_inc(h_turned, 1)

            def expert_step(q, s, last=False):
                e = 2 * q + s
                first = isinstance(q, int) and q == 0 and s == 0
                pq, p_s = (q, 0) if s else (q - 1, 1)
                pe.wait_ge(ew_in[0][s], 16 * q + 16)
                pe.wait_ge(act_x, e + 1)
                pe.wait_ge(dve_x, e + 1)
                if not first:
                    pe.wait_ge(silu_done, e)
                up_product(s, 0).then_inc(gated_done, 1)
                if not first:
                    turn_hidden(pq, p_s)
                pe.wait_ge(ew_in[1][s], 16 * q + 16)
                up_product(s, 1).then_inc(up_done, 1)
                if not last:
                    nq = q + s
                    pe.wait_ge(xg_in[1 - s], 16 * nq + 16)
                    turn_x(1 - s).then_inc(x_turned, 1)
                if not first:
                    finish_expert(pq, p_s)

            pe.wait_ge(xg_in[0], 16)
            turn_x(0).then_inc(x_turned, 1)
            expert_step(0, 0)
            expert_step(0, 1)
            with pe.Fori(1, N_EXP // 2 - 1) as q:
                expert_step(q, 0)
                expert_step(q, 1)
            expert_step(N_EXP // 2 - 1, 0)
            expert_step(N_EXP // 2 - 1, 1, last=True)
            turn_hidden(N_EXP // 2 - 1, 1)
            finish_expert(N_EXP // 2 - 1, 1)

            most = pe.value_load(count_i[0:1, :], min_val=0, max_val=TOK)
            with pe.If(most > P):
                pe.wait_ge(act_y, N_EXP)
                pe.wait_ge(dve_y, N_EXP)
                pe.nop().then_inc(over["down"], 1)
                with pe.Fori(1, N_BLOCK - N_EXP + 1) as b:
                    pe.wait_ge(over["x"], 16 * b)
                    turn_x(0).then_inc(over["x_turned"], 1)
                    pe.wait_ge(over["act_x"], b)
                    pe.wait_ge(over["dve_x"], b)
                    pe.wait_ge(over["w"], 48 * b)
                    up_product(0, 0).then_inc(over["gated"], 1)
                    up_product(0, 1).then_inc(over["up"], 1)
                    pe.wait_ge(over["h"], b)
                    turn_h().then_inc(over["h_turned"], 1)
                    pe.wait_ge(over["hT"], b)
                    down_product(0).then_inc(over["down"], 1)


        @block.scalar
        def _(act):
            link = chained(act, act_chain)
            for n, (kind, a) in enumerate(proj):
                if not p_owner[n][0]:
                    continue
                act.wait_ge(filled, n + 1)
                if kind == "x_T":
                    i, h = a
                    m = token_rows(i)
                    src = bank(n, 0)[:, 0:4 * m].rearrange("p (k t) -> p k t", k=4)
                    last = nc.scalar.copy(xT[:, 4 * h:4 * h + 4, i * P:i * P + m], src)
                elif kind == "conv_c":
                    last = nc.scalar.copy(halves(conv_tmp[:, a]), pair(n)[:, :, 0:HALF])
                elif kind == "u_T":
                    last = nc.scalar.copy(u_rows[0:18], bank(n, 0)[0:18, :])
                elif kind == "cmp":
                    if a == 0:
                        act.wait_ge(filled, at["x_T", (NT - 1, 1)] + 1)
                    nc.scalar.copy(rowsT[:, a, 0:HALF], bank(n, 0)[:, 0:HALF])
                    nc.scalar.copy(rowsT[:, a, HALF:SEQ], bank(n, 1)[:, 0:SEQ - HALF])
                    last = nc.scalar.copy(rowsT[:, a, NEW0:NEW0 + NS], bank(n, 1)[:, SEQ - HALF:HALF])
                elif kind == "rows":
                    if a == (0, 1):
                        act.wait_ge(bias_out, 16 * 4)
                    last = copy_rows(act, n, a)
                elif kind in ("dil_q", "nsa_q"):
                    c = a + (6 if kind == "nsa_q" else 0)
                    last = nc.scalar.mul(halves(qT[:, c]), pair(n)[:, :, 0:HALF], SCALE)
                elif kind == "dil_k":
                    last = nc.scalar.copy(halves(kT[:, a]), pair(n)[:, :, 0:HALF])
                elif kind == "hidden":
                    kv, g = a
                    if a == (0, 0):
                        act.wait_ge(dve_emptied, p_owner[at["conv_b", 3]][1])
                    b = gelu_b[:, 2 * kv + g:2 * kv + g + 1]
                    link(nc.scalar.copy(b, bank(n, 0)[:, NCMP:NCMP + 1]))
                    last = nc.scalar.activation(hidden[:, 2 * kv + g, 0:NCMP - 1], bank(n, 0)[:, 0:NCMP - 1],
                                                ACT.Gelu_apprx_tanh, bias=b)
                last.then_inc(act_emptied, 1)

            proj_all_emptied(act)
            nc.scalar.activation(nsa_gate[:, 0:QT, :], vtok[:, 0:QT, GATES:VW], ACT.Sigmoid)
            nc.scalar.activation(nsa_gate[0:NS, QT, :].rearrange("p (h b) -> p b h", b=3),
                                 vtok[0:NS, QT, GATES:VW].rearrange("p (b h) -> p b h", b=3),
                                 ACT.Sigmoid).then_inc(gates_ready, 1)

            def build_queries():
                act.wait_ge(queries_zeroed, 1)
                for t in range(3):
                    for pr in range(2):
                        for x in range(2):
                            rows = slice(x * DH, x * DH + DH)
                            dst = q_dil[rows, 2 * t + pr].rearrange("p n (h t) -> p n h t", h=4)[:, :, 2 * pr + x, :]
                            nc.scalar.copy(dst, qT[rows, 2 * t + pr, SEQ:TOK].rearrange("p (n t) -> p n t", n=NSEQ))
                for g in range(2):
                    rows = slice(g * DH, g * DH + DH)
                    dst = q_nsa[rows].rearrange("p n (g j t) -> p g j n t", g=2, j=4)[:, g]
                    for j in range(4):
                        last = nc.scalar.copy(dst[:, j], qT[rows, 6 + j, SEQ:TOK].rearrange("p (n t) -> p n t", n=NSEQ))
                last.then_inc(queries_built, 1)

            def put_queries(u):
                kind, h, qt = UNITS[u]
                r = h % 2 if kind == "dil" else h[0]
                rows = slice(r * DH, r * DH + DH)
                cols = slice(qt * P, qt * P + P)
                if kind == "dil":
                    last = nc.scalar.copy(q_pad[r][rows], qT[rows, h // 2:6:2, cols])
                else:
                    last = nc.scalar.copy(q_pad[r][rows, 0, :], qT[rows, 6 + h[1], cols])
                last.then_inc(q_put, 1)

            def load_sample_tables():
                for n in range(4):
                    act.dma_start(tab_sdil[32 * n:32 * n + 32, 0:136], bias_ap(0, 383, (P * RLEN, 4), (RLEN - 1, TNEW), (1, 136)))\
                       .then_inc(sample_tables_in, 16)
                    for t in (1, 2):
                        act.dma_start(tab_sdil[32 * n:32 * n + 32, 136 + 264 * (t - 1):136 + 264 * t],
                                      bias_ap(4 * t, 255, (P * RLEN, 4), (RLEN - 1, TNEW), (1, 264))).then_inc(sample_tables_in, 16)
                for n in range(2):
                    act.dma_start(tab_snsa[64 * n:64 * n + 64], bias_ap(12, 255, (P * RLEN, 8), (RLEN - 1, TNEW), (1, 264)))\
                       .then_inc(sample_tables_in, 16)

            act.wait_ge(q_pad_zeroed, 1)
            put_queries(0)
            put_queries(1)

            def exponentials(u):
                act.wait_ge(max_ready, u + 1)
                joint = UNITS[u][0] in ("dil", "sdil")
                _, neg_max, total, _ = stat[u % 2]
                for s, w in enumerate(segments(UNITS[u])):
                    seg = probs_of(u, s, 0, w)
                    b = neg_max[:, 0:1] if joint else neg_max[:, s:s + 1]
                    last = nc.scalar.activation(seg, seg, ACT.Exp, bias=b, accum_out=total[:, s:s + 1])
                last.then_inc(exp_ready, 1)

            def take_turned(u):
                tiles = key_tiles(UNITS[u])
                for f in range((len(tiles) + 3) // 4):
                    n = fill_at["probs", u, f]
                    act.wait_ge(turned, n + 1)
                    if u >= 2:
                        act.wait_ge(summed, u - 1)
                    part = tiles[4 * f:4 * f + 4]
                    x = 0
                    while x < len(part):
                        y = x
                        while y < len(part) and part[y][2] == part[x][2]:
                            y += 1
                        w = part[x][2]
                        last = nc.scalar.copy(probsT[u % 2][0:w, 4 * f + x:4 * f + y, :],
                                              turn_bank(n)[0:w, x * P:y * P].rearrange("p (a q) -> p a q", q=P))
                        x = y
                    last.then_inc(act_turned, 1)

            for u in range(len(UNITS) + 2):
                if u == 2:
                    build_queries()
                if begins_half(u):
                    take_turned(u - 2)
                if u < len(UNITS):
                    exponentials(u)
                if u + 2 < N_PROMPT:
                    put_queries(u + 2)
                if u >= 2 and not begins_half(u):
                    take_turned(u - 2)
                if u == N_PROMPT - 1:
                    act.wait_ge(score_read, 3 * N_PROMPT)
                    load_sample_tables()

            def root(i):
                act.wait_ge(var_ready, i + 1)
                m = token_rows(i % NT)
                nc.scalar.activation(lnsd[0:m, 1:2], lnsd[0:m, 0:1], ACT.Sqrt).then_inc(sqrt_ready, 1)

            for n, (kind, a) in enumerate(later):
                if kind == "mix":
                    root(a)
                    continue
                if not l_owner[n][0]:
                    continue
                act.wait_ge(later_filled, n + 1)
                if kind == "gate":
                    c, b = a
                    x = 3 * c + b
                    if x == 0:
                        act.wait_ge(scored, 3 * len(UNITS))
                    if x >= 2:
                        act.wait_ge(dve_later, l_owner[lat["branch", ((x - 2) // 3, (x - 2) % 3)]][1])
                    last = nc.scalar.activation(halves(sig[x % 2]), pair(n)[:, :, 0:HALF], ACT.Sigmoid)
                elif kind == "x1_T":
                    i, h = a
                    m = token_rows(i)
                    src = bank(n, 0)[:, 0:4 * m].rearrange("p (k t) -> p k t", k=4)
                    last = nc.scalar.copy(x1T[:, 4 * h:4 * h + 4, i * P:i * P + m], src)
                elif kind == "router":
                    act.wait_ge(route_zeroed, 1)
                    src = bank(n, 0)[:, 0:16 * NT].rearrange("p (i e) -> p i e", e=16)
                    nc.scalar.activation(routing(0)[:, 0:QT, :], src[:, 0:QT, :], ACT.Sigmoid)
                    last = nc.scalar.activation(routing(0)[0:NS, QT, :], src[0:NS, QT, :], ACT.Sigmoid)
                elif kind == "ple_gate":
                    if a >= 2:
                        act.wait_ge(dve_later, l_owner[lat["ple_proj", a - 2]][1])
                    m = token_rows(a)
                    last = nc.scalar.activation(ple_sig[a % 2][0:m].rearrange("p (h c) -> p h c", h=2), pair(n)[0:m],
                                                ACT.Sigmoid)
                last.then_inc(act_later, 1)

            def take_x(s):
                return nc.scalar.copy(xgT[s][:, 0:4, :], ps[:, 0, :].rearrange("p (k t) -> p k t", k=4))

            def take_y(s):
                return nc.scalar.copy(y_exp[s][:, 0:512], ps[:, 5, :])

            def expert_step(q, s, last=False):
                e = 2 * q + s
                first = isinstance(q, int) and q == 0 and s == 0
                act.wait_ge(gated_done, e + 1)
                if not first:
                    act.wait_ge(h_ready, e)
                nc.scalar.activation(silu, ps[:, 2, :], ACT.Silu).then_inc(silu_done, 1)
                if not last:
                    act.wait_ge(x_turned, e + 2)
                    if not first:
                        act.wait_ge(up_done, e)
                    take_x(1 - s).then_inc(act_x, 1)
                if not first:
                    finish_expert(*((q, 0) if s else (q - 1, 1)))

            def finish_expert(q, s):
                act.wait_ge(down_done, 2 * q + s + 1)
                if not (isinstance(q, int) and q == 0):
                    act.wait_ge(y_stored[s], 16 * q)
                take_y(s).then_inc(act_y, 1)

            act.wait_ge(x_turned, 1)
            take_x(0).then_inc(act_x, 1)
            expert_step(0, 0)
            expert_step(0, 1)
            with act.Fori(1, N_EXP // 2 - 1) as q:
                expert_step(q, 0)
                expert_step(q, 1)
            expert_step(N_EXP // 2 - 1, 0)
            expert_step(N_EXP // 2 - 1, 1, last=True)
            finish_expert(N_EXP // 2 - 1, 1)

            most = act.value_load(count_i[0:1, :], min_val=0, max_val=TOK)
            with act.If(most > P):
                with act.Fori(1, N_BLOCK - N_EXP + 1) as b:
                    act.wait_ge(over["x_turned"], b)
                    take_x(0).then_inc(over["act_x"], 1)
                    act.wait_ge(over["gated"], b)
                    nc.scalar.activation(silu, ps[:, 2, :], ACT.Silu).then_inc(over["silu"], 1)
                    act.wait_ge(over["down"], b + 1)
                    take_y(0).then_inc(over["act_y"], 1)

            for i in range(NT):
                root(NT + i)


        @block.vector
        def _(dve):
            link = chained(dve, dve_chain)
            v = nc.vector
            for c in range(4):
                ins = v.memset(uext_flat[:, c, 0:2], 0.0)
            ins.then_inc(zeroed, 1)
            dve.wait_ge(zeroed, 1)
            link(v.memset(ones, 1.0))
            for n, (kind, a) in enumerate(proj):
                if p_owner[n][0]:
                    continue
                dve.wait_ge(filled, n + 1)
                if kind == "x_T":
                    i, h = a
                    m = token_rows(i)
                    src = bank(n, 0)[:, 0:4 * m].rearrange("p (k t) -> p k t", k=4)
                    last = v.tensor_copy(xT[:, 4 * h:4 * h + 4, i * P:i * P + m], src)
                elif kind == "bias_row":
                    last = v.tensor_copy(bias_rows[0:20, a, :].rearrange("p (h c) -> p h c", h=2), pair(n)[0:20, :, 0:320])
                elif kind == "state_T":
                    src = bank(n, 0)[:, 0:76].rearrange("p (c r) -> p c r", c=4)
                    for c in range(4):
                        v.tensor_copy(sample_u[c][:, :, 0:2], src[:, c, 0:16].rearrange("p (s r) -> p s r", s=NSEQ))
                    last = v.tensor_copy(conv_w, src[:, :, 16:19])
                elif kind == "conv_h":
                    if a == 0:
                        dve.wait_ge(filled, at["x_T", (NT - 1, 1)] + 1)
                    dve.wait_ge(act_emptied, p_owner[at["conv_c", a]][1])
                    v.tensor_tensor(uext_flat[:, a, 2:2 + HALF], bank(n, 0)[:, 0:HALF], conv_tmp[:, a, 0:HALF], ALU.mult)
                    v.tensor_tensor(uext_flat[:, a, 2 + HALF:2 + SEQ], bank(n, 1)[:, 0:SEQ - HALF],
                                    conv_tmp[:, a, HALF:SEQ], ALU.mult)
                    link(v.tensor_tensor(sample_u[a][:, :, 2:10],
                                         bank(n, 1)[:, SEQ - HALF:HALF].rearrange("p (s t) -> p s t", s=NSEQ),
                                         conv_tmp[:, a, SEQ:TOK].rearrange("p (s t) -> p s t", s=NSEQ), ALU.mult))
                    v.tensor_copy(u_last[:, a, 0:2], uext_flat[:, a, SEQ:SEQ + 2])
                    link(v.tensor_copy(u_last[:, a, 2:18].rearrange("p (s r) -> p s r", s=NSEQ), sample_u[a][:, :, 8:10]))
                    if a == 3:
                        dve.engine_nop().then_inc(u_ready, 1)
                    y_p = conv_tmp[:, a, 0:SEQ]
                    y_s = conv_tmp[:, a, SEQ:TOK].rearrange("p (s t) -> p s t", s=NSEQ)
                    for j in range(3):
                        w = conv_w[:, a, j:j + 1]
                        u_p, u_s = uext_flat[:, a, j:j + SEQ], sample_u[a][:, :, j:j + TNEW]
                        if j == 0:
                            v.tensor_scalar(y_p, u_p, w, None, ALU.mult)
                            link(v.tensor_scalar(y_s, u_s, w, None, ALU.mult))
                        else:
                            v.scalar_tensor_tensor(out=y_p, in0=u_p, scalar=w, in1=y_p, op0=ALU.mult, op1=ALU.add)
                            ins = v.scalar_tensor_tensor(out=y_s, in0=u_s, scalar=w, in1=y_s, op0=ALU.mult, op1=ALU.add)
                            if j == 1:
                                link(ins)
                            else:
                                last = ins
                elif kind == "conv_b":
                    if a == 0:
                        dve.wait_ge(dve_emptied, p_owner[at["conv_h", 3]][1])
                    last = v.tensor_tensor(halves(yconvT[:, a]), pair(n)[:, :, 0:HALF], halves(conv_tmp[:, a]), ALU.mult)
                elif kind == "pos_T":
                    last = v.tensor_copy(rowsT[:, :, POS0:NEW0], bank(n, 0)[:, 0:64].rearrange("p (v l) -> p v l", v=2))
                elif kind == "cmp":
                    last = v.tensor_copy(halves(kT[:, 6]), pair(n)[:, :, 0:HALF])
                elif kind == "rows":
                    if a[0] == 0 and a[1] == 0:
                        dve.wait_ge(bias_out, 16 * 4)
                    last = copy_rows(dve, n, a)
                elif kind == "win_k_T":
                    v.tensor_copy(kT[:, 7, 0:SEQ], bank(n, 0))
                    last = v.tensor_copy(kT[:, 7, SEQ:TOK], bank(n, 1)[:, 0:NS])
                elif kind == "page_T":
                    last = v.tensor_copy(rowsT[:, :, SEQ + PAST * a:SEQ + PAST * (a + 1)],
                                         bank(n, 0).rearrange("p (v t) -> p v t", v=2))
                elif kind in ("dil_q", "nsa_q"):
                    c = a + (6 if kind == "nsa_q" else 0)
                    last = v.tensor_scalar(halves(qT[:, c]), pair(n)[:, :, 0:HALF], SCALE, None, ALU.mult)
                elif kind == "k_rows":
                    if a >= 3:
                        dve.wait_ge(stage_out[a % 3], 32 * (a // 3))
                    v.tensor_copy(stage[a % 3][:, 0:QT, :], bank(n, 0).rearrange("p (i c) -> p i c", i=QT))
                    last = v.tensor_copy(stage[a % 3][0:NS, QT, :], bank(n, 1)[0:NS, 0:P])
                elif kind == "cmp_k_T":
                    last = v.tensor_copy(kcT[:, 0:NCMP - 1], bank(n, 0)[:, 0:NCMP - 1])
                elif kind == "cmp_v":
                    if a == 0:
                        last = v.tensor_copy(vcp[0:PROMPT_CMP], bank(n, 0)[0:PROMPT_CMP, 0:P])
                    else:
                        last = v.tensor_copy(vcs[0:SAMPLE_CMP].rearrange("p (h s) c -> p h (s c)", h=2), pair(n)[0:SAMPLE_CMP])
                last.then_inc(dve_emptied, 1)

            proj_all_emptied(dve)

            def table(u, s, w):
                kind, h, qt = UNITS[u]
                if kind == "dil":
                    return tab_dil0[:, h, 256 - w:256] if s == 0 else tab_dil[:, s - 1, h, 512 - w:512]
                if kind == "nsa":
                    return unseen[:, qt, :] if s == 0 else tab_nsa[:, 4 * h[0] + h[1], 512 - w:512]
                if kind == "sdil":
                    o = (0, 136, 400)[s]
                    return tab_sdil[:, o:o + w]
                return unseen[:, QT - 1, 0:w] if s == 0 else tab_snsa

            def biased_scores(u):
                if u >= 3:
                    tiles = key_tiles(UNITS[u - 3])
                    dve.wait_ge(turned, fill_at["probs", u - 3, (len(tiles) - 1) // 4] + 1)
                top, neg_max, _, _ = stat[u % 2]
                for s, w in enumerate(segments(UNITS[u])):
                    dve.wait_ge(scored, 3 * u + s + 1)
                    ins = v.tensor_tensor_reduce(probs_of(u, s, 0, w), ps[:, (3 * u + s) % 4, 0:w],
                                                 table(u, s, w), 1.0, -3e38, ALU.add, ALU.max, top[:, s:s + 1])
                    ins.then_inc(score_read, 1)
                dve.wait_ge(score_read, 3 * u + 3)
                if UNITS[u][0] in ("dil", "sdil"):
                    v.tensor_reduce(neg_max[:, 0:1], top, AX_X, ALU.max, negate=True).then_inc(max_ready, 1)
                else:
                    v.tensor_scalar(neg_max, top, -1.0, CLAMP, ALU.mult, ALU.min).then_inc(max_ready, 1)

            def scale_probs(u):
                kind, h, qt = UNITS[u]
                _, _, total, scale = stat[u % 2]
                dve.wait_ge(exp_ready, u + 1)
                joint = kind in ("dil", "sdil")
                if joint:
                    link(v.tensor_reduce(total[:, 0:1], total, AX_X, ALU.add))
                    link(v.reciprocal(scale[:, 0:1], total[:, 0:1]))
                else:
                    link(v.tensor_scalar(total, total, TINY, None, ALU.max))
                    link(v.reciprocal(scale, total))
                    gate = nsa_gate[:, qt, 4 * h[0] + h[1]:24:8] if kind == "nsa" else gate_s[:, h, :]
                    link(v.tensor_tensor(scale, scale, gate, ALU.mult))
                for s, w in enumerate(segments(UNITS[u])):
                    seg = probs_of(u, s, 0, w)
                    last = v.tensor_scalar(seg, seg, scale[:, 0:1] if joint else scale[:, s:s + 1], None, ALU.mult)
                last.then_inc(scaled, 1)

            def take_sums(u):
                kind, h, qt = UNITS[u]
                dve.wait_ge(summed, u + 1)
                src = ps[:, 6 + u % 2, :]
                if kind == "dil":
                    rows = slice(h % 2 * DH, h % 2 * DH + DH)
                    last = v.tensor_copy(ydilT[rows, h // 2, qt * P:(qt + 1) * P], src[rows, 0:P])
                elif kind == "nsa":
                    rows = slice(h[0] * DH, h[0] * DH + DH)
                    last = v.tensor_copy(ynsaT[rows, h[1], qt * P:(qt + 1) * P], src[rows, 0:P])
                elif kind == "sdil":
                    last = v.tensor_copy(sum_rows, src[:, 0:256])
                else:
                    for g in range(2):
                        rows = slice(g * DH, g * DH + DH)
                        got = src[rows, 0:P].rearrange("p (n g j t) -> p g j n t", n=2, g=2, j=4)
                        c0 = SEQ + 2 * h * TNEW
                        last = v.tensor_copy(ynsaT[rows, :, c0:c0 + 16].rearrange("p j (n t) -> p j n t", n=2), got[:, g])
                last.then_inc(out_read, 1)

            def take_turned_sums(u):
                m = fill_at["sums", u, 0]
                dve.wait_ge(turned, m + 1)
                for pr in range(2):
                    for x in range(2):
                        rows = slice(x * DH, x * DH + DH)
                        got = turn_bank(m)[rows, 128 * pr:128 * pr + 128].rearrange("p (n h t) -> p n h t", n=4, h=4)
                        c0 = SEQ + 4 * UNITS[u][1] * TNEW
                        last = v.tensor_copy(ydilT[rows, pr, c0:c0 + 32].rearrange("p (n t) -> p n t", n=4),
                                             got[:, :, 2 * pr + x, :])
                last.then_inc(dve_turned, 1)

            dve.wait_ge(gates_ready, 1)
            dve.wait_ge(tables_in, 64)
            dve.wait_ge(u_out, 32)
            for u in range(len(UNITS) + 4):
                if u == N_PROMPT:
                    dve.wait_ge(queries_built, 1)
                    dve.wait_ge(keys_kept, 1)
                    dve.wait_ge(sample_tables_in, 16 * 14)
                    dve.wait_ge(gates_in, 128)
                if begins_half(u):
                    scale_probs(u - 1)
                    for n in range(4 * UNITS[u][1], 4 * UNITS[u][1] + 4):
                        for f in range(4):
                            m = fill_at["keys", n, f]
                            dve.wait_ge(turned, m + 1)
                            dst = cache_key_rows(n, f)
                            w = 2 * dst.shape[2]
                            v.tensor_copy(dst, turn_bank(m)[:, 0:w].rearrange("p (r c) -> p r c", r=2)).then_inc(dve_turned, 1)
                if u < len(UNITS):
                    biased_scores(u)
                if u >= 5 and UNITS[u - 5][0] == "sdil":
                    take_turned_sums(u - 5)
                if u >= 4:
                    take_sums(u - 4)
                if 1 <= u <= len(UNITS) and not begins_half(u):
                    scale_probs(u - 1)

            def layer_norm(i, which, x):
                m = token_rows(i)
                for h in range(2):
                    ins = v.bn_stats(lnst[0:m, 6 * h:6 * h + 6], x[0:m, 512 * h:512 * h + 512])
                link(ins)
                link(v.bn_aggr(lnmv[0:m], lnst[0:m]))
                v.tensor_scalar(lnsd[0:m, 0:1], lnmv[0:m, 1:2], LN_EPS, None, ALU.add).then_inc(var_ready, 1)
                dve.wait_ge(sqrt_ready, which * NT + i + 1)
                link(v.reciprocal(lnsd[0:m, 2:3], lnsd[0:m, 1:2]))
                link(v.tensor_scalar(x[0:m], x[0:m], lnmv[0:m, 0:1], lnsd[0:m, 2:3], ALU.subtract, ALU.mult))
                link(v.tensor_tensor(x[0:m], x[0:m], ln[0:m, 2 * which, :], ALU.mult))
                return v.tensor_tensor(x[0:m], x[0:m], ln[0:m, 2 * which + 1, :], ALU.add)

            def experts_of_group(i):
                return routing(i).rearrange("p t (g x) -> p t g x", g=4)

            def first_best(mask, values):
                best = tmp1[:, 0:NT]
                wide = best.unsqueeze(2).broadcast_to([P, NT, 16])
                places = ramp[:, 0:16].unsqueeze(1).broadcast_to([P, NT, 16])
                link(v.tensor_reduce(best, values, AX_X, ALU.max))
                link(v.tensor_tensor(mask, values, wide, ALU.is_equal))
                link(v.tensor_tensor(mask, mask, places, ALU.mult))
                link(v.tensor_reduce(best, mask, AX_X, ALU.max))
                link(v.tensor_tensor(mask, mask, wide, ALU.is_equal))

            def choose_experts():
                aff, score, masked, first, second, both, tmp = (routing(k) for k in range(7))
                later_emptied(dve, "router", 0)
                link(v.tensor_tensor(score, aff, router_b.unsqueeze(1).broadcast_to([P, NT, 16]), ALU.add))
                sg = experts_of_group(1)
                for o, x in ((0, 0), (3, 1), (5, 2)):
                    n = 3 - x
                    ins = v.tensor_tensor(pair_sums[:, :, :, o:o + n], sg[:, :, :, x + 1:4],
                                          sg[:, :, :, x:x + 1].broadcast_to([P, NT, 4, n]), ALU.add)
                link(ins)
                link(v.tensor_reduce(group_score, pair_sums, AX_X, ALU.max))
                best = tmp1[:, 0:NT]
                wide = best.unsqueeze(2).broadcast_to([P, NT, 4])
                link(v.tensor_reduce(best, group_score, AX_X, ALU.max))
                link(v.tensor_tensor(group_hot, group_score, wide, ALU.is_equal))
                link(v.tensor_tensor(group_hot, group_hot, ramp[:, 16:20].unsqueeze(1).broadcast_to([P, NT, 4]), ALU.mult))
                link(v.tensor_reduce(best, group_hot, AX_X, ALU.max))
                link(v.tensor_tensor(group_hot, group_hot, wide, ALU.is_equal))
                hot4 = group_hot.unsqueeze(3).broadcast_to([P, NT, 4, 4])
                v.tensor_tensor(experts_of_group(2), sg, hot4, ALU.mult)
                link(v.tensor_scalar(experts_of_group(6), hot4, -NEG, NEG, ALU.mult, ALU.add))
                link(v.tensor_tensor(masked, masked, tmp, ALU.add))
                first_best(first, masked)
                link(v.scalar_tensor_tensor(out=masked, in0=first, scalar=2 * NEG, in1=masked, op0=ALU.mult, op1=ALU.add))
                first_best(second, masked)
                link(v.tensor_tensor(both, first, second, ALU.add))
                ins = v.memset(both[64:P, QT, :], 0.0)
                ins.then_inc(chosen, 1)
                for j, hot_j in enumerate((first, second)):
                    link(v.tensor_tensor(tmp, aff, hot_j, ALU.mult))
                    link(v.tensor_reduce(gates2[:, j, :], tmp, AX_X, ALU.add))
                link(v.tensor_tensor(best, gates2[:, 0, :], gates2[:, 1, :], ALU.add))
                link(v.reciprocal(best, best))
                link(v.tensor_tensor(gates2, gates2, best.unsqueeze(1).broadcast_to([P, 2, NT]), ALU.mult))

            def place_tokens(n):
                _, _, _, first, second, _, tmp, rank, blk, row, entry = (routing(k) for k in range(11))
                link(v.tensor_copy(rank, bank(n, 0)[:, 0:16 * NT].rearrange("p (i e) -> p i e", e=16)))
                link(v.tensor_scalar(blk, rank, float(P), None, ALU.is_ge))
                for x in range(2, BIG_BLOCKS):
                    link(v.scalar_tensor_tensor(out=blk, in0=rank, scalar=float(x * P), in1=blk, op0=ALU.is_ge, op1=ALU.add))
                spread = lambda c0: ramp[:, c0:c0 + 16].unsqueeze(1).broadcast_to([P, NT, 16])
                link(v.tensor_tensor(row, rank, spread(20), ALU.add))
                link(v.scalar_tensor_tensor(out=row, in0=blk, scalar=float((N_EXP - 1) * P), in1=row, op0=ALU.mult, op1=ALU.add))
                link(v.scalar_tensor_tensor(out=entry, in0=rank, scalar=float(N_BLOCK), in1=spread(36), op0=ALU.mult, op1=ALU.add))
                link(v.scalar_tensor_tensor(out=entry, in0=blk, scalar=float(N_EXP - P * N_BLOCK), in1=entry, op0=ALU.mult, op1=ALU.add))
                for x, (hot_x, where) in enumerate(((first, row), (second, row), (first, entry), (second, entry))):
                    link(v.tensor_tensor(tmp, hot_x, where, ALU.mult))
                    link(v.tensor_reduce(dst_f[:, x, :], tmp, AX_X, ALU.add))
                v.tensor_copy(dst_i, dst_f)
                link(v.tensor_reduce(tmp1[:, 0:1], bank(n, 1)[:, 0:16], AX_X, ALU.max))
                link(v.tensor_copy(count_i, tmp1[:, 0:1]))
                dve.engine_nop().then_inc(indices_ready, 1)
                return v.memset(tmp1[:, 0:1], 0.0)

            branches = 0
            for n, (kind, a) in enumerate(later):
                if l_owner[n][0]:
                    continue
                if kind == "ple_proj" and a == 0:
                    choose_experts()
                dve.wait_ge(later_filled, n + 1)
                if kind == "branch":
                    c, b = a
                    later_emptied(dve, "gate", a)
                    src, g = pair(n)[:, :, 0:HALF], halves(sig[branches % 2])
                    branches += 1
                    if b == 0:
                        last = v.tensor_tensor(halves(mT[:, c]), g, src, ALU.mult)
                    else:
                        link(v.tensor_tensor(g, g, src, ALU.mult))
                        last = v.tensor_tensor(halves(mT[:, c]), halves(mT[:, c]), g, ALU.add)
                elif kind == "mix":
                    m = token_rows(a)
                    x = res[:, a, :]
                    if a == 0:
                        link(v.memset(routing(0), 1.0))
                        dve.engine_nop().then_inc(route_zeroed, 1)
                    dve.wait_ge(res_in[a], 16)
                    ins = v.scalar_tensor_tensor(out=x[0:m].rearrange("p (h c) -> p h c", h=2),
                                                 in0=x[0:m].rearrange("p (h c) -> p h c", h=2), scalar=ALPHA,
                                                 in1=pair(n)[0:m], op0=ALU.mult, op1=ALU.add)
                    ins.then_inc(dve_later, 1)
                    wait_emptied(dve, l_owner, n, act_later, dve_later)
                    if a == 0:
                        dve.wait_ge(late_in, 80)
                    layer_norm(a, 0, x).then_inc(x1_ready, 1)
                    continue
                elif kind == "x1_T":
                    i, h = a
                    m = token_rows(i)
                    src = bank(n, 0)[:, 0:4 * m].rearrange("p (k t) -> p k t", k=4)
                    last = v.tensor_copy(x1T[:, 4 * h:4 * h + 4, i * P:i * P + m], src)
                elif kind == "p_T":
                    m = token_rows(a)
                    last = v.tensor_copy(pT[:, :, a * P:a * P + m], bank(n, 0)[:, 0:2 * m].rearrange("p (k t) -> p k t", k=2))
                elif kind == "ple_proj":
                    m = token_rows(a)
                    later_emptied(dve, "ple_gate", a)
                    g = ple_sig[a % 2][0:m].rearrange("p (h c) -> p h c", h=2)
                    ins = v.tensor_tensor(g, g, pair(n)[0:m], ALU.mult)
                    link(ins)
                    if a == 0:
                        for i in range(NT):
                            dve.wait_ge(x1_stored[i], 16)
                        for h in range(2):
                            dve.wait_ge(later_filled, lat["x1_T", (NT - 1, h)] + 1)
                    last = v.scalar_tensor_tensor(out=res[0:m, a, :], in0=res[0:m, a, :], scalar=ALPHA,
                                                  in1=ple_sig[a % 2][0:m], op0=ALU.mult, op1=ALU.add)
                elif kind == "rank":
                    last = place_tokens(n)
                last.then_inc(dve_later, 1)

            def take_x(s):
                return v.tensor_copy(xgT[s][:, 4:8, :], ps[:, 1, :].rearrange("p (k t) -> p k t", k=4))

            def take_hT():
                return v.tensor_copy(hT, ps[:, 4, :].rearrange("p (k t) -> p k t", k=4))

            def take_y(s):
                return v.tensor_copy(y_exp[s][:, 512:1024], ps[:, 6, :])

            def turned_hidden(q, s):
                e = 2 * q + s
                dve.wait_ge(h_turned, e + 1)
                if not (isinstance(q, int) and q == 0 and s == 0):
                    dve.wait_ge(down_done, e)
                take_hT().then_inc(hT_ready, 1)

            def finish_expert(q, s):
                dve.wait_ge(down_done, 2 * q + s + 1)
                if not (isinstance(q, int) and q == 0):
                    dve.wait_ge(y_stored[s], 16 * q)
                take_y(s).then_inc(dve_y, 1)

            def expert_step(q, s, last=False):
                e = 2 * q + s
                first = isinstance(q, int) and q == 0 and s == 0
                pq, p_s = (q, 0) if s else (q - 1, 1)
                if not first:
                    turned_hidden(pq, p_s)
                dve.wait_ge(up_done, e + 1)
                dve.wait_ge(silu_done, e + 1)
                v.tensor_tensor(h_tok, silu, ps[:, 3, :], ALU.mult).then_inc(h_ready, 1)
                if not last:
                    dve.wait_ge(x_turned, e + 2)
                    take_x(1 - s).then_inc(dve_x, 1)
                if not first:
                    finish_expert(pq, p_s)

            dve.wait_ge(x_turned, 1)
            take_x(0).then_inc(dve_x, 1)
            expert_step(0, 0)
            expert_step(0, 1)
            with dve.Fori(1, N_EXP // 2 - 1) as q:
                expert_step(q, 0)
                expert_step(q, 1)
            expert_step(N_EXP // 2 - 1, 0)
            expert_step(N_EXP // 2 - 1, 1, last=True)
            turned_hidden(N_EXP // 2 - 1, 1)
            finish_expert(N_EXP // 2 - 1, 1)

            most = dve.value_load(count_i[0:1, :], min_val=0, max_val=TOK)
            with dve.If(most > P):
                with dve.Fori(1, N_BLOCK - N_EXP + 1) as b:
                    dve.wait_ge(over["x_turned"], b)
                    take_x(0).then_inc(over["dve_x"], 1)
                    dve.wait_ge(over["up"], b)
                    dve.wait_ge(over["silu"], b)
                    v.tensor_tensor(h_tok, silu, ps[:, 3, :], ALU.mult).then_inc(over["h"], 1)
                    dve.wait_ge(over["h_turned"], b)
                    take_hT().then_inc(over["hT"], 1)
                    dve.wait_ge(over["down"], b + 1)
                    take_y(0).then_inc(over["dve_y"], 1)

            for i in range(NT):
                m = token_rows(i)
                dve.wait_ge(picked_in[i % 2], 32 * (i // 2 + 1))
                x = res[0:m, i, :]
                for j in range(2):
                    link(v.scalar_tensor_tensor(out=x, in0=picked[i % 2][j][0:m], scalar=gates2[0:m, j, i:i + 1], in1=x,
                                                op0=ALU.mult, op1=ALU.add))
                layer_norm(i, 1, res[:, i, :]).then_inc(combined, 1)


        @block.gpsimd
        def _(pool):
            link = chained(pool, pool_chain)
            proj_emptied(pool, "bias_row", 3)
            for kind, rows in enumerate((range(12, 20), range(0, 4), range(4, 8), range(8, 12))):
                row = bias_rows[rows[0]:rows[-1] + 1, kind, :]
                pool.dma_start(bias_d[rows[0]:rows[-1] + 1], row.unsqueeze(1).broadcast_to([len(rows), P, RLEN])).then_inc(bias_out, 16)
            proj_emptied(pool, "u_T", 0)
            pool.dma_start(O["conv_prompt"][0, 0], u_rows[0:2]).then_inc(u_out, 16)
            pool.dma_start(O["conv_sample"][0].rearrange("n r c -> (n r) c"), u_rows[2:18]).then_inc(u_out, 16)
            for c in range(3):
                for i in range(NT):
                    proj_emptied(pool, "rows", (c, i))
                if c == 0:
                    store_rows(pool, "kv", 384, SEL_V, P)
                    store_rows(pool, "win", 0, WIN_K, 2 * P)
            for t in range(3):
                store_rows(pool, f"dil{t}", 256, 256 * t, 256)
            for c in range(9):
                proj_emptied(pool, "k_rows", c)
                name = "kv" if c >= 6 else f"dil{c // 2}"
                col = (256, 0, 128)[c - 6] if c >= 6 else c % 2 * P
                first = QT - O[name + "_prompt"].shape[2] // P
                dst = token_view(name + "_prompt").rearrange("(i p) c -> p i c", p=P)
                pool.dma_start(dst[:, :, col:col + P], stage[c % 3][:, first:QT, :]).then_inc(stage_out[c % 3], 16)
                pool.dma_start(token_view(name + "_sample")[:, col:col + P], stage[c % 3][0:NS, QT, :]).then_inc(stage_out[c % 3], 16)

            proj_all_emptied(pool)
            for i in range(3):
                pool.wait_ge(stage_out[i], 96)
            nc.gpsimd.memset(view(41464, 2, 3 * P), 0.0).then_inc(q_pad_zeroed, 1)
            nc.gpsimd.memset(q_dil, 0.0)
            nc.gpsimd.memset(q_nsa, 0.0).then_inc(queries_zeroed, 1)
            nc.gpsimd.tensor_copy(k_new, kT[:, :, SEQ:TOK]).then_inc(keys_kept, 1)
            pool.wait_ge(gates_ready, 1)
            pool.dma_start(gates_d, nsa_gate[0:NS, QT, :]).then_inc(gates_out, 16)
            pool.wait_ge(gates_out, 16)
            for m in range(4):
                for n2 in range(2):
                    src = bass.AP(tensor=gates_d.tensor, offset=(2 * m + n2) * TNEW * 24, ap=[[3, 8], [24, TNEW], [1, 3]])
                    pool.dma_start(gate_s[64 * n2:64 * n2 + 64, m, :], src).then_inc(gates_in, 16)
            pool.wait_ge(queries_built, 1)
            pool.wait_ge(keys_kept, 1)

            def load_dil_values(n):
                for t in range(3):
                    load_rows(pool, t, n, 1, v_cache[n % 4], dil_v_in[n % 4])
                pool.dma_start(new_dil_v[n % 4][0:TNEW], vtok[n * TNEW:(n + 1) * TNEW, QT, 0:768]).then_inc(dil_v_in[n % 4], 16)

            for n in range(NSEQ):
                pool.wait_ge(scored, 3 * (N_PROMPT + (0 if n < 4 else 3)))
                nc.gpsimd.tensor_copy(cacheT[n % 4][:, 0:272].rearrange("p (r c) -> p r c", r=2)[:, :, P:P + TNEW],
                                      k_new[:, 0:2, n * TNEW:(n + 1) * TNEW])
                nc.gpsimd.tensor_copy(cacheT[n % 4][:, 272:KT_W].rearrange("p (r c) -> p r c", r=6)[:, :, PAST:PAST + TNEW],
                                      k_new[:, 2:8, n * TNEW:(n + 1) * TNEW]).then_inc(new_keys_put, 1)
                if n == 3:
                    pool.wait_ge(score_read, 3 * N_PROMPT)
                    for x in range(4):
                        load_dil_values(x)
            pool.wait_ge(summed, N_PROMPT + 1)
            for n in range(4, NSEQ):
                load_dil_values(n)

            link(nc.gpsimd.memset(zeros_i, 0))
            flat_list = list_d.rearrange("(p b) o -> p (b o)", p=P)
            pool.dma_start(flat_list, zeros_i).then_inc(list_zeroed, 16)
            for i in range(NT):
                m = token_rows(i)
                pool.wait_ge(x1_ready, i + 1)
                pool.dma_start(x1_d[i * P:i * P + m, :], res[0:m, i, :]).then_inc(x1_stored[i], 16)
            pool.wait_ge(indices_ready, 1)
            pool.wait_ge(list_zeroed, 16)
            for j in range(2):
                for i in range(NT):
                    m = token_rows(i)
                    pool.indirect_dma_start(list_d, bass.IndirectOffsetOnAxis(ap=dst_i[0:m, 2 + j, i:i + 1], axis=0),
                                            token[0:m, i:i + 1], None).then_inc(listed, 16)
            pool.wait_ge(listed, 160)
            pool.dma_start(block_tok, flat_list.bitcast(U32)).then_inc(list_in, 16)
            pool.wait_ge(list_in, 16)
            for i in range(NT):
                pool.wait_ge(x1_stored[i], 16)

            def gather(e, signal):
                pool.indirect_dma_start(xg[e % 2], None, x1_d, bass.IndirectOffsetOnAxis(ap=block_tok[:, e:e + 1], axis=0))\
                    .then_inc(signal, 16)

            pool.wait_ge(later_filled, len(later))
            gather(0, xg_in[0])
            gather(1, xg_in[1])
            for e in range(N_EXP):
                if e + 2 < N_EXP:
                    pool.wait_ge(x_turned, e + 1)
                    gather(e + 2, xg_in[e % 2])
                pool.wait_ge(act_y, e + 1)
                pool.wait_ge(dve_y, e + 1)
                pool.dma_start(y_d[e * P:(e + 1) * P, :], y_exp[e % 2]).then_inc(y_stored[e % 2], 16)
            pool.wait_ge(y_stored[0], 16 * N_EXP // 2)
            pool.wait_ge(y_stored[1], 16 * N_EXP // 2)

            def pick_rows(written):
                for i in range(NT):
                    m = token_rows(i)
                    if i >= 2:
                        pool.wait_ge(combined, i - 1)
                    for j in range(2):
                        pool.indirect_dma_start(picked[i % 2][j][0:m], None, written,
                                                bass.IndirectOffsetOnAxis(ap=dst_i[0:m, j, i:i + 1], axis=0))\
                            .then_inc(picked_in[i % 2], 16)

            most = pool.value_load(count_i[0:1, :], min_val=0, max_val=TOK)
            with pool.If(most > P):
                with pool.Fori(1, N_BLOCK - N_EXP + 1) as b:
                    pool.wait_ge(over["down"], b)
                    last = nc.gpsimd.tensor_copy(zeros_i[:, 0:1].bitcast(U32), block_tok[:, bass.ds(b + N_EXP - 1, 1)])
                    last.then_inc(over["list"], 1)
                    pool.wait_ge(over["list"], b)
                    spare = zeros_i[:, 1:2].bitcast(F32)
                    nc.gpsimd.tensor_tensor(spare, spare, spare, ALU.add)
                    pool.indirect_dma_start(xg[0], None, x1_d, bass.IndirectOffsetOnAxis(ap=zeros_i[:, 0:1].bitcast(U32), axis=0))\
                        .then_inc(over["x"], 16)
                    pool.wait_ge(over["act_y"], b)
                    pool.wait_ge(over["dve_y"], b)
                    pool.dma_start(y_d[bass.ds((b + N_EXP - 1) * P, P), :], y_exp[0]).then_inc(over["stored"], 16)
                    pool.wait_ge(over["stored"], 16 * b)
                pick_rows(y_d)
            with pool.Else():
                pick_rows(y_d[0:N_EXP * P])
            for i in range(3):
                pool.wait_ge(stage_out[i], 96)
            pool.wait_ge(v_out, 160)



OUTPUTS = [
    ("y_prompt", (1, SEQ, D)), ("y_sample", (NSEQ, TNEW, D)),
    ("conv_prompt", (1, 1, 2, CONV)), ("conv_sample", (1, NSEQ, 2, CONV)),
    ("dil0_prompt", (1, 1, 128, 2, 4, DH)), ("dil0_sample", (1, NSEQ, TNEW, 2, 4, DH)),
    ("dil1_prompt", (1, 1, SEQ, 2, 4, DH)), ("dil1_sample", (1, NSEQ, TNEW, 2, 4, DH)),
    ("dil2_prompt", (1, 1, SEQ, 2, 4, DH)), ("dil2_sample", (1, NSEQ, TNEW, 2, 4, DH)),
    ("win_prompt", (1, 1, SEQ, 2, 2, DH)), ("win_sample", (1, NSEQ, TNEW, 2, 2, DH)),
    ("kv_prompt", (1, 1, SEQ, 4, 2, DH)), ("kv_sample", (1, NSEQ, TNEW, 4, 2, DH)),
]


def build(nc, inputs):
    arrays, A, C, O = {}, {}, {}, {}
    for group, values in ((A, inputs), (C, shape_constants())):
        for name, value in values.items():
            a = np.ascontiguousarray(value)
            arrays[name + "_dram"] = a
            group[name] = nc.dram_tensor(name + "_dram", a.shape, mybir.dt.from_np(a.dtype), kind="ExternalInput").ap()
    for name, shape in OUTPUTS:
        O[name] = nc.dram_tensor(name + "_out", shape, F32, kind="ExternalOutput").ap()
    bass_hybrid_decoder_step_kernel(nc, A, C, O)
    return arrays


def kernel(**inputs):
    import concourse.bacc as bacc
    from concourse.bass_utils import run_bass_kernel_spmd

    nc = bacc.Bacc("TRN2", target_bir_lowering=False, num_devices=1)
    arrays = build(nc, inputs)
    r = run_bass_kernel_spmd(nc, [arrays], core_ids=[0])
    return tuple(r.results[0][name + "_out"] for name, _ in OUTPUTS)
```

```python
from contextlib import ExitStack

import numpy as np

import concourse.bass as bass
from concourse import mybir

F32 = mybir.dt.float32
I32 = mybir.dt.int32
U32 = mybir.dt.uint32
ALU = mybir.AluOpType
ACT = mybir.ActivationFunctionType
AX_X = mybir.AxisListType.X

P = 128
D = 1024
KC = D // P
SEQ = 512
NSEQ = 8
TNEW = 8
NS = NSEQ * TNEW
TOK = SEQ + NS
NT = (TOK + P - 1) // P
QT = SEQ // P
HALF = TOK // 2
PAST = 256
DH = 64
CONV = 512
CMP_BLOCK, CMP_STRIDE, CMP_HID = 32, 16, 128
N_EXP, D_EXP = 16, 512
MERGE0 = 5144
NEG = -1e30
TINY = 1e-30
CLAMP = 1e29
ALPHA = 2.0 ** 0.25
LN_EPS = 1e-5
RLEN = 640
NCMP = (SEQ + NSEQ * PAST) // CMP_STRIDE
POS0 = SEQ + NSEQ * PAST
PAIRS = (POS0 + CMP_BLOCK) // 2
PROMPT_CMP = (SEQ - CMP_BLOCK) // CMP_STRIDE + 1
SAMPLE_CMP = (PAST + TNEW - CMP_BLOCK) // CMP_STRIDE + 1
BIG_BLOCKS = (TOK + P - 1) // P
N_BLOCK = N_EXP * BIG_BLOCKS
VW = 1176
SEL_V, WIN_K, WIN_V, GATES = 768, 896, 1024, 1152
KT_W = 2 * 136 + 4 * 264 + 2 * 264
SCALE = DH ** -0.5


def token_rows(i):
    return P if i < NT - 1 else NS


def bucket_of(dist):
    if dist < 16:
        return dist
    return min(16 + int(np.log(dist / 16) / np.log(2048 / 16) * 16), 31)


def bias_one_hot():
    hot = np.zeros((33, 4, RLEN), np.float32)
    for kind, (step, reach) in enumerate([(1, 511), (1, 128), (4, 512), (16, 2048)]):
        for i in range(RLEN):
            dist = 511 - i
            masked = dist < 0 or dist % step or dist > reach
            hot[32 if masked else bucket_of(dist), kind, i] = 1.0
    return hot


def shape_constants():
    query = np.arange(SEQ)[:, None]
    end = np.arange(PROMPT_CMP)[None, :] * CMP_STRIDE + CMP_BLOCK - 1
    unseen = np.where(end <= query, 0.0, NEG).astype(np.float32)
    ramp = np.zeros((P, 52), np.float32)
    ramp[:, 0:16] = 16 - np.arange(16)
    ramp[:, 16:20] = 4 - np.arange(4)
    ramp[:, 20:36] = np.arange(16) * P
    ramp[:, 36:52] = np.arange(16)
    token = np.arange(NT)[None, :] * P + np.arange(P)[:, None]
    return {
        "c_ident": np.eye(P, dtype=np.float32),
        "c_before": np.triu(np.ones((P, P), np.float32), 1),
        "c_hot": bias_one_hot(),
        "c_neg": np.full((1, 20), NEG, np.float32),
        "c_unseen": np.ascontiguousarray(unseen.reshape(QT, P, PROMPT_CMP).transpose(1, 0, 2)),
        "c_ramp": ramp,
        "c_token": token.astype(np.int32),
    }


GROUPS = [(512, 512), (1024, 512), (0, 512), (4352, 384), (4736, 408), (3072, 384), (3456, 384),
          (1536, 384), (1920, 384), (2304, 384), (2688, 384), (3840, 512)]
WSLOTS = 3
NSA_Q_GROUP = 11
FEATURE = {"conv_c": (0, 4), "conv_h": (1, 4), "conv_b": (2, 4), "cmp": (3, 3), "dil_q": (7, 3),
           "dil_k": (9, 3), "nsa_q": (11, 4)}


def projection_tasks():
    t = [("x_T", (i, h)) for i in range(NT) for h in range(2)]
    t += [("bias_row", k) for k in range(4)]
    t += [("state_T", 0)]
    t += [("conv_c", c) for c in range(4)] + [("conv_h", c) for c in range(4)]
    t += [("u_T", 0)]
    t += [("conv_b", c) for c in range(4)]
    t += [("pos_T", 0)]
    t += [("cmp", c) for c in range(3)]
    t += [("rows", (c, i)) for c in range(3) for i in range(NT)]
    t += [("win_k_T", 0)]
    for c in range(6):
        t += [("dil_q", c)] + [("page_T", s) for s in range(2 * c, min(2 * c + 2, NSEQ))]
    t += [("dil_k", c) for c in range(6)]
    t += [("k_rows", c) for c in range(6)]
    t += [("nsa_q", c) for c in range(4)]
    t += [("hidden", (kv, g)) for kv in range(2) for g in range(2)]
    t += [("k_rows", c) for c in range(6, 9)]
    t += [("cmp_k_T", 0), ("cmp_v", 0), ("cmp_v", 1)]
    return t


ACT_EMPTIES = {"conv_c", "u_T", "cmp", "dil_k", "hidden"}


def emptied_by_act(kind, a):
    if kind == "x_T":
        return a[1] == 1
    if kind == "rows":
        return a[1] % 2 == 1
    if kind == "cmp":
        return a < 2
    if kind in ("dil_q", "nsa_q"):
        return a % 2 == 1
    return kind in ACT_EMPTIES


def owners(tasks, by_act):
    done, out = [0, 0], []
    for kind, a in tasks:
        act = by_act(kind, a)
        done[act] += 1
        out.append((act, done[act]))
    return out, done[1], done[0]


def attention_units():
    dil = [("dil", 2 * c + r, qt) for c in range(2) for qt in range(QT) for r in range(2)]
    nsa = [("nsa", (g, j), qt) for j in range(4) for qt in range(QT) for g in range(2)]
    return dil + nsa


def sample_units():
    out = []
    for half in range(2):
        out += [("sdil", half, 0), ("snsa", 2 * half, 0), ("snsa", 2 * half + 1, 0)]
    return out


UNITS = attention_units() + sample_units()
N_DIL, N_PROMPT = QT * 4, QT * 12


def segments(unit):
    kind, _, qt = unit
    if kind == "dil":
        return [P * min(2, qt + 1), P * (qt + 1), P * (qt + 1)]
    if kind == "nsa":
        return [PROMPT_CMP, P * (qt + 1), P * (qt + 1)]
    if kind == "sdil":
        return [136, 264, 264]
    return [SAMPLE_CMP, 264, 264]


def first_column(unit, s):
    if unit[0] in ("dil", "sdil"):
        return sum(segments(unit)[:s])
    return (0, 256, 768)[s] if unit[0] == "nsa" else (0, 16, 280)[s]


def key_tiles(unit):
    out = []
    for s, w in enumerate(segments(unit)):
        out += [(s, a, min(P, w - a)) for a in range(0, w, P)]
    return out


def begins_half(u):
    return u < len(UNITS) and UNITS[u][0] == "sdil"


def fill_plan():
    fills = []
    for u in range(len(UNITS) + 3):
        if 2 <= u < len(UNITS) + 2:
            tiles = len(key_tiles(UNITS[u - 2]))
            fills += [("probs", u - 2, f) for f in range((tiles + 3) // 4)]
        if begins_half(u):
            half = UNITS[u][1]
            fills += [("keys", 4 * half + n, f) for n in range(4) for f in range(4)]
        if u >= 4 and UNITS[u - 4][0] == "sdil":
            fills.append(("sums", u - 4, 0))
    return fills


FILLS = fill_plan()


def later_tasks():
    t = []
    for c in range(KC):
        for b in range(3):
            t += [("gate", (c, b)), ("branch", (c, b))]
    for i in range(NT):
        t += [("mix", i)]
        if 1 <= i < QT:
            t += [("x1_T", (i - 1, h)) for h in range(2)]
    t += [("p_T", i) for i in range(NT)]
    t += [("x1_T", (i, h)) for i in (QT - 1, QT) for h in range(2)]
    t += [("router", 0)]
    for i in range(NT):
        t += [("ple_gate", i), ("ple_proj", i)]
        if i == 1:
            t += [("rank", 0)]
    return t


def later_by_act(kind, a):
    return kind in ("gate", "ple_gate", "router", "p_T") or (kind == "x1_T" and a[1] == 1)


def bass_hybrid_decoder_step_kernel(nc, A, C, O):
    proj = projection_tasks()
    p_owner, p_act, p_dve = owners(proj, emptied_by_act)
    at = {}
    for n, t in enumerate(proj):
        at[t] = n
    later = later_tasks()
    l_owner, l_act, l_dve = owners(later, later_by_act)
    lat = {t: n for n, t in enumerate(later)}
    fill_at = {f: n for n, f in enumerate(FILLS)}
    f_owner, f_act, f_dve = owners([(k, (w, f)) for k, w, f in FILLS], lambda k, a: k == "probs")

    def group_of(kind, a):
        if kind == "rows":
            return 4 + a[0], 0
        first, n = FEATURE[kind]
        return first + a // n, a % n * P

    group_done = [0] * len(GROUPS)
    for n, (kind, a) in enumerate(proj):
        if kind in FEATURE or kind == "rows":
            group_done[group_of(kind, a)[0]] = n + 1

    ctx = ExitStack()
    with ctx:
        arena = ctx.enter_context(nc.sbuf_tensor("arena", [P, 53200], F32))
        ps = ctx.enter_context(nc.psum_tensor("ps", [P, 8, 512], F32))

        def sem(name):
            return ctx.enter_context(nc.semaphore(name))

        def sems(name, n):
            return [sem(f"{name}{i}") for i in range(n)]

        def view(off, *shape):
            n = int(np.prod(shape))
            flat = arena[:, off:off + n]
            if len(shape) == 1:
                return flat
            names = "abcde"[:len(shape)]
            sizes = {c: s for c, s in zip(names, shape)}
            return flat.rearrange(f"p ({' '.join(names)}) -> p {' '.join(names)}", **sizes)

        def dram(name, shape, dt=F32):
            return nc.dram_tensor(name, shape, dt, kind="Internal").ap()

        xT = view(0, KC, TOK)
        qT = view(4608, 10, TOK)
        kT = view(10368, 8, TOK)
        vtok = view(14976, NT, VW)
        yconvT = view(20856, 4, TOK)
        ydilT = view(23160, 2, TOK)
        ynsaT = view(24312, 4, TOK)
        hot = view(23160, 4, RLEN)
        bias_rows = view(14976, 4, RLEN)
        state_tok = view(25720, CONV)
        pos_tok = view(26232, P)
        u_rows = view(25720, CONV)
        wslot = [view(26616 + 4096 * i, 4096) for i in range(WSLOTS)]
        xtok = view(38904, NT, D)
        row_pairs = [view(38904 + 2 * PAIRS * g, 2, PAIRS) for g in range(2)]
        swap = view(46296, 2, PAIRS)
        cmp_rows = view(44856, 2, TOK)
        uext_flat = view(44216, 4, 594)
        conv_tmp = view(46592, 4, TOK)
        stage = [view(48896 + 640 * i, NT, P) for i in range(3)]
        pages = [view(50816 + 512 * i, 2, 256) for i in range(2)]
        w1 = view(26616, 2, CMP_BLOCK // 2, CMP_HID)
        hidden = view(44216, 4, 160)
        vcs = view(44856, NSEQ, P)
        vcp = view(45880, P)
        w2 = view(46008, 2, DH)
        kcT = view(46136, 160)
        tab_nsa = view(26616, 8, 512)
        tab_dil0 = view(30712, 4, 256)
        tab_dil = view(31736, 2, 4, 512)
        probs = [view(o, 1280) for o in (42232, 35832, 37112)]
        probsT = [view(38904 + 1280 * i, 10, P) for i in range(2)]
        q_pad = [view(41464 + 384 * r, 3, P) for r in range(2)]
        cacheT = [view(4608 + KT_W * i, KT_W) for i in range(4)]
        new_dil_v = [view(o, 768) for o in (12032, 12800, 13568, 34712)]
        new_nsa_v = [view(o, 256) for o in (14336, 14592, 38392, 35480, 17024, 17280, 17536, 17792)]
        sum_rows = view(46296, 256)
        k_new = view(43512, 8, NS)
        q_nsa = view(44216, NSEQ, 64)
        k_cache = [view(o, 1792) for o in (46592, 48384, 41464)]
        q_dil = view(50176, 6, NSEQ, 32)
        dil_v_cache = [view(o, 1280) for o in (30712, 31992, 26616, 27896, 18048, 31992, 26616, 27896)]
        nsa_v_cache = [view(o, 512) for o in [33272, 29176, 29688, 30200] + [14976 + 512 * i for i in range(4)]]
        tab_sdil = view(33784, 664)
        tab_snsa = view(34448, 264)
        sample_probs = [view(o, 664) for o in (36448, 35832, 37112)]
        gate_w = [view(o, KC, 3, 256) for o in (4608, 26616, 32760, 26616)]
        w_nsa = view(38904, 4, D)
        w_dil = view(43000, 2, D)
        w_conv = view(46592, 4, D)
        sig = [view(50688 + 576 * i, TOK) for i in range(2)]
        gated = view(45048, TOK)
        mT = view(14976, KC, TOK)
        w_out = view(4608, KC, D)
        res = view(46720, NT, D)
        x1T = view(42112, KC, TOK)
        ln = view(38016, 4, D)
        ple_w = view(29824, KC, D)
        ple_p = view(27776, 2, D)
        p_tok = view(24576, NT, 256)
        pT = view(25856, 2, TOK)
        ple_sig = [view(19584 + 1024 * i, D) for i in range(2)]
        group_score = view(21632 + 80 * 12, NT, 4)
        group_hot = view(21632 + 80 * 13, NT, 4)
        pair_sums = view(21632 + 80 * 14, NT, 4, 6)

        def routing(k):
            return view(21632 + 80 * k, NT, 16)

        ew = [[view(12288 * i + 4096 * j, 4096) for j in range(3)] for i in range(2)]
        xg = [view(29824 + 1024 * i, D) for i in range(2)]
        xg_first = view(24576, D)
        gate_diag = view(25856, 2, NT, P)
        xgT = [view(31872 + 1024 * i, KC, P) for i in range(2)]
        silu = view(33920, D_EXP)
        h_tok = view(34432, D_EXP)
        hT = view(34944, 4, P)
        y_exp = [view(35456 + 1024 * i, D) for i in range(2)]
        picked = [[view(12288 + 2048 * i + 1024 * j, D) for j in range(2)] for i in range(NT)]
        ident = view(51840, P)
        before = view(51968, P)
        ones = view(52096, P)
        ramp = view(52224, 52)
        unseen = view(52280, QT, PROMPT_CMP)
        conv_w = view(52404, 4, 3)
        rel = view(52424, 20)
        nsa_gate = view(52444, NT, 24)
        gate_s = view(52564, 4, 3)
        router_w = view(52576, KC, 16)
        router_b = view(52704, 16)
        u_last = view(52720, 4, 18)
        stat = [[view(52792 + 16 * i + 4 * j, 3) for j in range(4)] for i in range(2)]
        gelu_b = view(52824, 4)
        lnst = view(52828, 12)
        lnmv = view(52840, 2)
        lnsd = view(52842, 4)
        gates2 = view(52846, 2, NT)
        dst_f = view(52856, 4, NT)
        tmp1 = view(52876, 20)
        token = view(52416, NT).bitcast(I32)
        dst_i = view(52896, 4, NT).bitcast(U32)
        count_i = view(52916, 1).bitcast(I32)
        block_tok = view(52920, N_BLOCK).bitcast(U32)
        page_ids = view(53000, 16).bitcast(I32)
        zeros_i = view(53016, N_BLOCK).bitcast(I32)

        bias_d = dram("bias_d", [20, P, RLEN])
        gates_d = dram("gates_d", [NS, 24])
        x1_d = dram("x1_d", [TOK, D])
        list_d = dram("list_d", [P * N_BLOCK, 1], I32)
        y_d = dram("y_d", [N_BLOCK * P, D])

        x_in = sems("x_in", NT)
        const_in = sem("const_in")
        early_in = sem("early_in")
        w_in = sems("w_in", WSLOTS)
        page_in = sems("page_in", 2)
        page_ids_in = sem("page_ids_in")
        filled = sem("filled")
        act_emptied, dve_emptied = sem("act_emptied"), sem("dve_emptied")
        zeroed = sem("zeroed")
        u_ready = sem("u_ready")
        bias_out = sem("bias_out")
        u_out = sem("u_out")
        stage_out = sems("stage_out", 3)
        v_out = sem("v_out")
        cmp_in, swapped = sem("cmp_in"), sem("swapped")
        dil_tables_in, nsa_tables_in = sem("dil_tables_in"), sem("nsa_tables_in")
        sample_tables_in = sem("sample_tables_in")
        gates_ready, gates_out, gates_in = sem("gates_ready"), sem("gates_out"), sem("gates_in")
        k_in, dil_v_in, nsa_v_in = sems("k_in", 3), sems("dil_v_in", NSEQ), sems("nsa_v_in", NSEQ)
        new_dil_v_in = [sem(name) for name in ("new_dil_v_in_0_to_3", "new_dil_v_in_4_5", "new_dil_v_in_6_7")]
        q_pad_zeroed = sem("q_pad_zeroed")
        q_put = sem("q_put")
        queries_zeroed = sem("queries_zeroed")
        queries_built = sem("queries_built")
        keys_kept = sem("keys_kept")
        new_keys_put = sem("new_keys_put")
        scored = sem("scored")
        score_read = sem("score_read")
        max_ready = sem("max_ready")
        exp_ready = sem("exp_ready")
        scaled = sem("scaled")
        turned = sem("turned")
        act_turned, dve_turned = sem("act_turned"), sem("dve_turned")
        summed = sem("summed")
        out_read = sem("out_read")
        conv_w_in, merge_w_in, w_out_in = sem("conv_w_in"), sem("merge_w_in"), sem("w_out_in")
        gate_w_in = sems("gate_w_in", 4)
        res_in, late_in, ple_in = sems("res_in", NT), sem("late_in"), sem("ple_in")
        later_filled = sem("later_filled")
        act_later, dve_later = sem("act_later"), sem("dve_later")
        var_ready, sqrt_ready = sem("var_ready"), sem("sqrt_ready")
        x1_ready, x1_stored = sem("x1_ready"), sems("x1_stored", NT)
        route_zeroed, chosen = sem("route_zeroed"), sem("chosen")
        indices_ready = sem("indices_ready")
        list_zeroed, listed, list_in = sem("list_zeroed"), sem("listed"), sem("list_in")
        diag_ready, weighed, added = sem("diag_ready"), sem("weighed"), sem("added")
        rstd_ready, normalized, gained = sem("rstd_ready"), sem("normalized"), sem("gained")
        ew_in = [sems(f"{w}_in", 2) for w in ("gate_w_e", "up_w_e", "down_w_e")]
        xg_in = sems("xg_in", 2)
        x_turned, gated_done, up_done, h_turned, down_done = (sem(s) for s in
            ("x_turned", "gated_done", "up_done", "h_turned", "down_done"))
        act_x, dve_x, silu_done, h_ready, hT_ready = (sem(s) for s in ("act_x", "dve_x", "silu_done", "h_ready", "hT_ready"))
        act_y, dve_y, y_stored = sem("act_y"), sem("dve_y"), sems("y_stored", 2)
        over = {name: sem("over_" + name) for name in
                ("w", "x", "x_turned", "act_x", "dve_x", "gated", "up", "silu", "h", "h_turned", "hT", "down",
                 "act_y", "dve_y", "stored", "list")}
        picked_in = sems("picked_in", NT)
        combined, last_combined, y_out = sem("combined"), sem("last_combined"), sem("y_out")
        dve_chain, act_chain, pool_chain = sem("dve_chain"), sem("act_chain"), sem("pool_chain")

        block = ctx.enter_context(nc.Block())

        def bank(n, b):
            return ps[:, 2 * (n % 4) + b, :]

        def pair(n):
            return ps[:, 2 * (n % 4):2 * (n % 4) + 2, :]

        def wait_emptied(eng, owner, n, act_sem, dve_sem):
            by_act, count = owner[n]
            eng.wait_ge(act_sem if by_act else dve_sem, count)

        def token_product(n, i, h, lhs, rhs, chunks):
            m = token_rows(i)
            w = rhs(0, h).shape[-1]
            return lambda k: nc.tensor.matmul(product_rows(n, i, h)[:, 0:w], lhs(k)[:, i * P:i * P + m], rhs(k, h),
                                              start=(k == 0), stop=(k == chunks - 1))

        def product_rows(n, i, h):
            return bank(n, h)[0:P] if i < QT else bank(n, h)[h * NS:(h + 1) * NS]

        def product_parts(n, i, rows):
            if i < QT:
                return [(rows.rearrange("p (h c) -> p h c", h=2), pair(n))]
            return [(rows[0:NS, 512 * h:512 * h + 512], product_rows(n, i, h)) for h in range(2)]

        def proj_emptied(eng, *task):
            wait_emptied(eng, p_owner, at[task], act_emptied, dve_emptied)

        def chained(eng, chain):
            count = [0]

            def link(ins):
                count[0] += 1
                ins.then_inc(chain, 1)
                eng.wait_ge(chain, count[0])
            return link

        x_p, x_s = A["x_prompt"][0], A["x_sample"].rearrange("n t d -> (n t) d")

        def x_rows(i):
            return x_p[i * P:(i + 1) * P, :] if i < QT else x_s

        def weights_of(kind, a):
            g, col = group_of(kind, a)
            w = GROUPS[g][1]
            slot = wslot[g % WSLOTS][:, 0:KC * w].rearrange("p (k c) -> p k c", k=KC)
            return lambda k: slot[:, k, col:col + P]

        kv_pool = A["cache_nsa_kv"][0].rearrange("n r k g d -> n r (k g d)")


        def bias_ap(head, start, *dims):
            return bass.AP(tensor=bias_d.tensor, offset=head * P * RLEN + start, ap=[list(d) for d in dims])

        caches = [A["cache_dil_w128"], A["cache_dil_w512"], A["cache_dil_w2048"], A["cache_nsa_win"]]

        def pair_pieces(kv, row, src):
            j, n = row // 2, src.shape[-1] // 2
            low, high = slice(0, DH), slice(DH, P)
            even, odd = slice(0, 2 * n, 2), slice(1, 2 * n, 2)
            for dst, rows, step in ((row_pairs[0], low, even), (swap, low, odd), (swap, high, even), (row_pairs[1], high, odd)):
                if kv is None:
                    yield dst[rows, :, j:j + n], src[rows, :, step]
                else:
                    yield dst[rows, kv, j:j + n], src[rows, step]

        def load_rows(eng, t, n, kv, dst, signal):
            src = caches[t][0, n].rearrange("r k h d -> r k (h d)")[:, kv]
            rows, w = src.shape
            o = (0, 256, 768, 256)[t]
            eng.dma_start(dst[:, o:o + rows // P * w].rearrange("p (a c) -> p a c", c=w),
                          src.rearrange("(a p) c -> p a c", p=P)).then_inc(signal, 16)

        def probs_of(u, s, a, w):
            o = first_column(UNITS[u], s) + a
            return (probs if u < N_PROMPT else sample_probs)[u % 3][:, o:o + w]

        def load_dil_values(eng, n):
            for t in range(3):
                load_rows(eng, t, n, 1, dil_v_cache[n], dil_v_in[n])

        def load_new_dil_values(eng, n):
            eng.dma_start(new_dil_v[n % 4][0:TNEW], vtok[n * TNEW:(n + 1) * TNEW, QT, 0:768]).then_inc(new_dil_v_in[max(0, n // 2 - 1)], 16)

        def turn_bank(f):
            return ps[:, 4 + f % 2, :]

        def fill_emptied(eng, kind, which, f):
            wait_emptied(eng, f_owner, fill_at[kind, which, f], act_turned, dve_turned)

        def proj_all_emptied(eng):
            eng.wait_ge(act_emptied, p_act)
            eng.wait_ge(dve_emptied, p_dve)

        def cache_key_rows(n, f):
            if f == 0:
                return cacheT[n % 4][:, 0:272].rearrange("p (r c) -> p r c", r=2)[:, :, 0:P]
            o = 272 + 528 * (f - 1)
            return cacheT[n % 4][:, o:o + 528].rearrange("p (r c) -> p r c", r=2)[:, :, 0:PAST]

        def later_emptied(eng, *task):
            wait_emptied(eng, l_owner, lat[task], act_later, dve_later)

        def halves(ap):
            return ap.rearrange("p (b c) -> p b c", b=2)

        sample_u = [uext_flat[:, c, 2 + SEQ:594].rearrange("p (s t) -> p s t", s=NSEQ) for c in range(4)]

        def copy_rows(eng, n, a):
            c, i = a
            m, w, dst = token_rows(i), GROUPS[4 + c][1], (768, 0, 384)[c]
            for h in range(1 if i < QT else 2):
                src = bank(n, 0)[0:m, 0:w] if i < QT else product_rows(n, i, h)[:, 0:w // 2]
                at_h = dst + w // 2 * h
                out = vtok[0:m, i, at_h:at_h + src.shape[-1]]
                last = nc.scalar.copy(out, src) if p_owner[n][0] else nc.vector.tensor_copy(out, src)
            return last

        def token_view(name):
            return O[name].rearrange("l n t k g d -> (l n t) (k g d)")

        def store_rows(eng, name, col, src, w):
            first = QT - O[name + "_prompt"].shape[2] // P
            dst = token_view(name + "_prompt").rearrange("(i p) c -> p i c", p=P)
            eng.dma_start(dst[:, :, col:col + w], vtok[:, first:QT, src:src + w]).then_inc(v_out, 16)
            eng.dma_start(token_view(name + "_sample")[:, col:col + w], vtok[0:NS, QT, src:src + w]).then_inc(v_out, 16)

        @block.sync
        def _(sp):
            for i in range(NT):
                sp.dma_start(xtok[0:token_rows(i), i, :], x_rows(i)).then_inc(x_in[i], 16)
                if i == 0:
                    sp.dma_start(ident, C["c_ident"]).then_inc(const_in, 16)

            def load_group(g):
                if g >= WSLOTS:
                    sp.wait_ge(filled, group_done[g - WSLOTS])
                c0, w = GROUPS[g]
                dst = wslot[g % WSLOTS][:, 0:KC * w].rearrange("p (k c) -> p k c", k=KC)
                src = A["w_in"][0, :, c0:c0 + w].rearrange("(k p) c -> p k c", p=P)
                if g < NSA_Q_GROUP:
                    sp.dma_start(dst, src).then_inc(w_in[g % WSLOTS], 16)
                    return
                for j in range(4):
                    for kv in range(2):
                        sp.dma_start(dst[:, :, P * j + DH * kv:P * j + DH * (kv + 1)],
                                     src[:, :, 256 * kv + DH * j:256 * kv + DH * (j + 1)]).then_inc(w_in[g % WSLOTS], 16)

            for dst, src in ((hot[0:33], C["c_hot"]), (rel[0:32], A["rel_bias"]), (rel[32:33], C["c_neg"]),
                             (state_tok[0:16], A["state_conv"][0].rearrange("n r c -> (n r) c")),
                             (pos_tok[0:64, 0:DH], A["cmp_pos"][0].rearrange("v l d -> (v l) d")),
                             (pos_tok[0:64, DH:P], A["cmp_pos"][0].rearrange("v l d -> (v l) d")),
                             (unseen, C["c_unseen"]), (ramp, C["c_ramp"]), (token, C["c_token"]),
                             (before, C["c_before"]), (state_tok[16:19], A["conv_w"][0])):
                sp.dma_start(dst, src).then_inc(early_in, 16)
            load_group(0)
            sp.dma_start(page_ids[0:1], A["page_table"].rearrange("n g -> (n g)").unsqueeze(0)).then_inc(page_ids_in, 16)
            load_group(1)
            load_group(2)
            sp.wait_ge(page_ids_in, 16)

            def load_page(s):
                if s >= 2:
                    sp.wait_ge(filled, at["page_T", s - 2] + 1)
                for g in range(2):
                    page = sp.value_load(page_ids[0:1, 2 * s + g:2 * s + g + 1], min_val=0,
                                         max_val=A["cache_nsa_kv"].shape[1] - 1)
                    src = kv_pool[bass.ds(page, 1), :, 0:256].rearrange("o p c -> (o p) c")
                    sp.dma_start(pages[s % 2][:, g, :], src).then_inc(page_in[s % 2], 16)

            for g in range(3, 7):
                load_group(g)
            load_page(0)
            load_page(1)
            for g in range(7, 10):
                load_group(g)
            for s in range(2, NSEQ):
                load_page(s)
            load_group(10)
            proj_emptied(sp, "page_T", NSEQ - 1)
            proj_emptied(sp, "cmp", 1)
            sp.dma_start(row_pairs[0][DH:P], swap[0:DH]).then_inc(swapped, 16)
            sp.dma_start(row_pairs[1][0:DH], swap[DH:P]).then_inc(swapped, 16)
            load_group(11)
            sp.wait_ge(filled, at["dil_k", 2] + 1)
            sp.dma_start(w1, A["cmp_w1"][0].rearrange("v (m p) h -> p v m h", p=P)).then_inc(cmp_in, 16)
            sp.wait_ge(dve_emptied, p_owner[at["conv_b", 3]][1])
            sp.dma_start(w2, A["cmp_w2"][0].rearrange("v h d -> h v d")).then_inc(cmp_in, 16)

            sp.wait_ge(filled, at["nsa_q", 3] + 1)
            sp.wait_ge(bias_out, 16 * 4)
            sp.dma_start(tab_dil0, bias_ap(0, 383, (RLEN - 1, P), (P * RLEN, 4), (1, 256))).then_inc(dil_tables_in, 16)
            for t in (1, 2):
                sp.dma_start(tab_dil[:, t - 1], bias_ap(4 * t, 127, (RLEN - 1, P), (P * RLEN, 4), (1, 512))).then_inc(dil_tables_in, 16)
            sp.wait_ge(filled, at["hidden", (1, 1)] + 1)
            sp.dma_start(tab_nsa, bias_ap(12, 127, (RLEN - 1, P), (P * RLEN, 8), (1, 512))).then_inc(nsa_tables_in, 16)

            def load_page_half(n, kv, dst, signal):
                for g in range(2):
                    page = sp.value_load(page_ids[0:1, 2 * n + g:2 * n + g + 1], min_val=0,
                                         max_val=A["cache_nsa_kv"].shape[1] - 1)
                    src = kv_pool[bass.ds(page, 1), :, 256 + P * kv:256 + P * (kv + 1)].rearrange("o p c -> (o p) c")
                    sp.dma_start(dst[:, P * g:P * (g + 1)], src).then_inc(signal, 16)

            def load_keys(n):
                if n >= 3:
                    sp.wait_ge(turned, fill_at["keys", n - 3, 3] + 1)
                keys = k_cache[n % 3]
                for t in range(3):
                    load_rows(sp, t, n, 0, keys, k_in[n % 3])
                load_rows(sp, 3, n, 0, keys[:, 1280:], k_in[n % 3])
                load_page_half(n, 0, keys[:, 1280:], k_in[n % 3])

            def load_nsa_values(n):
                load_rows(sp, 3, n, 1, nsa_v_cache[n], nsa_v_in[n])
                load_page_half(n, 1, nsa_v_cache[n], nsa_v_in[n])

            def load_new_nsa_values(n):
                for c, src in ((0, SEL_V), (P, WIN_V)):
                    sp.dma_start(new_nsa_v[n][0:TNEW, c:c + P], vtok[n * TNEW:(n + 1) * TNEW, QT, src:src + P])\
                      .then_inc(nsa_v_in[n], 16)

            for i in range(3):
                sp.wait_ge(stage_out[i], 96)
            load_keys(0)
            load_keys(1)
            sp.wait_ge(score_read, 3 * N_DIL)
            for n in range(4):
                sp.dma_start(tab_sdil[32 * n:32 * n + 32, 0:136], bias_ap(0, 383, (P * RLEN, 4), (RLEN - 1, TNEW), (1, 136)))\
                   .then_inc(sample_tables_in, 16)
                for t in (1, 2):
                    sp.dma_start(tab_sdil[32 * n:32 * n + 32, 136 + 264 * (t - 1):136 + 264 * t],
                                  bias_ap(4 * t, 255, (P * RLEN, 4), (RLEN - 1, TNEW), (1, 264))).then_inc(sample_tables_in, 16)
            for n in range(2):
                sp.dma_start(tab_snsa[64 * n:64 * n + 64], bias_ap(12, 255, (P * RLEN, 8), (RLEN - 1, TNEW), (1, 264)))\
                   .then_inc(sample_tables_in, 16)
            load_dil_values(sp, 0)
            load_dil_values(sp, 1)
            load_nsa_values(0)
            sp.wait_ge(scored, 3 * N_PROMPT)
            sp.wait_ge(turned, fill_at["probs", N_PROMPT - 3, len(key_tiles(UNITS[N_PROMPT - 3])) // 4] + 1)
            load_keys(2)
            load_keys(3)
            sp.wait_ge(score_read, 3 * N_PROMPT)
            sp.wait_ge(keys_kept, 1)
            for n in range(1, 4):
                load_nsa_values(n)
            for n in range(4):
                load_new_nsa_values(n)
            for n in range(4, 7):
                load_keys(n)
            sp.wait_ge(summed, N_PROMPT)
            load_nsa_values(4)
            load_keys(7)
            sp.wait_ge(summed, N_PROMPT + 1)
            load_dil_values(sp, 5)
            load_new_dil_values(sp, 4)
            load_new_dil_values(sp, 5)
            for n in range(5, NSEQ):
                load_nsa_values(n)
            for n in range(4, NSEQ):
                load_new_nsa_values(n)

            def load_gates(cc):
                for b in range(3):
                    c0 = MERGE0 + D * b + 256 * cc
                    sp.dma_start(gate_w[cc][:, :, b, :], A["w_in"][0, :, c0:c0 + 256].rearrange("(k p) c -> p k c", p=P))\
                      .then_inc(gate_w_in[cc], 16)

            sp.wait_ge(scored, 3 * (N_PROMPT + 4))
            sp.dma_start(w_conv, A["w_branch_conv"][0].rearrange("(k p) c -> p k c", p=P)).then_inc(conv_w_in, 16)
            sp.wait_ge(scored, 3 * len(UNITS))
            load_gates(0)
            sp.wait_ge(summed, len(UNITS))
            sp.wait_ge(dve_turned, f_dve)
            sp.dma_start(w_dil, A["w_branch_dil"][0].rearrange("(k p) c -> p k c", p=P)).then_inc(merge_w_in, 16)
            for g in range(2):
                sp.dma_start(w_nsa[g * DH:(g + 1) * DH], A["w_branch_nsa"][0, 256 * g:256 * g + 256, :]
                             .rearrange("(j d) c -> d j c", d=DH)).then_inc(merge_w_in, 16)
            load_gates(1)
            load_gates(2)
            sp.wait_ge(later_filled, lat["gate", (1, 2)] + 1)
            sp.dma_start(w_out, A["w_out"][0].rearrange("(k p) c -> p k c", p=P)).then_inc(w_out_in, 16)
            sp.wait_ge(later_filled, lat["gate", (3, 2)] + 1)
            load_gates(3)

            sp.wait_ge(later_filled, lat["branch", (KC - 1, 2)] + 1)
            later_emptied(sp, "branch", (KC - 1, 2))
            for i in range(NT):
                sp.dma_start(res[0:token_rows(i), i, :], x_rows(i)).then_inc(res_in[i], 16)
                if i == 0:
                    for k, name in enumerate(("ln1_g", "ln1_b", "ln2_g", "ln2_b")):
                        sp.dma_start(ln[:, k, :], A[name].partition_broadcast(P).rearrange("p o c -> p (o c)")).then_inc(late_in, 16)
            sp.dma_start(router_b, A["router_b"].unsqueeze(0).partition_broadcast(P).rearrange("p o c -> p (o c)")).then_inc(late_in, 16)
            sp.dma_start(router_w, A["router_w"].rearrange("(k p) e -> p k e", p=P)).then_inc(ple_in, 16)
            sp.dma_start(p_tok[:, 0:QT, :], A["p_prompt"][0, 0].rearrange("(i p) c -> p i c", p=P)).then_inc(ple_in, 16)
            sp.dma_start(p_tok[0:NS, QT, :], A["p_sample"][0].rearrange("n t c -> (n t) c")).then_inc(ple_in, 16)
            sp.dma_start(ple_w, A["ple_w_gate"][0].rearrange("(k p) c -> p k c", p=P)).then_inc(ple_in, 16)
            sp.dma_start(ple_p, A["ple_w_proj"][0].rearrange("(k p) c -> p k c", p=P)).then_inc(ple_in, 16)

            names = ("expert_w_gate", "expert_w_up", "expert_w_down")

            def load_expert_weights(q, s, j):
                if not (isinstance(q, int) and q == 0):
                    sp.wait_ge((gated_done, up_done, down_done)[j], 2 * q + s - 1)
                src = A[names[j]][0][bass.ds(2 * q + s, 1)].rearrange("o (k p) c -> p (o k) c", p=P)
                dst = ew[s][j].rearrange("p (k c) -> p k c", k=src.shape[1])
                sp.dma_start(dst, src).then_inc(ew_in[j][s], 16)

            sp.wait_ge(later_filled, lat["mix", NT - 1] + 1)
            for j in range(3):
                load_expert_weights(0, 0, j)
            sp.wait_ge(later_filled, len(later))
            sp.wait_ge(dve_later, l_dve)
            sp.wait_ge(indices_ready, 1)
            for j in range(3):
                load_expert_weights(0, 1, j)
            load_expert_weights(1, 0, 0)
            load_expert_weights(1, 0, 1)
            load_expert_weights(1, 1, 0)
            load_expert_weights(1, 1, 1)
            load_expert_weights(1, 0, 2)
            with sp.Fori(2, N_EXP // 2) as q:
                load_expert_weights(q, 0, 0)
                load_expert_weights(q, 0, 1)
                load_expert_weights(q - 1, 1, 2)
                load_expert_weights(q, 1, 0)
                load_expert_weights(q, 1, 1)
                load_expert_weights(q, 0, 2)
            load_expert_weights(N_EXP // 2 - 1, 1, 2)

            most = sp.value_load(count_i[0:1, :], min_val=0, max_val=TOK)
            with sp.If(most > P):
                sp.wait_ge(down_done, N_EXP)
                with sp.Fori(1, N_BLOCK - N_EXP + 1) as b:
                    sp.wait_ge(over["down"], b)
                    for j, name in enumerate(names):
                        src = A[name][0][bass.ds((b + N_EXP - 1) % N_EXP, 1)].rearrange("o (k p) c -> p (o k) c", p=P)
                        sp.dma_start(ew[0][j].rearrange("p (k c) -> p k c", k=src.shape[1]), src).then_inc(over["w"], 16)

            for i in range(NT):
                if i < NT - 1:
                    sp.wait_ge(combined, i + 1)
                else:
                    sp.wait_ge(last_combined, 1)
                dst = O["y_prompt"][0, i * P:(i + 1) * P, :] if i < QT else O["y_sample"].rearrange("n t d -> (n t) d")
                sp.dma_start(dst, res[0:token_rows(i), i, :]).then_inc(y_out, 16)
            sp.wait_ge(y_out, 16 * NT)


        @block.tensor
        def _(pe):
            def feature_major(n, lhs, chunks, rhs):
                for b in range(2):
                    for k in range(chunks):
                        mm = nc.tensor.matmul(bank(n, b)[:, 0:HALF], lhs(k), rhs[:, k, b * HALF:(b + 1) * HALF],
                                              start=(k == 0), stop=(k == chunks - 1))
                return mm

            def two_halves(n, i, lhs, rhs, chunks):
                part = [token_product(n, i, h, lhs, rhs, chunks) for h in range(2)]
                for h, k in [(h, k) for h in range(2) for k in range(chunks)] if i < QT else \
                        [(h, k) for k in range(chunks) for h in range(2)]:
                    mm = part[h](k)
                return mm

            pe.wait_ge(const_in, 16)
            for n, (kind, a) in enumerate(proj):
                if n >= 4:
                    wait_emptied(pe, p_owner, n - 4, act_emptied, dve_emptied)
                if kind in FEATURE or kind == "rows":
                    g = group_of(kind, a)[0]
                    pe.wait_ge(w_in[g % WSLOTS], 16 * (g // WSLOTS + 1 + 7 * (g == NSA_Q_GROUP)))
                if kind == "x_T":
                    i, h = a
                    pe.wait_ge(x_in[i], 16)
                    m = token_rows(i)
                    for k in range(4):
                        mm = nc.tensor.transpose(bank(n, 0)[:, k * m:(k + 1) * m],
                                                 xtok[0:m, i, (4 * h + k) * P:(4 * h + k + 1) * P], ident[0:m, 0:m])
                elif kind == "bias_row":
                    pe.wait_ge(early_in, 16 * 11)
                    for h in range(2):
                        mm = nc.tensor.matmul(bank(n, h)[0:20, 0:320], rel[0:33], hot[0:33, a, 320 * h:320 * h + 320],
                                              start=True, stop=True)
                elif kind == "state_T":
                    for c in range(4):
                        mm = nc.tensor.transpose(bank(n, 0)[:, 19 * c:19 * c + 19], state_tok[0:19, c * P:(c + 1) * P],
                                                 ident[0:19, 0:19])
                elif kind == "pos_T":
                    mm = nc.tensor.transpose(bank(n, 0)[:, 0:64], pos_tok[0:64], ident[0:64, 0:64])
                elif kind in FEATURE:
                    if n == at["conv_c", 0]:
                        for h in range(2):
                            proj_emptied(pe, "x_T", (NT - 1, h))
                    mm = feature_major(n, weights_of(kind, a), KC, xT)
                elif kind == "rows":
                    c, i = a
                    w = GROUPS[4 + c][1]
                    m = token_rows(i)
                    slot = wslot[(4 + c) % WSLOTS][:, 0:KC * w].rearrange("p (k c) -> p k c", k=KC)
                    if i < QT:
                        for k in range(KC):
                            mm = nc.tensor.matmul(bank(n, 0)[0:m, 0:w], xT[:, k, i * P:i * P + m], slot[:, k, :],
                                                  start=(k == 0), stop=(k == KC - 1))
                    else:
                        mm = two_halves(n, i, lambda k: xT[:, k], lambda k, h: slot[:, k, w // 2 * h:w // 2 * (h + 1)], KC)
                elif kind == "u_T":
                    pe.wait_ge(u_ready, 1)
                    for c in range(4):
                        mm = nc.tensor.transpose(bank(n, 0)[0:18, c * P:(c + 1) * P], u_last[:, c, :], ident)
                elif kind == "win_k_T":
                    for i in range(NT):
                        proj_emptied(pe, "rows", (0, i))
                    for i in range(NT):
                        m = token_rows(i)
                        dst = bank(n, 0)[:, i * P:(i + 1) * P] if i < QT else bank(n, 1)[:, 0:m]
                        mm = nc.tensor.transpose(dst, vtok[0:m, i, WIN_K:WIN_K + P], ident[0:m, 0:m])
                elif kind == "page_T":
                    pe.wait_ge(page_in[a % 2], 32 * (a // 2 + 1))
                    for kv in range(2):
                        for g in range(2):
                            mm = nc.tensor.transpose(bank(n, 0)[:, (2 * kv + g) * P:(2 * kv + g + 1) * P],
                                                     pages[a % 2][:, g, kv * P:(kv + 1) * P], ident)
                elif kind == "k_rows":
                    proj_emptied(pe, *(("dil_k", a) if a < 6 else ("cmp", (2, 0, 1)[a - 6])))
                    for i in range(NT):
                        src = kT[:, a] if a < 7 else cmp_rows[:, a - 7]
                        m = token_rows(i)
                        dst = bank(n, 0)[:, i * P:(i + 1) * P] if i < QT else bank(n, 1)[0:m, 0:P]
                        mm = nc.tensor.transpose(dst, src[:, i * P:i * P + m], ident)
                elif kind == "hidden":
                    kv, g = a
                    if a == (0, 0):
                        pe.wait_ge(cmp_in, 16 * 2)
                        pe.wait_ge(swapped, 32)
                        proj_emptied(pe, "cmp", 1)
                        proj_emptied(pe, "page_T", NSEQ - 1)
                    step = CMP_STRIDE // 2
                    for l in range(CMP_BLOCK // 2):
                        mm = nc.tensor.matmul(bank(n, 0)[:, 0:NCMP + 1], w1[:, kv, l, :],
                                              row_pairs[g][:, kv, l:l + step * NCMP + 1:step],
                                              start=(l == 0), stop=(l == CMP_BLOCK // 2 - 1))
                elif kind == "cmp_k_T":
                    for g in range(2):
                        proj_emptied(pe, "hidden", (0, g))
                        mm = nc.tensor.matmul(bank(n, 0)[g * DH:(g + 1) * DH, 0:NCMP - 1], w2[:, 0, :],
                                              hidden[:, g, 0:NCMP - 1], start=True, stop=True)
                elif kind == "cmp_v":
                    for g in range(2):
                        proj_emptied(pe, "hidden", (1, g))
                        h = hidden[:, 2 + g]
                        if a == 0:
                            mm = nc.tensor.matmul(bank(n, 0)[0:PROMPT_CMP, g * DH:(g + 1) * DH], h[:, 0:PROMPT_CMP],
                                                  w2[:, 1, :], start=True, stop=True)
                            continue
                        for s in range(NSEQ):
                            c0 = (SEQ + PAST * s) // CMP_STRIDE
                            mm = nc.tensor.matmul(bank(n, s // 4)[0:SAMPLE_CMP, s % 4 * P + g * DH:s % 4 * P + (g + 1) * DH],
                                                  h[:, c0:c0 + SAMPLE_CMP], w2[:, 1, :], start=True, stop=True)
                mm.then_inc(filled, 1)

            proj_all_emptied(pe)

            def scores(u):
                kind, h, qt = UNITS[u]
                widths = segments(UNITS[u])
                if kind == "sdil":
                    half = h
                    for n in range(4 * half, 4 * half + 4):
                        fill_emptied(pe, "keys", n, 3)
                    pe.wait_ge(new_keys_put, 4 * (half + 1))
                if u < N_PROMPT:
                    pe.wait_ge(q_put, u + 1)
                for s, w in enumerate(widths):
                    seg = 3 * u + s
                    if seg >= 4:
                        pe.wait_ge(score_read, seg - 3)
                    dst = ps[:, seg % 4, :]
                    if kind == "dil":
                        end = (qt + 1) * P
                        mm = nc.tensor.matmul(dst[:, 0:w], q_pad[h % 2][:, s, :], kT[:, 2 * s + h // 2, end - w:end],
                                              start=True, stop=True)
                    elif kind == "nsa":
                        g, j = h
                        keys = kcT[:, 0:w] if s == 0 else kT[:, 5 + s, 0:w]
                        mm = nc.tensor.matmul(dst[:, 0:w], q_pad[g][:, 0, :], keys, start=True, stop=True)
                    elif kind == "sdil":
                        o = 272 + 528 * (s - 1) if s else 0
                        for pr in range(2):
                            for n in range(4):
                                mm = nc.tensor.matmul(dst[32 * n:32 * n + 32, 0:w], q_dil[:, 2 * s + pr, 4 * half + n, :],
                                                      cacheT[n][:, o + pr * w:o + (pr + 1) * w],
                                                      start=(pr == 0), stop=(pr == 1))
                    else:
                        for n2 in range(2):
                            n = 2 * h + n2
                            c0 = (SEQ + PAST * n) // CMP_STRIDE
                            o = 1328 + 264 * (s - 1)
                            keys = kcT[:, c0:c0 + w] if s == 0 else cacheT[n % 4][:, o:o + w]
                            mm = nc.tensor.matmul(dst[64 * n2:64 * n2 + 64, 0:w], q_nsa[:, n, :], keys,
                                                  start=True, stop=True)
                    mm.then_inc(scored, 1)

            def turn(u):
                pe.wait_ge(scaled, u + 1)
                tiles = key_tiles(UNITS[u])
                for f in range((len(tiles) + 3) // 4):
                    n = fill_at["probs", u, f]
                    if n >= 2:
                        wait_emptied(pe, f_owner, n - 2, act_turned, dve_turned)
                    for x, (s, a, w) in enumerate(tiles[4 * f:4 * f + 4]):
                        mm = nc.tensor.transpose(turn_bank(n)[0:w, x * P:(x + 1) * P],
                                                 probs_of(u, s, a, w), ident)
                    mm.then_inc(turned, 1)

            def turn_keys(n):
                pe.wait_ge(k_in[n % 3], 96 * (n // 3 + 1))
                keys = k_cache[n % 3]
                for f in range(4):
                    m = fill_at["keys", n, f]
                    wait_emptied(pe, f_owner, m - 2, act_turned, dve_turned)
                    if f == 0:
                        cols = [P * pr for pr in range(2)]
                    elif f < 3:
                        cols = [512 * f - 256 + 256 * a + P * pr for pr in range(2) for a in range(2)]
                    else:
                        cols = [1280 + P * x for x in range(4)]
                    for x, c in enumerate(cols):
                        mm = nc.tensor.transpose(turn_bank(m)[:, x * P:(x + 1) * P], keys[:, c:c + P], ident)
                    mm.then_inc(turned, 1)

            def sums(u):
                kind, h, qt = UNITS[u]
                tiles = key_tiles(UNITS[u])
                fill_emptied(pe, "probs", u, (len(tiles) - 1) // 4)
                if u >= 2:
                    pe.wait_ge(out_read, u - 1)
                dst = ps[:, 6 + u % 2, :]
                pT_u = probsT[u % 2]
                first, final = 0, len(tiles) - 1
                if kind in ("dil", "nsa"):
                    r0 = h % 2 * DH if kind == "dil" else h[0] * DH
                    start = (qt + 1) * P - segments(UNITS[u])[0]
                    for x, (s, a, w) in enumerate(tiles):
                        if kind == "dil":
                            key = a + (start if s == 0 else 0)
                            vals = vtok[:, key // P, s * 256 + h * DH:s * 256 + h * DH + DH]
                        elif s == 0:
                            vals = vcp[0:w, h[0] * DH:h[0] * DH + DH]
                        else:
                            c = (SEL_V, WIN_V)[s - 1] + h[0] * DH
                            vals = vtok[:, a // P, c:c + DH]
                        mm = nc.tensor.matmul(dst[r0:r0 + DH, 0:P], vals, pT_u[0:w, x, :],
                                              start=(x == first), stop=(x == final))
                elif kind == "sdil":
                    for i, count in ((0, 64),) if h == 0 else ((1, 32), (2, 32)):
                        pe.wait_ge(new_dil_v_in[i], count)
                    for n in range(4):
                        pe.wait_ge(dil_v_in[4 * h + n], 48)
                    for x, (s, a, w) in enumerate(tiles):
                        for n in range(4):
                            if w == TNEW:
                                vals = new_dil_v[n][0:w, s * 256:(s + 1) * 256]
                            else:
                                o = (0, 256, 768)[s] + 2 * a
                                vals = dil_v_cache[4 * h + n][:, o:o + 256]
                            mm = nc.tensor.matmul(dst[32 * n:32 * n + 32, 0:256], pT_u[0:w, x, 32 * n:32 * n + 32], vals,
                                                  start=(x == first), stop=(x == final))
                else:
                    for n2 in range(2):
                        n = 2 * h + n2
                        pe.wait_ge(nsa_v_in[n], 80)
                        for x, (s, a, w) in enumerate(tiles):
                            if s == 0:
                                vals = vcs[0:w, n, :]
                            elif w == TNEW:
                                vals = new_nsa_v[n][0:w, P * (s - 1):P * s]
                            else:
                                o = 256 * (s - 1) + a
                                vals = nsa_v_cache[n][:, o:o + P]
                            mm = nc.tensor.matmul(dst[:, 64 * n2:64 * n2 + 64], vals,
                                                  pT_u[0:w, x, 64 * n2:64 * n2 + 64], start=(x == first), stop=(x == final))
                mm.then_inc(summed, 1)

            def turn_sums(u):
                m = fill_at["sums", u, 0]
                wait_emptied(pe, f_owner, m - 2, act_turned, dve_turned)
                pe.wait_ge(out_read, u + 1)
                for pr in range(2):
                    mm = nc.tensor.transpose(turn_bank(m)[:, pr * P:(pr + 1) * P], sum_rows[:, pr * P:(pr + 1) * P], ident)
                mm.then_inc(turned, 1)

            for u in range(len(UNITS) + 3):
                if u == N_PROMPT:
                    pe.wait_ge(queries_built, 1)
                if u < len(UNITS) and not begins_half(u):
                    scores(u)
                if 2 <= u < len(UNITS) + 2:
                    turn(u - 2)
                if u >= 3:
                    sums(u - 3)
                if begins_half(u):
                    for n in range(4 * UNITS[u][1], 4 * UNITS[u][1] + 4):
                        turn_keys(n)
                    scores(u)
                if u >= 4 and UNITS[u - 4][0] == "sdil":
                    turn_sums(u - 4)

            pe.wait_ge(out_read, len(UNITS))
            pe.wait_ge(dve_turned, f_dve)
            for n, (kind, a) in enumerate(later):
                if n >= 4:
                    wait_emptied(pe, l_owner, n - 4, act_later, dve_later)
                if kind == "gate":
                    c, b = a
                    pe.wait_ge(gate_w_in[c // 2], 48)
                    w = gate_w[c // 2]
                    mm = feature_major(n, lambda k: w[:, k, b, c % 2 * P:(c % 2 + 1) * P], KC, xT)
                elif kind == "branch":
                    c, b = a
                    if b == 0:
                        pe.wait_ge(conv_w_in, 16)
                    else:
                        pe.wait_ge(merge_w_in, 48)
                    w, y = ((w_conv, yconvT), (w_dil, ydilT), (w_nsa, ynsaT))[b]
                    mm = feature_major(n, lambda k: w[:, k, c * P:(c + 1) * P], (4, 2, 4)[b], y)
                elif kind == "mix":
                    pe.wait_ge(w_out_in, 16)
                    if a == 0:
                        later_emptied(pe, "branch", (KC - 1, 2))
                    mm = two_halves(n, a, lambda k: mT[:, k], lambda k, h: w_out[:, k, 512 * h:512 * h + 512], KC)
                elif kind == "x1_T":
                    i, h = a
                    pe.wait_ge(x1_ready, i + 1)
                    m = token_rows(i)
                    for k in range(4):
                        mm = nc.tensor.transpose(bank(n, 0)[:, k * m:(k + 1) * m],
                                                 res[0:m, i, (4 * h + k) * P:(4 * h + k + 1) * P], ident[0:m, 0:m])
                elif kind == "router":
                    for h in range(2):
                        later_emptied(pe, "x1_T", (NT - 1, h))
                    for i in range(NT):
                        m = token_rows(i)
                        for k in range(KC):
                            mm = nc.tensor.matmul(bank(n, 0)[0:m, 16 * i:16 * i + 16], x1T[:, k, i * P:i * P + m],
                                                  router_w[:, k, :], start=(k == 0), stop=(k == KC - 1))
                elif kind == "p_T":
                    pe.wait_ge(ple_in, 80)
                    m = token_rows(a)
                    for k in range(2):
                        mm = nc.tensor.transpose(bank(n, 0)[:, k * m:(k + 1) * m], p_tok[0:m, a, k * P:(k + 1) * P],
                                                 ident[0:m, 0:m])
                elif kind in ("ple_gate", "ple_proj"):
                    gate = kind == "ple_gate"
                    if not gate and a == 0:
                        later_emptied(pe, "p_T", NT - 1)
                    lhs, w, chunks = (x1T, ple_w, KC) if gate else (pT, ple_p, 2)
                    mm = two_halves(n, a, lambda k: lhs[:, k], lambda k, h: w[:, k, 512 * h:512 * h + 512], chunks)
                elif kind == "rank":
                    pe.wait_ge(chosen, 1)
                    for i in range(NT):
                        for x in range(i + 1):
                            mm = nc.tensor.matmul(bank(n, 0)[:, 16 * i:16 * i + 16], before if x == i else ones,
                                                  routing(5)[:, x, :], start=(x == 0), stop=(x == i))
                    for i in range(NT):
                        mm = nc.tensor.matmul(bank(n, 1)[:, 0:16], ones, routing(5)[:, i, :], start=(i == 0), stop=(i == NT - 1))
                mm.then_inc(later_filled, 1)

            pe.wait_ge(act_later, l_act)
            pe.wait_ge(dve_later, l_dve)

            def turn_x(rows):
                for k in range(KC):
                    mm = nc.tensor.transpose(ps[:, k // 4, k % 4 * P:(k % 4 + 1) * P], rows[:, k * P:(k + 1) * P], ident)
                return mm

            def up_product(s, j):
                w = ew[s][j].rearrange("p (k c) -> p k c", k=KC)
                for k in range(KC):
                    mm = nc.tensor.matmul(ps[:, 2 + j, :], xgT[s][:, k, :], w[:, k, :], start=(k == 0), stop=(k == KC - 1))
                return mm

            def turn_h():
                for k in range(4):
                    mm = nc.tensor.transpose(ps[:, 4, k * P:(k + 1) * P], h_tok[:, k * P:(k + 1) * P], ident)
                return mm

            def down_product(s):
                w = ew[s][2].rearrange("p (k c) -> p k c", k=4)
                for h in range(2):
                    for k in range(4):
                        mm = nc.tensor.matmul(ps[:, 5 + h, :], hT[:, k, :], w[:, k, 512 * h:512 * h + 512],
                                              start=(k == 0), stop=(k == 3))
                return mm

            def finish_expert(q, s):
                e = 2 * q + s
                first = isinstance(q, int) and q == 0 and s == 0
                pe.wait_ge(hT_ready, e + 1)
                pe.wait_ge(ew_in[2][s], 16 * q + 16)
                if not first:
                    pe.wait_ge(act_y, e)
                    pe.wait_ge(dve_y, e)
                down_product(s).then_inc(down_done, 1)

            def turn_hidden(q, s):
                e = 2 * q + s
                pe.wait_ge(h_ready, e + 1)
                if not (isinstance(q, int) and q == 0 and s == 0):
                    pe.wait_ge(hT_ready, e)
                turn_h().then_inc(h_turned, 1)

            def expert_step(q, s, last=False):
                e = 2 * q + s
                first = isinstance(q, int) and q == 0 and s == 0
                pq, p_s = (q, 0) if s else (q - 1, 1)
                pe.wait_ge(ew_in[0][s], 16 * q + 16)
                pe.wait_ge(act_x, e + 1)
                pe.wait_ge(dve_x, e + 1)
                if not first:
                    pe.wait_ge(silu_done, e)
                up_product(s, 0).then_inc(gated_done, 1)
                if not first:
                    turn_hidden(pq, p_s)
                pe.wait_ge(ew_in[1][s], 16 * q + 16)
                up_product(s, 1).then_inc(up_done, 1)
                if not last:
                    nq = q + s
                    pe.wait_ge(xg_in[1 - s], 16 * nq + 16)
                    turn_x(xg[1 - s]).then_inc(x_turned, 1)
                if not first:
                    finish_expert(pq, p_s)

            pe.wait_ge(xg_in[0], 16)
            turn_x(xg_first).then_inc(x_turned, 1)
            expert_step(0, 0)
            expert_step(0, 1)
            with pe.Fori(1, N_EXP // 2 - 1) as q:
                expert_step(q, 0)
                expert_step(q, 1)
            expert_step(N_EXP // 2 - 1, 0)
            expert_step(N_EXP // 2 - 1, 1, last=True)
            turn_hidden(N_EXP // 2 - 1, 1)
            finish_expert(N_EXP // 2 - 1, 1)

            most = pe.value_load(count_i[0:1, :], min_val=0, max_val=TOK)
            with pe.If(most > P):
                pe.wait_ge(act_y, N_EXP)
                pe.wait_ge(dve_y, N_EXP)
                pe.nop().then_inc(over["down"], 1)
                with pe.Fori(1, N_BLOCK - N_EXP + 1) as b:
                    pe.wait_ge(over["x"], 16 * b)
                    turn_x(xg[0]).then_inc(over["x_turned"], 1)
                    pe.wait_ge(over["act_x"], b)
                    pe.wait_ge(over["dve_x"], b)
                    pe.wait_ge(over["w"], 48 * b)
                    up_product(0, 0).then_inc(over["gated"], 1)
                    up_product(0, 1).then_inc(over["up"], 1)
                    pe.wait_ge(over["h"], b)
                    turn_h().then_inc(over["h_turned"], 1)
                    pe.wait_ge(over["hT"], b)
                    down_product(0).then_inc(over["down"], 1)

            pe.wait_ge(diag_ready, 1)
            for i in range(NT):
                m = token_rows(i)
                pe.wait_ge(picked_in[i], 32)
                if i >= 4:
                    pe.wait_ge(added, i - 3)
                for h in range(2):
                    for j in range(2):
                        mm = nc.tensor.matmul(bank(i, h)[0:m, :], gate_diag[0:m, j, i, 0:m],
                                              picked[i][j][0:m, 512 * h:512 * h + 512], start=(j == 0), stop=(j == 1))
                mm.then_inc(weighed, 1)


        @block.scalar
        def _(act):
            link = chained(act, act_chain)
            for n, (kind, a) in enumerate(proj):
                if not p_owner[n][0]:
                    continue
                act.wait_ge(filled, n + 1)
                if kind == "x_T":
                    i, h = a
                    m = token_rows(i)
                    src = bank(n, 0)[:, 0:4 * m].rearrange("p (k t) -> p k t", k=4)
                    last = nc.scalar.copy(xT[:, 4 * h:4 * h + 4, i * P:i * P + m], src)
                elif kind == "conv_c":
                    last = nc.scalar.copy(halves(conv_tmp[:, a]), pair(n)[:, :, 0:HALF])
                elif kind == "u_T":
                    last = nc.scalar.copy(u_rows[0:18], bank(n, 0)[0:18, :])
                elif kind == "cmp":
                    if a == 0:
                        act.wait_ge(filled, at["x_T", (NT - 1, 1)] + 1)
                        act.wait_ge(dve_emptied, p_owner[at["conv_b", 3]][1])
                    link(nc.scalar.copy(halves(cmp_rows[:, a]), pair(n)[:, :, 0:HALF]))
                    for dst, src in pair_pieces(a, 0, cmp_rows[:, a, 0:SEQ]):
                        last = nc.scalar.copy(dst, src)
                elif kind == "rows":
                    if a == (0, 1):
                        act.wait_ge(bias_out, 16 * 4)
                    last = copy_rows(act, n, a)
                elif kind in ("dil_q", "nsa_q"):
                    c = a + (6 if kind == "nsa_q" else 0)
                    last = nc.scalar.mul(halves(qT[:, c]), pair(n)[:, :, 0:HALF], SCALE)
                elif kind == "dil_k":
                    last = nc.scalar.copy(halves(kT[:, a]), pair(n)[:, :, 0:HALF])
                elif kind == "hidden":
                    kv, g = a
                    if a == (0, 0):
                        act.wait_ge(dve_emptied, p_owner[at["conv_b", 3]][1])
                    b = gelu_b[:, 2 * kv + g:2 * kv + g + 1]
                    link(nc.scalar.copy(b, bank(n, 0)[:, NCMP:NCMP + 1]))
                    last = nc.scalar.activation(hidden[:, 2 * kv + g, 0:NCMP - 1], bank(n, 0)[:, 0:NCMP - 1],
                                                ACT.Gelu_apprx_tanh, bias=b)
                last.then_inc(act_emptied, 1)

            def put_queries(u):
                kind, h, qt = UNITS[u]
                r = h % 2 if kind == "dil" else h[0]
                rows = slice(r * DH, r * DH + DH)
                cols = slice(qt * P, qt * P + P)
                if kind == "dil":
                    last = nc.scalar.copy(q_pad[r][rows], qT[rows, h // 2:6:2, cols])
                else:
                    last = nc.scalar.copy(q_pad[r][rows, 0, :], qT[rows, 6 + h[1], cols])
                last.then_inc(q_put, 1)

            act.wait_ge(q_pad_zeroed, 1)
            proj_emptied(act, "nsa_q", 2)
            put_queries(0)
            put_queries(1)
            proj_all_emptied(act)
            nc.scalar.activation(nsa_gate[:, 0:QT, :], vtok[:, 0:QT, GATES:VW], ACT.Sigmoid)
            nc.scalar.activation(nsa_gate[0:NS, QT, :].rearrange("p (h b) -> p b h", b=3),
                                 vtok[0:NS, QT, GATES:VW].rearrange("p (b h) -> p b h", b=3),
                                 ACT.Sigmoid).then_inc(gates_ready, 1)

            def build_queries():
                act.wait_ge(queries_zeroed, 1)
                for t in range(3):
                    for pr in range(2):
                        for x in range(2):
                            rows = slice(x * DH, x * DH + DH)
                            dst = q_dil[rows, 2 * t + pr].rearrange("p n (h t) -> p n h t", h=4)[:, :, 2 * pr + x, :]
                            nc.scalar.copy(dst, qT[rows, 2 * t + pr, SEQ:TOK].rearrange("p (n t) -> p n t", n=NSEQ))
                for g in range(2):
                    rows = slice(g * DH, g * DH + DH)
                    dst = q_nsa[rows].rearrange("p n (g j t) -> p g j n t", g=2, j=4)[:, g]
                    for j in range(4):
                        last = nc.scalar.copy(dst[:, j], qT[rows, 6 + j, SEQ:TOK].rearrange("p (n t) -> p n t", n=NSEQ))
                last.then_inc(queries_built, 1)

            def exponentials(u):
                act.wait_ge(max_ready, u + 1)
                joint = UNITS[u][0] in ("dil", "sdil")
                _, neg_max, total, _ = stat[u % 2]
                for s, w in enumerate([sum(segments(UNITS[u]))] if joint else segments(UNITS[u])):
                    seg = probs_of(u, s, 0, w)
                    last = nc.scalar.activation(seg, seg, ACT.Exp, bias=neg_max[:, s:s + 1], accum_out=total[:, s:s + 1])
                last.then_inc(exp_ready, 1)

            def take_turned(u):
                tiles = key_tiles(UNITS[u])
                for f in range((len(tiles) + 3) // 4):
                    n = fill_at["probs", u, f]
                    act.wait_ge(turned, n + 1)
                    if u >= 2:
                        act.wait_ge(summed, u - 1)
                    part = tiles[4 * f:4 * f + 4]
                    x = 0
                    while x < len(part):
                        y = x
                        while y < len(part) and part[y][2] == part[x][2]:
                            y += 1
                        w = part[x][2]
                        last = nc.scalar.copy(probsT[u % 2][0:w, 4 * f + x:4 * f + y, :],
                                              turn_bank(n)[0:w, x * P:y * P].rearrange("p (a q) -> p a q", q=P))
                        x = y
                    last.then_inc(act_turned, 1)

            for u in range(len(UNITS) + 2):
                if u == 2:
                    build_queries()
                if u >= 2:
                    take_turned(u - 2)
                if u < len(UNITS):
                    exponentials(u)
                if u + 2 < N_PROMPT:
                    put_queries(u + 2)

            def root(i):
                act.wait_ge(var_ready, i + 1)
                m = token_rows(i % NT)
                nc.scalar.activation(lnsd[0:m, 1:2], lnsd[0:m, 0:1], ACT.Sqrt).then_inc(sqrt_ready, 1)

            for n, (kind, a) in enumerate(later):
                if kind == "mix":
                    root(a)
                    continue
                if not l_owner[n][0]:
                    continue
                act.wait_ge(later_filled, n + 1)
                if kind == "gate":
                    c, b = a
                    x = 3 * c + b
                    if x == 0:
                        act.wait_ge(scored, 3 * len(UNITS))
                    if x >= 2:
                        act.wait_ge(dve_later, l_owner[lat["branch", ((x - 2) // 3, (x - 2) % 3)]][1])
                    last = nc.scalar.activation(halves(sig[x % 2]), pair(n)[:, :, 0:HALF], ACT.Sigmoid)
                elif kind == "x1_T":
                    i, h = a
                    m = token_rows(i)
                    src = bank(n, 0)[:, 0:4 * m].rearrange("p (k t) -> p k t", k=4)
                    last = nc.scalar.copy(x1T[:, 4 * h:4 * h + 4, i * P:i * P + m], src)
                elif kind == "p_T":
                    m = token_rows(a)
                    last = nc.scalar.copy(pT[:, :, a * P:a * P + m], bank(n, 0)[:, 0:2 * m].rearrange("p (k t) -> p k t", k=2))
                elif kind == "router":
                    act.wait_ge(route_zeroed, 1)
                    src = bank(n, 0)[:, 0:16 * NT].rearrange("p (i e) -> p i e", e=16)
                    nc.scalar.activation(routing(0)[:, 0:QT, :], src[:, 0:QT, :], ACT.Sigmoid)
                    last = nc.scalar.activation(routing(0)[0:NS, QT, :], src[0:NS, QT, :], ACT.Sigmoid)
                elif kind == "ple_gate":
                    if a >= 2:
                        act.wait_ge(dve_later, l_owner[lat["ple_proj", a - 2]][1])
                    for out, product in product_parts(n, a, ple_sig[a % 2]):
                        last = nc.scalar.activation(out, product, ACT.Sigmoid)
                last.then_inc(act_later, 1)

            def take_x(s):
                return nc.scalar.copy(xgT[s][:, 0:4, :], ps[:, 0, :].rearrange("p (k t) -> p k t", k=4))

            def take_y(s):
                return nc.scalar.copy(y_exp[s][:, 0:512], ps[:, 5, :])

            def expert_step(q, s, last=False):
                e = 2 * q + s
                first = isinstance(q, int) and q == 0 and s == 0
                act.wait_ge(gated_done, e + 1)
                if not first:
                    act.wait_ge(h_ready, e)
                nc.scalar.activation(silu, ps[:, 2, :], ACT.Silu).then_inc(silu_done, 1)
                if not last:
                    act.wait_ge(x_turned, e + 2)
                    if not first:
                        act.wait_ge(up_done, e)
                    take_x(1 - s).then_inc(act_x, 1)
                if not first:
                    finish_expert(*((q, 0) if s else (q - 1, 1)))

            def finish_expert(q, s):
                act.wait_ge(down_done, 2 * q + s + 1)
                if not (isinstance(q, int) and q == 0):
                    act.wait_ge(y_stored[s], 16 * q)
                take_y(s).then_inc(act_y, 1)

            act.wait_ge(x_turned, 1)
            take_x(0).then_inc(act_x, 1)
            expert_step(0, 0)
            expert_step(0, 1)
            with act.Fori(1, N_EXP // 2 - 1) as q:
                expert_step(q, 0)
                expert_step(q, 1)
            expert_step(N_EXP // 2 - 1, 0)
            expert_step(N_EXP // 2 - 1, 1, last=True)
            finish_expert(N_EXP // 2 - 1, 1)

            most = act.value_load(count_i[0:1, :], min_val=0, max_val=TOK)
            with act.If(most > P):
                with act.Fori(1, N_BLOCK - N_EXP + 1) as b:
                    act.wait_ge(over["x_turned"], b)
                    take_x(0).then_inc(over["act_x"], 1)
                    act.wait_ge(over["gated"], b)
                    nc.scalar.activation(silu, ps[:, 2, :], ACT.Silu).then_inc(over["silu"], 1)
                    act.wait_ge(over["down"], b + 1)
                    take_y(0).then_inc(over["act_y"], 1)

            for i in range(NT):
                root(NT + i)
                act.wait_ge(rstd_ready, i + 1)
                x = res[0:token_rows(i), i, :]
                nc.scalar.activation(x, x, ACT.Identity, bias=lnsd[0:token_rows(i), 3:4], scale=lnsd[0:token_rows(i), 2:3])\
                  .then_inc(normalized, 1)


        @block.vector
        def _(dve):
            link = chained(dve, dve_chain)
            v = nc.vector
            for c in range(4):
                ins = v.memset(uext_flat[:, c, 0:2], 0.0)
            ins.then_inc(zeroed, 1)
            dve.wait_ge(zeroed, 1)
            link(v.memset(ones, 1.0))
            for n, (kind, a) in enumerate(proj):
                if p_owner[n][0]:
                    continue
                dve.wait_ge(filled, n + 1)
                if kind == "x_T":
                    i, h = a
                    m = token_rows(i)
                    src = bank(n, 0)[:, 0:4 * m].rearrange("p (k t) -> p k t", k=4)
                    last = v.tensor_copy(xT[:, 4 * h:4 * h + 4, i * P:i * P + m], src)
                elif kind == "bias_row":
                    last = v.tensor_copy(bias_rows[0:20, a, :].rearrange("p (h c) -> p h c", h=2), pair(n)[0:20, :, 0:320])
                elif kind == "state_T":
                    src = bank(n, 0)[:, 0:76].rearrange("p (c r) -> p c r", c=4)
                    for c in range(4):
                        v.tensor_copy(sample_u[c][:, :, 0:2], src[:, c, 0:16].rearrange("p (s r) -> p s r", s=NSEQ))
                    last = v.tensor_copy(conv_w, src[:, :, 16:19])
                elif kind == "conv_h":
                    if a == 0:
                        dve.wait_ge(filled, at["x_T", (NT - 1, 1)] + 1)
                    dve.wait_ge(act_emptied, p_owner[at["conv_c", a]][1])
                    v.tensor_tensor(uext_flat[:, a, 2:2 + HALF], bank(n, 0)[:, 0:HALF], conv_tmp[:, a, 0:HALF], ALU.mult)
                    v.tensor_tensor(uext_flat[:, a, 2 + HALF:2 + SEQ], bank(n, 1)[:, 0:SEQ - HALF],
                                    conv_tmp[:, a, HALF:SEQ], ALU.mult)
                    link(v.tensor_tensor(sample_u[a][:, :, 2:10],
                                         bank(n, 1)[:, SEQ - HALF:HALF].rearrange("p (s t) -> p s t", s=NSEQ),
                                         conv_tmp[:, a, SEQ:TOK].rearrange("p (s t) -> p s t", s=NSEQ), ALU.mult))
                    v.tensor_copy(u_last[:, a, 0:2], uext_flat[:, a, SEQ:SEQ + 2])
                    link(v.tensor_copy(u_last[:, a, 2:18].rearrange("p (s r) -> p s r", s=NSEQ), sample_u[a][:, :, 8:10]))
                    if a == 3:
                        dve.engine_nop().then_inc(u_ready, 1)
                    y_p = conv_tmp[:, a, 0:SEQ]
                    y_s = conv_tmp[:, a, SEQ:TOK].rearrange("p (s t) -> p s t", s=NSEQ)
                    for j in range(3):
                        w = conv_w[:, a, j:j + 1]
                        u_p, u_s = uext_flat[:, a, j:j + SEQ], sample_u[a][:, :, j:j + TNEW]
                        if j == 0:
                            v.tensor_scalar(y_p, u_p, w, None, ALU.mult)
                            link(v.tensor_scalar(y_s, u_s, w, None, ALU.mult))
                        else:
                            v.scalar_tensor_tensor(out=y_p, in0=u_p, scalar=w, in1=y_p, op0=ALU.mult, op1=ALU.add)
                            ins = v.scalar_tensor_tensor(out=y_s, in0=u_s, scalar=w, in1=y_s, op0=ALU.mult, op1=ALU.add)
                            if j == 1:
                                link(ins)
                            else:
                                last = ins
                elif kind == "conv_b":
                    if a == 0:
                        dve.wait_ge(dve_emptied, p_owner[at["conv_h", 3]][1])
                    last = v.tensor_tensor(halves(yconvT[:, a]), pair(n)[:, :, 0:HALF], halves(conv_tmp[:, a]), ALU.mult)
                elif kind == "pos_T":
                    dve.wait_ge(dve_emptied, p_owner[at["conv_b", 3]][1])
                    for dst, src in pair_pieces(None, POS0, bank(n, 0)[:, 0:64].rearrange("p (v l) -> p v l", v=2)):
                        last = v.tensor_copy(dst, src)
                elif kind == "cmp":
                    last = v.tensor_copy(halves(kT[:, 6]), pair(n)[:, :, 0:HALF])
                elif kind == "rows":
                    if a[0] == 0 and a[1] == 0:
                        dve.wait_ge(bias_out, 16 * 4)
                    last = copy_rows(dve, n, a)
                elif kind == "win_k_T":
                    v.tensor_copy(kT[:, 7, 0:SEQ], bank(n, 0))
                    last = v.tensor_copy(kT[:, 7, SEQ:TOK], bank(n, 1)[:, 0:NS])
                elif kind == "page_T":
                    for dst, src in pair_pieces(None, SEQ + PAST * a, bank(n, 0).rearrange("p (v t) -> p v t", v=2)):
                        last = v.tensor_copy(dst, src)
                elif kind in ("dil_q", "nsa_q"):
                    c = a + (6 if kind == "nsa_q" else 0)
                    last = v.tensor_scalar(halves(qT[:, c]), pair(n)[:, :, 0:HALF], SCALE, None, ALU.mult)
                elif kind == "k_rows":
                    if a >= 3:
                        dve.wait_ge(stage_out[a % 3], 32 * (a // 3))
                    v.tensor_copy(stage[a % 3][:, 0:QT, :], bank(n, 0).rearrange("p (i c) -> p i c", i=QT))
                    last = v.tensor_copy(stage[a % 3][0:NS, QT, :], bank(n, 1)[0:NS, 0:P])
                elif kind == "cmp_k_T":
                    last = v.tensor_copy(kcT[:, 0:NCMP - 1], bank(n, 0)[:, 0:NCMP - 1])
                elif kind == "cmp_v":
                    if a == 0:
                        last = v.tensor_copy(vcp[0:PROMPT_CMP], bank(n, 0)[0:PROMPT_CMP, 0:P])
                    else:
                        last = v.tensor_copy(vcs[0:SAMPLE_CMP].rearrange("p (h s) c -> p h (s c)", h=2), pair(n)[0:SAMPLE_CMP])
                last.then_inc(dve_emptied, 1)

            proj_all_emptied(dve)

            def table(u, s, w):
                kind, h, qt = UNITS[u]
                if kind == "dil":
                    return tab_dil0[:, h, 256 - w:256] if s == 0 else tab_dil[:, s - 1, h, 512 - w:512]
                if kind == "nsa":
                    return unseen[:, qt, :] if s == 0 else tab_nsa[:, 4 * h[0] + h[1], 512 - w:512]
                if kind == "sdil":
                    o = (0, 136, 400)[s]
                    return tab_sdil[:, o:o + w]
                return unseen[:, QT - 1, 0:w] if s == 0 else tab_snsa

            def biased_scores(u):
                if u >= 3:
                    tiles = key_tiles(UNITS[u - 3])
                    dve.wait_ge(turned, fill_at["probs", u - 3, (len(tiles) - 1) // 4] + 1)
                top, neg_max, _, _ = stat[u % 2]
                for s, w in enumerate(segments(UNITS[u])):
                    dve.wait_ge(scored, 3 * u + s + 1)
                    ins = v.tensor_tensor_reduce(probs_of(u, s, 0, w), ps[:, (3 * u + s) % 4, 0:w],
                                                 table(u, s, w), 1.0, -3e38, ALU.add, ALU.max, top[:, s:s + 1])
                    ins.then_inc(score_read, 1)
                dve.wait_ge(score_read, 3 * u + 3)
                if UNITS[u][0] in ("dil", "sdil"):
                    v.tensor_reduce(neg_max[:, 0:1], top, AX_X, ALU.max, negate=True).then_inc(max_ready, 1)
                else:
                    v.tensor_scalar(neg_max, top, -1.0, CLAMP, ALU.mult, ALU.min).then_inc(max_ready, 1)

            def scale_probs(u):
                kind, h, qt = UNITS[u]
                _, _, total, scale = stat[u % 2]
                dve.wait_ge(exp_ready, u + 1)
                joint = kind in ("dil", "sdil")
                if joint:
                    link(v.reciprocal(scale[:, 0:1], total[:, 0:1]))
                else:
                    link(v.tensor_scalar(total, total, TINY, None, ALU.max))
                    link(v.reciprocal(scale, total))
                    gate = nsa_gate[:, qt, 4 * h[0] + h[1]:24:8] if kind == "nsa" else gate_s[:, h, :]
                    link(v.tensor_tensor(scale, scale, gate, ALU.mult))
                for s, w in enumerate([sum(segments(UNITS[u]))] if joint else segments(UNITS[u])):
                    seg = probs_of(u, s, 0, w)
                    last = v.tensor_scalar(seg, seg, scale[:, s:s + 1], None, ALU.mult)
                last.then_inc(scaled, 1)

            def take_sums(u):
                kind, h, qt = UNITS[u]
                dve.wait_ge(summed, u + 1)
                src = ps[:, 6 + u % 2, :]
                if kind == "dil":
                    rows = slice(h % 2 * DH, h % 2 * DH + DH)
                    last = v.tensor_copy(ydilT[rows, h // 2, qt * P:(qt + 1) * P], src[rows, 0:P])
                elif kind == "nsa":
                    rows = slice(h[0] * DH, h[0] * DH + DH)
                    last = v.tensor_copy(ynsaT[rows, h[1], qt * P:(qt + 1) * P], src[rows, 0:P])
                elif kind == "sdil":
                    last = v.tensor_copy(sum_rows, src[:, 0:256])
                else:
                    for g in range(2):
                        rows = slice(g * DH, g * DH + DH)
                        got = src[rows, 0:P].rearrange("p (n g j t) -> p g j n t", n=2, g=2, j=4)
                        c0 = SEQ + 2 * h * TNEW
                        last = v.tensor_copy(ynsaT[rows, :, c0:c0 + 16].rearrange("p j (n t) -> p j n t", n=2), got[:, g])
                last.then_inc(out_read, 1)

            def take_turned_sums(u):
                m = fill_at["sums", u, 0]
                dve.wait_ge(turned, m + 1)
                for pr in range(2):
                    for x in range(2):
                        rows = slice(x * DH, x * DH + DH)
                        got = turn_bank(m)[rows, 128 * pr:128 * pr + 128].rearrange("p (n h t) -> p n h t", n=4, h=4)
                        c0 = SEQ + 4 * UNITS[u][1] * TNEW
                        last = v.tensor_copy(ydilT[rows, pr, c0:c0 + 32].rearrange("p (n t) -> p n t", n=4),
                                             got[:, :, 2 * pr + x, :])
                last.then_inc(dve_turned, 1)

            dve.wait_ge(gates_ready, 1)
            dve.wait_ge(dil_tables_in, 48)
            dve.wait_ge(u_out, 32)
            for u in range(len(UNITS) + 4):
                if UNITS[min(u, N_PROMPT)][0] == "nsa":
                    dve.wait_ge(nsa_tables_in, 16)
                if u == N_PROMPT:
                    dve.wait_ge(queries_built, 1)
                    dve.wait_ge(keys_kept, 1)
                if begins_half(u):
                    scale_probs(u - 1)
                    for n in range(4 * UNITS[u][1], 4 * UNITS[u][1] + 4):
                        for f in range(4):
                            m = fill_at["keys", n, f]
                            dve.wait_ge(turned, m + 1)
                            dst = cache_key_rows(n, f)
                            w = 2 * dst.shape[2]
                            v.tensor_copy(dst, turn_bank(m)[:, 0:w].rearrange("p (r c) -> p r c", r=2)).then_inc(dve_turned, 1)
                if u == N_PROMPT:
                    dve.wait_ge(sample_tables_in, 16 * 14)
                    dve.wait_ge(gates_in, 128)
                if u < len(UNITS):
                    biased_scores(u)
                if u >= 5 and UNITS[u - 5][0] == "sdil":
                    take_turned_sums(u - 5)
                if u >= 4:
                    take_sums(u - 4)
                if 1 <= u <= len(UNITS) and not begins_half(u):
                    scale_probs(u - 1)

            def row_statistics(i, x):
                m = token_rows(i)
                for h in range(2):
                    ins = v.bn_stats(lnst[0:m, 6 * h:6 * h + 6], x[0:m, 512 * h:512 * h + 512])
                link(ins)
                link(v.bn_aggr(lnmv[0:m], lnst[0:m]))
                v.tensor_scalar(lnsd[0:m, 0:1], lnmv[0:m, 1:2], LN_EPS, None, ALU.add).then_inc(var_ready, 1)

            def layer_norm(i, x):
                m = token_rows(i)
                row_statistics(i, x)
                dve.wait_ge(sqrt_ready, i + 1)
                link(v.reciprocal(lnsd[0:m, 2:3], lnsd[0:m, 1:2]))
                link(v.tensor_scalar(x[0:m], x[0:m], lnmv[0:m, 0:1], lnsd[0:m, 2:3], ALU.subtract, ALU.mult))
                link(v.tensor_tensor(x[0:m], x[0:m], ln[0:m, 0, :], ALU.mult))
                return v.tensor_tensor(x[0:m], x[0:m], ln[0:m, 1, :], ALU.add)

            def experts_of_group(i):
                return routing(i).rearrange("p t (g x) -> p t g x", g=4)

            def first_best(mask, values):
                best = tmp1[:, 0:NT]
                wide = best.unsqueeze(2).broadcast_to([P, NT, 16])
                places = ramp[:, 0:16].unsqueeze(1).broadcast_to([P, NT, 16])
                link(v.tensor_reduce(best, values, AX_X, ALU.max))
                link(v.tensor_tensor(mask, values, wide, ALU.is_equal))
                link(v.tensor_tensor(mask, mask, places, ALU.mult))
                link(v.tensor_reduce(best, mask, AX_X, ALU.max))
                link(v.tensor_tensor(mask, mask, wide, ALU.is_equal))

            def choose_experts():
                aff, score, masked, first, second, both, tmp = (routing(k) for k in range(7))
                later_emptied(dve, "router", 0)
                link(v.tensor_tensor(score, aff, router_b.unsqueeze(1).broadcast_to([P, NT, 16]), ALU.add))
                sg = experts_of_group(1)
                for o, x in ((0, 0), (3, 1), (5, 2)):
                    n = 3 - x
                    ins = v.tensor_tensor(pair_sums[:, :, :, o:o + n], sg[:, :, :, x + 1:4],
                                          sg[:, :, :, x:x + 1].broadcast_to([P, NT, 4, n]), ALU.add)
                link(ins)
                link(v.tensor_reduce(group_score, pair_sums, AX_X, ALU.max))
                best = tmp1[:, 0:NT]
                wide = best.unsqueeze(2).broadcast_to([P, NT, 4])
                link(v.tensor_reduce(best, group_score, AX_X, ALU.max))
                link(v.tensor_tensor(group_hot, group_score, wide, ALU.is_equal))
                link(v.tensor_tensor(group_hot, group_hot, ramp[:, 16:20].unsqueeze(1).broadcast_to([P, NT, 4]), ALU.mult))
                link(v.tensor_reduce(best, group_hot, AX_X, ALU.max))
                link(v.tensor_tensor(group_hot, group_hot, wide, ALU.is_equal))
                hot4 = group_hot.unsqueeze(3).broadcast_to([P, NT, 4, 4])
                v.tensor_tensor(experts_of_group(2), sg, hot4, ALU.mult)
                link(v.tensor_scalar(experts_of_group(6), hot4, -NEG, NEG, ALU.mult, ALU.add))
                link(v.tensor_tensor(masked, masked, tmp, ALU.add))
                first_best(first, masked)
                link(v.scalar_tensor_tensor(out=masked, in0=first, scalar=2 * NEG, in1=masked, op0=ALU.mult, op1=ALU.add))
                first_best(second, masked)
                link(v.tensor_tensor(both, first, second, ALU.add))
                ins = v.memset(both[64:P, QT, :], 0.0)
                ins.then_inc(chosen, 1)
                for j, hot_j in enumerate((first, second)):
                    link(v.tensor_tensor(tmp, aff, hot_j, ALU.mult))
                    link(v.tensor_reduce(gates2[:, j, :], tmp, AX_X, ALU.add))
                link(v.tensor_tensor(best, gates2[:, 0, :], gates2[:, 1, :], ALU.add))
                link(v.reciprocal(best, best))
                link(v.tensor_tensor(gates2, gates2, best.unsqueeze(1).broadcast_to([P, 2, NT]), ALU.mult))

            def place_tokens(n):
                _, _, _, first, second, _, tmp, rank, blk, row, entry = (routing(k) for k in range(11))
                link(v.tensor_copy(rank, bank(n, 0)[:, 0:16 * NT].rearrange("p (i e) -> p i e", e=16)))
                link(v.tensor_scalar(blk, rank, float(P), None, ALU.is_ge))
                for x in range(2, BIG_BLOCKS):
                    link(v.scalar_tensor_tensor(out=blk, in0=rank, scalar=float(x * P), in1=blk, op0=ALU.is_ge, op1=ALU.add))
                spread = lambda c0: ramp[:, c0:c0 + 16].unsqueeze(1).broadcast_to([P, NT, 16])
                link(v.tensor_tensor(row, rank, spread(20), ALU.add))
                link(v.scalar_tensor_tensor(out=row, in0=blk, scalar=float((N_EXP - 1) * P), in1=row, op0=ALU.mult, op1=ALU.add))
                link(v.scalar_tensor_tensor(out=entry, in0=rank, scalar=float(N_BLOCK), in1=spread(36), op0=ALU.mult, op1=ALU.add))
                link(v.scalar_tensor_tensor(out=entry, in0=blk, scalar=float(N_EXP - P * N_BLOCK), in1=entry, op0=ALU.mult, op1=ALU.add))
                for x, (hot_x, where) in enumerate(((first, row), (second, row), (first, entry), (second, entry))):
                    link(v.tensor_tensor(tmp, hot_x, where, ALU.mult))
                    link(v.tensor_reduce(dst_f[:, x, :], tmp, AX_X, ALU.add))
                v.tensor_copy(dst_i, dst_f)
                link(v.tensor_reduce(tmp1[:, 0:1], bank(n, 1)[:, 0:16], AX_X, ALU.max))
                link(v.tensor_copy(count_i, tmp1[:, 0:1]))
                dve.engine_nop().then_inc(indices_ready, 1)
                return v.memset(tmp1[:, 0:1], 0.0)

            branches = 0
            for n, (kind, a) in enumerate(later):
                if l_owner[n][0]:
                    continue
                if kind == "ple_proj" and a == 0:
                    choose_experts()
                dve.wait_ge(later_filled, n + 1)
                if kind == "branch":
                    c, b = a
                    later_emptied(dve, "gate", a)
                    src, g = pair(n)[:, :, 0:HALF], halves(sig[branches % 2])
                    branches += 1
                    if b == 0:
                        last = v.tensor_tensor(halves(mT[:, c]), g, src, ALU.mult)
                    else:
                        link(v.tensor_tensor(g, g, src, ALU.mult))
                        last = v.tensor_tensor(halves(mT[:, c]), halves(mT[:, c]), g, ALU.add)
                elif kind == "mix":
                    m = token_rows(a)
                    x = res[:, a, :]
                    if a == 0:
                        link(v.memset(routing(0), 1.0))
                        dve.engine_nop().then_inc(route_zeroed, 1)
                    dve.wait_ge(res_in[a], 16)
                    for out, product in product_parts(n, a, x):
                        ins = v.scalar_tensor_tensor(out=out, in0=out, scalar=ALPHA, in1=product, op0=ALU.mult, op1=ALU.add)
                    ins.then_inc(dve_later, 1)
                    wait_emptied(dve, l_owner, n, act_later, dve_later)
                    if a == 0:
                        dve.wait_ge(late_in, 80)
                    layer_norm(a, x).then_inc(x1_ready, 1)
                    continue
                elif kind == "x1_T":
                    i, h = a
                    m = token_rows(i)
                    src = bank(n, 0)[:, 0:4 * m].rearrange("p (k t) -> p k t", k=4)
                    last = v.tensor_copy(x1T[:, 4 * h:4 * h + 4, i * P:i * P + m], src)
                elif kind == "ple_proj":
                    m = token_rows(a)
                    later_emptied(dve, "ple_gate", a)
                    for g, product in product_parts(n, a, ple_sig[a % 2]):
                        ins = v.tensor_tensor(g, g, product, ALU.mult)
                    link(ins)
                    if a == 0:
                        for i in range(NT):
                            dve.wait_ge(x1_stored[i], 16)
                        for h in range(2):
                            dve.wait_ge(later_filled, lat["x1_T", (NT - 1, h)] + 1)
                    last = v.scalar_tensor_tensor(out=res[0:m, a, :], in0=res[0:m, a, :], scalar=ALPHA,
                                                  in1=ple_sig[a % 2][0:m], op0=ALU.mult, op1=ALU.add)
                elif kind == "rank":
                    last = place_tokens(n)
                last.then_inc(dve_later, 1)

            def take_x(s):
                return v.tensor_copy(xgT[s][:, 4:8, :], ps[:, 1, :].rearrange("p (k t) -> p k t", k=4))

            def take_hT():
                return v.tensor_copy(hT, ps[:, 4, :].rearrange("p (k t) -> p k t", k=4))

            def take_y(s):
                return v.tensor_copy(y_exp[s][:, 512:1024], ps[:, 6, :])

            def turned_hidden(q, s):
                e = 2 * q + s
                dve.wait_ge(h_turned, e + 1)
                if not (isinstance(q, int) and q == 0 and s == 0):
                    dve.wait_ge(down_done, e)
                take_hT().then_inc(hT_ready, 1)

            def finish_expert(q, s):
                dve.wait_ge(down_done, 2 * q + s + 1)
                if not (isinstance(q, int) and q == 0):
                    dve.wait_ge(y_stored[s], 16 * q)
                take_y(s).then_inc(dve_y, 1)

            def expert_step(q, s, last=False):
                e = 2 * q + s
                first = isinstance(q, int) and q == 0 and s == 0
                pq, p_s = (q, 0) if s else (q - 1, 1)
                if not first:
                    turned_hidden(pq, p_s)
                dve.wait_ge(up_done, e + 1)
                dve.wait_ge(silu_done, e + 1)
                v.tensor_tensor(h_tok, silu, ps[:, 3, :], ALU.mult).then_inc(h_ready, 1)
                if not last:
                    dve.wait_ge(x_turned, e + 2)
                    take_x(1 - s).then_inc(dve_x, 1)
                if not first:
                    finish_expert(pq, p_s)

            dve.wait_ge(x_turned, 1)
            take_x(0).then_inc(dve_x, 1)
            for j in range(2):
                for i in range(NT):
                    last = v.tensor_scalar(gate_diag[:, j, i, :], ident, gates2[:, j, i:i + 1], None, ALU.mult)
            last.then_inc(diag_ready, 1)
            expert_step(0, 0)
            expert_step(0, 1)
            with dve.Fori(1, N_EXP // 2 - 1) as q:
                expert_step(q, 0)
                expert_step(q, 1)
            expert_step(N_EXP // 2 - 1, 0)
            expert_step(N_EXP // 2 - 1, 1, last=True)
            turned_hidden(N_EXP // 2 - 1, 1)
            finish_expert(N_EXP // 2 - 1, 1)

            most = dve.value_load(count_i[0:1, :], min_val=0, max_val=TOK)
            with dve.If(most > P):
                with dve.Fori(1, N_BLOCK - N_EXP + 1) as b:
                    dve.wait_ge(over["x_turned"], b)
                    take_x(0).then_inc(over["dve_x"], 1)
                    dve.wait_ge(over["up"], b)
                    dve.wait_ge(over["silu"], b)
                    v.tensor_tensor(h_tok, silu, ps[:, 3, :], ALU.mult).then_inc(over["h"], 1)
                    dve.wait_ge(over["h_turned"], b)
                    take_hT().then_inc(over["hT"], 1)
                    dve.wait_ge(over["down"], b + 1)
                    take_y(0).then_inc(over["dve_y"], 1)

            def gain(i):
                x = res[0:token_rows(i), i, :]
                dve.wait_ge(normalized, i + 1)
                ins = v.tensor_tensor(x, x, ln[0:token_rows(i), 2, :], ALU.mult)
                if i < NT - 1:
                    ins.then_inc(gained, 1)
                    return
                link(ins)
                v.tensor_tensor(x, x, ln[0:token_rows(i), 3, :], ALU.add).then_inc(last_combined, 1)

            for i in range(NT):
                m = token_rows(i)
                dve.wait_ge(weighed, i + 1)
                x = res[0:m, i, :]
                xh = x.rearrange("p (h c) -> p h c", h=2)
                v.tensor_tensor(xh, xh, pair(i)[0:m], ALU.add).then_inc(added, 1)
                dve.wait_ge(added, i + 1)
                row_statistics(i, x)
                if i:
                    gain(i - 1)
                dve.wait_ge(sqrt_ready, NT + i + 1)
                link(v.reciprocal(lnsd[0:m, 2:3], lnsd[0:m, 1:2]))
                v.scalar_tensor_tensor(out=lnsd[0:m, 3:4], in0=lnmv[0:m, 0:1], scalar=-1.0, in1=lnsd[0:m, 2:3],
                                       op0=ALU.mult, op1=ALU.mult).then_inc(rstd_ready, 1)
            gain(NT - 1)


        @block.gpsimd
        def _(pool):
            link = chained(pool, pool_chain)
            proj_emptied(pool, "bias_row", 3)
            for kind, rows in enumerate((range(12, 20), range(0, 4), range(4, 8), range(8, 12))):
                row = bias_rows[rows[0]:rows[-1] + 1, kind, :]
                pool.dma_start(bias_d[rows[0]:rows[-1] + 1], row.unsqueeze(1).broadcast_to([len(rows), P, RLEN])).then_inc(bias_out, 16)
            proj_emptied(pool, "u_T", 0)
            pool.dma_start(O["conv_prompt"][0, 0], u_rows[0:2]).then_inc(u_out, 16)
            pool.dma_start(O["conv_sample"][0].rearrange("n r c -> (n r) c"), u_rows[2:18]).then_inc(u_out, 16)
            for c in range(3):
                for i in range(NT):
                    proj_emptied(pool, "rows", (c, i))
                if c == 0:
                    store_rows(pool, "kv", 384, SEL_V, P)
                    store_rows(pool, "win", 0, WIN_K, 2 * P)
            for t in range(3):
                store_rows(pool, f"dil{t}", 256, 256 * t, 256)
            for c in range(9):
                if c == 6:
                    pool.wait_ge(filled, at["hidden", (1, 1)] + 1)
                    nc.gpsimd.memset(view(41464, 2, 3 * P), 0.0).then_inc(q_pad_zeroed, 1)
                proj_emptied(pool, "k_rows", c)
                name = "kv" if c >= 6 else f"dil{c // 2}"
                col = (256, 0, 128)[c - 6] if c >= 6 else c % 2 * P
                first = QT - O[name + "_prompt"].shape[2] // P
                dst = token_view(name + "_prompt").rearrange("(i p) c -> p i c", p=P)
                pool.dma_start(dst[:, :, col:col + P], stage[c % 3][:, first:QT, :]).then_inc(stage_out[c % 3], 16)
                pool.dma_start(token_view(name + "_sample")[:, col:col + P], stage[c % 3][0:NS, QT, :]).then_inc(stage_out[c % 3], 16)

            proj_all_emptied(pool)
            for i in range(3):
                pool.wait_ge(stage_out[i], 96)
            nc.gpsimd.memset(q_dil, 0.0)
            nc.gpsimd.memset(q_nsa, 0.0).then_inc(queries_zeroed, 1)
            nc.gpsimd.tensor_copy(k_new, kT[:, :, SEQ:TOK]).then_inc(keys_kept, 1)
            pool.wait_ge(gates_ready, 1)
            pool.dma_start(gates_d, nsa_gate[0:NS, QT, :]).then_inc(gates_out, 16)
            pool.wait_ge(gates_out, 16)
            for m in range(4):
                for n2 in range(2):
                    src = bass.AP(tensor=gates_d.tensor, offset=(2 * m + n2) * TNEW * 24, ap=[[3, 8], [24, TNEW], [1, 3]])
                    pool.dma_start(gate_s[64 * n2:64 * n2 + 64, m, :], src).then_inc(gates_in, 16)
            pool.wait_ge(queries_built, 1)
            pool.wait_ge(keys_kept, 1)

            for n in range(NSEQ):
                pool.wait_ge(scored, 3 * (N_PROMPT + (0 if n < 4 else 3)))
                nc.gpsimd.tensor_copy(cacheT[n % 4][:, 0:272].rearrange("p (r c) -> p r c", r=2)[:, :, P:P + TNEW],
                                      k_new[:, 0:2, n * TNEW:(n + 1) * TNEW])
                nc.gpsimd.tensor_copy(cacheT[n % 4][:, 272:KT_W].rearrange("p (r c) -> p r c", r=6)[:, :, PAST:PAST + TNEW],
                                      k_new[:, 2:8, n * TNEW:(n + 1) * TNEW]).then_inc(new_keys_put, 1)
                if n == 3:
                    pool.wait_ge(score_read, 3 * N_PROMPT)
                    load_dil_values(pool, 2)
                    load_dil_values(pool, 3)
                    for x in range(4):
                        load_new_dil_values(pool, x)
                    pool.wait_ge(summed, N_PROMPT)
                    load_dil_values(pool, 4)
            pool.wait_ge(summed, N_PROMPT + 1)
            for n in (6, 7):
                load_dil_values(pool, n)
                load_new_dil_values(pool, n)

            link(nc.gpsimd.memset(zeros_i, 0))
            flat_list = list_d.rearrange("(p b) o -> p (b o)", p=P)
            pool.dma_start(flat_list, zeros_i).then_inc(list_zeroed, 16)
            for i in range(NT):
                m = token_rows(i)
                pool.wait_ge(x1_ready, i + 1)
                pool.dma_start(x1_d[i * P:i * P + m, :], res[0:m, i, :]).then_inc(x1_stored[i], 16)
            pool.wait_ge(indices_ready, 1)
            pool.wait_ge(list_zeroed, 16)
            for j in range(2):
                for i in range(NT):
                    m = token_rows(i)
                    pool.indirect_dma_start(list_d, bass.IndirectOffsetOnAxis(ap=dst_i[0:m, 2 + j, i:i + 1], axis=0),
                                            token[0:m, i:i + 1], None).then_inc(listed, 16)
            pool.wait_ge(listed, 160)
            pool.dma_start(block_tok, flat_list.bitcast(U32)).then_inc(list_in, 16)
            pool.wait_ge(list_in, 16)
            for i in range(NT):
                pool.wait_ge(x1_stored[i], 16)

            def gather(e, signal):
                pool.indirect_dma_start(xg[e % 2] if e else xg_first, None, x1_d, bass.IndirectOffsetOnAxis(ap=block_tok[:, e:e + 1], axis=0))\
                    .then_inc(signal, 16)

            later_emptied(pool, "p_T", NT - 1)
            gather(0, xg_in[0])
            pool.wait_ge(later_filled, len(later))
            gather(1, xg_in[1])
            for e in range(N_EXP):
                if e + 2 < N_EXP:
                    pool.wait_ge(x_turned, e + 1)
                    gather(e + 2, xg_in[e % 2])
                pool.wait_ge(act_y, e + 1)
                pool.wait_ge(dve_y, e + 1)
                pool.dma_start(y_d[e * P:(e + 1) * P, :], y_exp[e % 2]).then_inc(y_stored[e % 2], 16)
            pool.wait_ge(y_stored[0], 16 * N_EXP // 2)
            pool.wait_ge(y_stored[1], 16 * N_EXP // 2)

            def shift(i):
                pool.wait_ge(gained, i + 1)
                nc.gpsimd.tensor_tensor(res[:, i, :], res[:, i, :], ln[:, 3, :], ALU.add).then_inc(combined, 1)

            def pick_rows(written):
                for i in range(NT):
                    m = token_rows(i)
                    for j in range(2):
                        pool.indirect_dma_start(picked[i][j][0:m], None, written,
                                                bass.IndirectOffsetOnAxis(ap=dst_i[0:m, j, i:i + 1], axis=0))\
                            .then_inc(picked_in[i], 16)
                for i in range(NT - 1):
                    shift(i)

            most = pool.value_load(count_i[0:1, :], min_val=0, max_val=TOK)
            with pool.If(most > P):
                with pool.Fori(1, N_BLOCK - N_EXP + 1) as b:
                    pool.wait_ge(over["down"], b)
                    last = nc.gpsimd.tensor_copy(zeros_i[:, 0:1].bitcast(U32), block_tok[:, bass.ds(b + N_EXP - 1, 1)])
                    last.then_inc(over["list"], 1)
                    pool.wait_ge(over["list"], b)
                    spare = zeros_i[:, 1:2].bitcast(F32)
                    nc.gpsimd.tensor_tensor(spare, spare, spare, ALU.add)
                    pool.indirect_dma_start(xg[0], None, x1_d, bass.IndirectOffsetOnAxis(ap=zeros_i[:, 0:1].bitcast(U32), axis=0))\
                        .then_inc(over["x"], 16)
                    pool.wait_ge(over["act_y"], b)
                    pool.wait_ge(over["dve_y"], b)
                    pool.dma_start(y_d[bass.ds((b + N_EXP - 1) * P, P), :], y_exp[0]).then_inc(over["stored"], 16)
                    pool.wait_ge(over["stored"], 16 * b)
                pick_rows(y_d)
            with pool.Else():
                pick_rows(y_d[0:N_EXP * P])
            for i in range(3):
                pool.wait_ge(stage_out[i], 96)
            pool.wait_ge(v_out, 160)



OUTPUTS = [
    ("y_prompt", (1, SEQ, D)), ("y_sample", (NSEQ, TNEW, D)),
    ("conv_prompt", (1, 1, 2, CONV)), ("conv_sample", (1, NSEQ, 2, CONV)),
    ("dil0_prompt", (1, 1, 128, 2, 4, DH)), ("dil0_sample", (1, NSEQ, TNEW, 2, 4, DH)),
    ("dil1_prompt", (1, 1, SEQ, 2, 4, DH)), ("dil1_sample", (1, NSEQ, TNEW, 2, 4, DH)),
    ("dil2_prompt", (1, 1, SEQ, 2, 4, DH)), ("dil2_sample", (1, NSEQ, TNEW, 2, 4, DH)),
    ("win_prompt", (1, 1, SEQ, 2, 2, DH)), ("win_sample", (1, NSEQ, TNEW, 2, 2, DH)),
    ("kv_prompt", (1, 1, SEQ, 4, 2, DH)), ("kv_sample", (1, NSEQ, TNEW, 4, 2, DH)),
]


def build(nc, inputs):
    arrays, A, C, O = {}, {}, {}, {}
    for group, values in ((A, inputs), (C, shape_constants())):
        for name, value in values.items():
            a = np.ascontiguousarray(value)
            arrays[name + "_dram"] = a
            group[name] = nc.dram_tensor(name + "_dram", a.shape, mybir.dt.from_np(a.dtype), kind="ExternalInput").ap()
    for name, shape in OUTPUTS:
        O[name] = nc.dram_tensor(name + "_out", shape, F32, kind="ExternalOutput").ap()
    bass_hybrid_decoder_step_kernel(nc, A, C, O)
    return arrays


def kernel(**inputs):
    import concourse.bacc as bacc
    from concourse.bass_utils import run_bass_kernel_spmd

    nc = bacc.Bacc("TRN2", target_bir_lowering=False, num_devices=1)
    arrays = build(nc, inputs)
    r = run_bass_kernel_spmd(nc, [arrays], core_ids=[0])
    return tuple(r.results[0][name + "_out"] for name, _ in OUTPUTS)
```
